# Optimizing a Trainium2 kernel written in Bass

```python
import math
import jax
import jax.numpy as jnp
from jax import lax
import numpy as np
import jax, jax.numpy as jnp

D_MODEL = 1024
BATCH = 1
SEQ = 256
DEPTH = 2

GRID_W = 64
CTX_LEN = 256
EPS = 1e-6

MLSTM_HEADS = 8
MLSTM_DQK = 64
MLSTM_DV = 64
MLSTM_CONV = 3
MLSTM_CHUNK = 64
DIFF_HEADS = 4
DIFF_DQK = 64
DIFF_DV = 128
ROPE_BASE = 10000.0
Q_BLOCK = 128
CONV_WIDTH = 31
D_FF = 2816
N_EXPERTS = 8
TOP_K = 2
D_FF_EXPERT = 2816
MOE_BLOCK = 128

MQK = MLSTM_HEADS * MLSTM_DQK
MV = MLSTM_HEADS * MLSTM_DV
MG = 4 * MLSTM_HEADS
DQK = DIFF_HEADS * 2 * DIFF_DQK
DVW = DIFF_HEADS * DIFF_DV
OFF_MQ = 0
OFF_MK = OFF_MQ + MQK
OFF_MV = OFF_MK + MQK
OFF_MO = OFF_MV + MV
OFF_MG = OFF_MO + MV
OFF_DQ = OFF_MG + MG
OFF_DK = OFF_DQ + DQK
OFF_DV = OFF_DK + DQK
IN0_WIDTH = OFF_DV + DVW
MIX0_WIDTH = MV + DVW


F32 = jnp.float32

def rmsnorm(x, g):
    xf = x.astype(F32)
    y = xf * lax.rsqrt(jnp.mean(xf * xf, axis=-1, keepdims=True) + EPS)
    return (y * g.astype(F32)).astype(x.dtype)

def layernorm(x, g, b):
    xf = x.astype(F32)
    mu = jnp.mean(xf, axis=-1, keepdims=True)
    var = jnp.mean(jnp.square(xf - mu), axis=-1, keepdims=True)
    return ((xf - mu) * lax.rsqrt(var + EPS) * g.astype(F32) + b.astype(F32)).astype(x.dtype)

def adaln(cond, w, b):
    return jax.nn.silu(cond) @ w + b

def modulate(x, g, shift, scale):
    return rmsnorm(x, g) * (1 + scale) + shift

def depthwise_conv(x, w):
    k = w.shape[0]
    return lax.conv_general_dilated(
        x, w[:, None, :].astype(x.dtype), window_strides=(1,),
        padding=[((k - 1) // 2, k // 2)], dimension_numbers=('NWC', 'WIO', 'NWC'),
        feature_group_count=x.shape[-1])

def to_heads(a, n_heads):
    b, t, _ = a.shape
    return a.reshape(b, t, n_heads, -1).transpose(0, 2, 1, 3)

def axial_rope_tables(t_len):
    rows = t_len // GRID_W
    row = jnp.repeat(jnp.arange(rows, dtype=F32), GRID_W)
    col = jnp.tile(jnp.arange(GRID_W, dtype=F32), rows)
    axis_dim = DIFF_DQK // 2
    inv = ROPE_BASE ** (-jnp.arange(0, axis_dim, 2, dtype=F32) / axis_dim)
    ang_r = row[:, None] * inv
    ang_c = col[:, None] * inv
    return jnp.cos(ang_r), jnp.sin(ang_r), jnp.cos(ang_c), jnp.sin(ang_c)

def rotate(x, cos, sin):
    x1, x2 = jnp.split(x, 2, axis=-1)
    return jnp.concatenate([x1 * cos - x2 * sin, x2 * cos + x1 * sin], axis=-1)

def apply_axial_rope(x, tables):
    cr, sr, cc, sc = tables
    xr, xc = jnp.split(x.astype(F32), 2, axis=-1)
    return jnp.concatenate([rotate(xr, cr, sr), rotate(xc, cc, sc)], axis=-1).astype(x.dtype)

def mlstm_gates(g, gate_b):
    g = (g + gate_b).astype(F32)
    b, t, _ = g.shape
    g = g.reshape(b, t, 4, MLSTM_HEADS).transpose(2, 0, 3, 1)
    return g[0], jax.nn.log_sigmoid(g[1]), g[2], jax.nn.log_sigmoid(g[3])

def mlstm_state_update(C, n, m, k, v, ig, b):
    b_last = b[..., -1]
    log_s = b_last[..., None] - b + ig
    m_new = jnp.maximum(b_last + m, jnp.max(log_s, axis=-1))
    ws = jnp.exp(log_s - m_new[..., None])
    decay = jnp.exp(b_last + m - m_new)
    C_new = decay[..., None, None] * C + jnp.einsum('bhs,bhsd,bhse->bhde', ws, k, v)
    n_new = decay[..., None] * n + jnp.einsum('bhs,bhsd->bhd', ws, k)
    return C_new, n_new, m_new

def mlstm_chunk(carry, inp):
    C, n, m = carry
    q, k, v, ig, lf = inp
    L = q.shape[2]
    b = jnp.cumsum(lf, axis=-1)
    order = jnp.tril(jnp.ones((L, L), dtype=bool))
    log_d = jnp.where(order, b[..., :, None] - b[..., None, :] + ig[..., None, :], -jnp.inf)
    log_inter = b + m[..., None]
    m_t = jnp.maximum(log_inter, jnp.max(log_d, axis=-1))
    s = jnp.einsum('bhtd,bhsd->bhts', q, k) * jnp.exp(log_d - m_t[..., None])
    w_inter = jnp.exp(log_inter - m_t)
    num = w_inter[..., None] * jnp.einsum('bhtd,bhde->bhte', q, C) + jnp.einsum('bhts,bhse->bhte', s, v)
    den = w_inter * jnp.einsum('bhtd,bhd->bht', q, n) + jnp.sum(s, axis=-1)
    h = num / jnp.maximum(jnp.abs(den), jnp.exp(-m_t))[..., None]
    return mlstm_state_update(C, n, m, k, v, ig, b), h

def mlstm_scan(q, k, v, ig, lf, state):
    b, h, t, _ = q.shape
    nc = t // MLSTM_CHUNK

    def chunks(a):
        return jnp.moveaxis(a.reshape(a.shape[:2] + (nc, MLSTM_CHUNK) + a.shape[3:]), 2, 0)

    _, out = lax.scan(mlstm_chunk, state, (chunks(q), chunks(k), chunks(v), chunks(ig), chunks(lf)))
    return jnp.moveaxis(out, 0, 2).reshape(b, h, t, -1)

def mlstm_context_state(k, v, ig, lf):
    b, h, _, dk = k.shape
    C0 = jnp.zeros((b, h, dk, v.shape[-1]), F32)
    n0 = jnp.zeros((b, h, dk), F32)
    m0 = jnp.zeros((b, h), F32)
    return mlstm_state_update(C0, n0, m0, k, v, ig, jnp.cumsum(lf, axis=-1))

def mlstm_mixer(q, k, v, o, ig_f, lf_f, ig_b, lf_b, k_c, v_c, igc_f, lfc_f, igc_b, lfc_b, norm_g):
    H = MLSTM_HEADS
    B_, T_, _ = q.shape
    q = to_heads(q, H).astype(F32) * (MLSTM_DQK ** -0.5)
    k = to_heads(k, H).astype(F32)
    v = to_heads(v, H).astype(F32)
    k_c = to_heads(k_c, H).astype(F32)
    v_c = to_heads(v_c, H).astype(F32)
    st_f = mlstm_context_state(k_c, v_c, igc_f, lfc_f)
    st_b = mlstm_context_state(jnp.flip(k_c, 2), jnp.flip(v_c, 2), jnp.flip(igc_b, -1), jnp.flip(lfc_b, -1))
    h_f = mlstm_scan(q, k, v, ig_f, lf_f, st_f)
    h_b = jnp.flip(mlstm_scan(jnp.flip(q, 2), jnp.flip(k, 2), jnp.flip(v, 2),
                              jnp.flip(ig_b, -1), jnp.flip(lf_b, -1), st_b), 2)
    h = (h_f + h_b).transpose(0, 2, 1, 3)
    h = rmsnorm(h, norm_g.reshape(H, MLSTM_DV)).reshape(B_, T_, MV)
    return (h * jax.nn.sigmoid(o.astype(F32))).astype(o.dtype)

def diff_attention_blocks(q1, q2, k1_all, k2_all, v_all, lam):
    B_, H, T_, d = q1.shape
    nb = T_ // Q_BLOCK
    scale = DIFF_DQK ** -0.5

    def blocks(a):
        return a.reshape(B_, H, nb, Q_BLOCK, d).transpose(2, 0, 1, 3, 4)

    def one_block(qs):
        a1, a2 = qs
        s1 = jnp.einsum('bhqd,bhkd->bhqk', a1, k1_all).astype(F32) * scale
        s2 = jnp.einsum('bhqd,bhkd->bhqk', a2, k2_all).astype(F32) * scale
        p = jax.nn.softmax(s1, axis=-1) - lam * jax.nn.softmax(s2, axis=-1)
        return jnp.einsum('bhqk,bhkv->bhqv', p.astype(v_all.dtype), v_all)

    out = lax.map(one_block, (blocks(q1), blocks(q2)))
    return out.transpose(1, 2, 0, 3, 4).reshape(B_, H, T_, -1)

def diff_mixer(q, k, v, k_c, v_c, lq1, lk1, lq2, lk2, norm_g, layer_idx):
    H = DIFF_HEADS
    B_, T_, _ = q.shape

    def split_qk(a):
        a = a.reshape(a.shape[0], a.shape[1], H, 2, DIFF_DQK)
        return a[..., 0, :].transpose(0, 2, 1, 3), a[..., 1, :].transpose(0, 2, 1, 3)

    tables = axial_rope_tables(T_)
    q1, q2 = [apply_axial_rope(a, tables) for a in split_qk(q)]
    k1, k2 = [apply_axial_rope(a, tables) for a in split_qk(k)]
    k1c, k2c = split_qk(k_c)
    k1_all = jnp.concatenate([k1c, k1], axis=2)
    k2_all = jnp.concatenate([k2c, k2], axis=2)
    v_all = jnp.concatenate([to_heads(v_c, H), to_heads(v, H)], axis=2)
    lam_init = 0.8 - 0.6 * math.exp(-0.3 * layer_idx)
    lam = (jnp.exp(jnp.sum(lq1.astype(F32) * lk1.astype(F32)))
           - jnp.exp(jnp.sum(lq2.astype(F32) * lk2.astype(F32))) + lam_init)
    o = diff_attention_blocks(q1, q2, k1_all, k2_all, v_all, lam).transpose(0, 2, 1, 3)
    o = rmsnorm(o, norm_g.reshape(H, DIFF_DV)) * (1.0 - lam_init)
    return o.reshape(B_, T_, DVW)

def swiglu(u, w1, w3, w2):
    return (jax.nn.silu(u @ w1) * (u @ w3)) @ w2

def moe_swiglu(u, router_w, w1, w3, w2):
    B_, T_, D = u.shape
    tokens = u.reshape(-1, D)
    N = tokens.shape[0]
    logits = (tokens @ router_w).astype(F32)
    top_vals, top_idx = lax.top_k(logits, TOP_K)
    gates = jax.nn.softmax(top_vals, axis=-1)
    A = N * TOP_K
    flat_e = top_idx.reshape(-1)
    flat_tok = jnp.repeat(jnp.arange(N, dtype=jnp.int32), TOP_K)
    flat_g = gates.reshape(-1)
    order = jnp.argsort(flat_e)
    s_e, s_tok, s_g = flat_e[order], flat_tok[order], flat_g[order]
    counts = jnp.bincount(flat_e, length=N_EXPERTS)
    starts = jnp.cumsum(counts) - counts
    padded = ((counts + MOE_BLOCK - 1) // MOE_BLOCK) * MOE_BLOCK
    pends = jnp.cumsum(padded)
    pstarts = pends - padded
    dest = pstarts[s_e] + (jnp.arange(A) - starts[s_e])
    n_blk = (A + MOE_BLOCK - 1) // MOE_BLOCK + N_EXPERTS
    R = n_blk * MOE_BLOCK
    slot_tok = jnp.zeros((R,), jnp.int32).at[dest].set(s_tok)
    slot_g = jnp.zeros((R,), F32).at[dest].set(s_g)
    block_e = jnp.clip(jnp.searchsorted(pends, jnp.arange(n_blk) * MOE_BLOCK, side='right'), 0, N_EXPERTS - 1)

    def run_block(args):
        tok_idx, e = args
        xb = tokens[tok_idx]
        return (jax.nn.silu(xb @ w1[e]) * (xb @ w3[e])) @ w2[e]

    y = lax.map(run_block, (slot_tok.reshape(n_blk, MOE_BLOCK), block_e)).reshape(R, D)
    y = y * slot_g[:, None].astype(y.dtype)
    out = jnp.zeros((N, D), y.dtype).at[slot_tok].add(y)
    return out.reshape(B_, T_, D)

def even_layer(x, c, ctx, c_ctx, layer_idx, mod_w, mod_b, mix_pre_g, mix_post_g, w_in, mlstm_gate_b,
               mlstm_conv_w, mlstm_norm_g, lambda_q1, lambda_k1, lambda_q2, lambda_k2, diff_norm_g,
               w_out, ffn_pre_g, ffn_post_g, ffn_w1, ffn_w3, ffn_w2):
    sh_m, sc_m, gt_m, sh_f, sc_f, gt_f = jnp.split(adaln(c, mod_w, mod_b)[:, None, :], 6, axis=-1)
    sh_c, sc_c = jnp.split(adaln(c_ctx, mod_w, mod_b), 6, axis=-1)[:2]
    u = modulate(x, mix_pre_g, sh_m, sc_m)
    p = u @ w_in
    q_m = jax.nn.silu(depthwise_conv(p[..., OFF_MQ:OFF_MK], mlstm_conv_w[:, :MQK]))
    k_m = jax.nn.silu(depthwise_conv(p[..., OFF_MK:OFF_MV], mlstm_conv_w[:, MQK:]))
    v_m = p[..., OFF_MV:OFF_MO]
    o_m = p[..., OFF_MO:OFF_MG]
    ig_f, lf_f, ig_b, lf_b = mlstm_gates(p[..., OFF_MG:OFF_DQ], mlstm_gate_b)
    uc = modulate(ctx, mix_pre_g, sh_c, sc_c)
    kv_mc = uc @ w_in[:, OFF_MK:OFF_MO]
    k_mc = jax.nn.silu(depthwise_conv(kv_mc[..., :MQK], mlstm_conv_w[:, MQK:]))
    v_mc = kv_mc[..., MQK:]
    igc_f, lfc_f, igc_b, lfc_b = mlstm_gates(uc @ w_in[:, OFF_MG:OFF_DQ], mlstm_gate_b)
    kv_dc = uc @ w_in[:, OFF_DK:]
    h_m = mlstm_mixer(q_m, k_m, v_m, o_m, ig_f, lf_f, ig_b, lf_b,
                      k_mc, v_mc, igc_f, lfc_f, igc_b, lfc_b, mlstm_norm_g)
    h_d = diff_mixer(p[..., OFF_DQ:OFF_DK], p[..., OFF_DK:OFF_DV], p[..., OFF_DV:],
                     kv_dc[..., :DQK], kv_dc[..., DQK:],
                     lambda_q1, lambda_k1, lambda_q2, lambda_k2, diff_norm_g, layer_idx)
    mix = jnp.concatenate([h_m, h_d], axis=-1) @ w_out
    x = x + gt_m * rmsnorm(mix, mix_post_g)
    y = swiglu(modulate(x, ffn_pre_g, sh_f, sc_f), ffn_w1, ffn_w3, ffn_w2)
    return x + gt_f * rmsnorm(y, ffn_post_g)

def odd_layer(x, c, mod_w, mod_b, mix_pre_g, mix_post_g, pw1_w, pw1_b, dw_w, dw_b, ln_g, ln_b,
              pw2_w, pw2_b, ffn_pre_g, ffn_post_g, router_w, moe_w1, moe_w3, moe_w2):
    sh_m, sc_m, gt_m, sh_f, sc_f, gt_f = jnp.split(adaln(c, mod_w, mod_b)[:, None, :], 6, axis=-1)
    u = modulate(x, mix_pre_g, sh_m, sc_m)
    a, g = jnp.split(u @ pw1_w + pw1_b, 2, axis=-1)
    h = a * jax.nn.sigmoid(g)
    h = depthwise_conv(h, dw_w) + dw_b
    h = jax.nn.silu(layernorm(h, ln_g, ln_b))
    y = h @ pw2_w + pw2_b
    x = x + gt_m * rmsnorm(y, mix_post_g)
    y = moe_swiglu(modulate(x, ffn_pre_g, sh_f, sc_f), router_w, moe_w1, moe_w3, moe_w2)
    return x + gt_f * rmsnorm(y, ffn_post_g)

def first_inputs(seed: int = 0) -> dict:
    key = jax.random.key(seed)
    keys = list(jax.random.split(key, 48))
    D = D_MODEL

    def nrm(shape, scale):
        return jax.random.normal(keys.pop(), shape, F32) * scale

    def gain(n):
        return 1.0 + nrm((n,), 0.05)

    inp = {}
    inp['x'] = nrm((BATCH, SEQ, D), 1.0)
    inp['c'] = nrm((BATCH, D), 1.0)
    inp['ctx'] = nrm((BATCH, CTX_LEN, D), 1.0)
    inp['c_ctx'] = nrm((D,), 1.0)
    inp['l0_mod_w'] = nrm((D, 6 * D), 0.5 * D ** -0.5)
    inp['l0_mod_b'] = nrm((6 * D,), 0.02)
    inp['l0_mix_pre_g'] = gain(D)
    inp['l0_mix_post_g'] = gain(D)
    inp['l0_w_in'] = nrm((D, IN0_WIDTH), D ** -0.5)
    gate_offsets = jnp.concatenate([
        jnp.full((MLSTM_HEADS,), -1.0, F32), jnp.linspace(3.0, 6.0, MLSTM_HEADS, dtype=F32),
        jnp.full((MLSTM_HEADS,), -1.0, F32), jnp.linspace(3.0, 6.0, MLSTM_HEADS, dtype=F32)])
    inp['l0_mlstm_gate_b'] = gate_offsets + nrm((MG,), 0.1)
    inp['l0_mlstm_conv_w'] = nrm((MLSTM_CONV, 2 * MQK), MLSTM_CONV ** -0.5)
    inp['l0_mlstm_norm_g'] = gain(MV)
    inp['l0_lambda_q1'] = nrm((DIFF_DQK,), 0.1)
    inp['l0_lambda_k1'] = nrm((DIFF_DQK,), 0.1)
    inp['l0_lambda_q2'] = nrm((DIFF_DQK,), 0.1)
    inp['l0_lambda_k2'] = nrm((DIFF_DQK,), 0.1)
    inp['l0_diff_norm_g'] = gain(DVW)
    inp['l0_w_out'] = nrm((MIX0_WIDTH, D), MIX0_WIDTH ** -0.5)
    inp['l0_ffn_pre_g'] = gain(D)
    inp['l0_ffn_post_g'] = gain(D)
    inp['l0_ffn_w1'] = nrm((D, D_FF), D ** -0.5)
    inp['l0_ffn_w3'] = nrm((D, D_FF), D ** -0.5)
    inp['l0_ffn_w2'] = nrm((D_FF, D), D_FF ** -0.5)
    inp['l1_mod_w'] = nrm((D, 6 * D), 0.5 * D ** -0.5)
    inp['l1_mod_b'] = nrm((6 * D,), 0.02)
    inp['l1_mix_pre_g'] = gain(D)
    inp['l1_mix_post_g'] = gain(D)
    inp['l1_conv_pw1_w'] = nrm((D, 2 * D), D ** -0.5)
    inp['l1_conv_pw1_b'] = nrm((2 * D,), 0.02)
    inp['l1_conv_dw_w'] = nrm((CONV_WIDTH, D), CONV_WIDTH ** -0.5)
    inp['l1_conv_dw_b'] = nrm((D,), 0.02)
    inp['l1_conv_ln_g'] = gain(D)
    inp['l1_conv_ln_b'] = nrm((D,), 0.02)
    inp['l1_conv_pw2_w'] = nrm((D, D), D ** -0.5)
    inp['l1_conv_pw2_b'] = nrm((D,), 0.02)
    inp['l1_ffn_pre_g'] = gain(D)
    inp['l1_ffn_post_g'] = gain(D)
    inp['l1_router_w'] = nrm((D, N_EXPERTS), D ** -0.5)
    inp['l1_moe_w1'] = nrm((N_EXPERTS, D, D_FF_EXPERT), D ** -0.5)
    inp['l1_moe_w3'] = nrm((N_EXPERTS, D, D_FF_EXPERT), D ** -0.5)
    inp['l1_moe_w2'] = nrm((N_EXPERTS, D_FF_EXPERT, D), D_FF_EXPERT ** -0.5)
    return inp

def first_block(x, c, ctx, c_ctx,
              l0_mod_w, l0_mod_b, l0_mix_pre_g, l0_mix_post_g, l0_w_in, l0_mlstm_gate_b,
              l0_mlstm_conv_w, l0_mlstm_norm_g, l0_lambda_q1, l0_lambda_k1, l0_lambda_q2,
              l0_lambda_k2, l0_diff_norm_g, l0_w_out, l0_ffn_pre_g, l0_ffn_post_g,
              l0_ffn_w1, l0_ffn_w3, l0_ffn_w2,
              l1_mod_w, l1_mod_b, l1_mix_pre_g, l1_mix_post_g, l1_conv_pw1_w, l1_conv_pw1_b,
              l1_conv_dw_w, l1_conv_dw_b, l1_conv_ln_g, l1_conv_ln_b, l1_conv_pw2_w,
              l1_conv_pw2_b, l1_ffn_pre_g, l1_ffn_post_g, l1_router_w, l1_moe_w1, l1_moe_w3,
              l1_moe_w2):
    layer_params = (
        (l0_mod_w, l0_mod_b, l0_mix_pre_g, l0_mix_post_g, l0_w_in, l0_mlstm_gate_b,
         l0_mlstm_conv_w, l0_mlstm_norm_g, l0_lambda_q1, l0_lambda_k1, l0_lambda_q2,
         l0_lambda_k2, l0_diff_norm_g, l0_w_out, l0_ffn_pre_g, l0_ffn_post_g,
         l0_ffn_w1, l0_ffn_w3, l0_ffn_w2),
        (l1_mod_w, l1_mod_b, l1_mix_pre_g, l1_mix_post_g, l1_conv_pw1_w, l1_conv_pw1_b,
         l1_conv_dw_w, l1_conv_dw_b, l1_conv_ln_g, l1_conv_ln_b, l1_conv_pw2_w,
         l1_conv_pw2_b, l1_ffn_pre_g, l1_ffn_post_g, l1_router_w, l1_moe_w1, l1_moe_w3,
         l1_moe_w2),
    )
    for layer in range(DEPTH):
        if layer % 2 == 0:
            x = even_layer(x, c, ctx, c_ctx, layer, *layer_params[layer])
        else:
            x = odd_layer(x, c, *layer_params[layer])
    return x


HEAD_DIM = 64
DSA_HEADS = 4
DSA_TOPK = 256
IDX_HEADS = 8
IDX_DIM = 32
FOX_HEADS = 6
NSA_HEADS = 6
NSA_KV_GROUPS = 2
NSA_HPG = NSA_HEADS // NSA_KV_GROUPS
NSA_CMP_LEN = 32
NSA_CMP_STRIDE = 16
NSA_SEL_BLOCK = 64
NSA_SEL_N = 16
NSA_WINDOW = 512
NSA_Q_BLOCK = 64

ROPE_THETA = 10000.0
LN_EPS = 1e-5
ALPHA = (2.0 * DEPTH) ** 0.25
BETA = (8.0 * DEPTH) ** -0.25

DSA_W = DSA_HEADS * HEAD_DIM
FOX_W = FOX_HEADS * HEAD_DIM
NSA_W = NSA_HEADS * HEAD_DIM
NSA_KV_W = NSA_KV_GROUPS * HEAD_DIM
MIX_W = DSA_W + FOX_W + NSA_W

IN_SPLITS = (
    ("dsa_q", DSA_W), ("dsa_k", HEAD_DIM), ("dsa_v", HEAD_DIM),
    ("idx_q", IDX_HEADS * IDX_DIM), ("idx_k", IDX_DIM), ("idx_w", IDX_HEADS),
    ("fox_q", FOX_W), ("fox_k", FOX_W), ("fox_v", FOX_W), ("fox_f", FOX_HEADS),
    ("nsa_q", NSA_W),
    ("nsa_kc", NSA_KV_W), ("nsa_vc", NSA_KV_W),
    ("nsa_ks", NSA_KV_W), ("nsa_vs", NSA_KV_W),
    ("nsa_kw", NSA_KV_W), ("nsa_vw", NSA_KV_W),
    ("nsa_g", 3 * NSA_HEADS),
    ("gate", MIX_W),
)
IN_WIDTH = sum(w for _, w in IN_SPLITS)


def split_cols(h):
    out, off = {}, 0
    for name, w in IN_SPLITS:
        out[name] = h[..., off:off + w]
        off += w
    return out

def layer_norm(x, g, b):
    xf = x.astype(jnp.float32)
    mu = jnp.mean(xf, -1, keepdims=True)
    var = jnp.mean(jnp.square(xf - mu), -1, keepdims=True)
    return ((xf - mu) * lax.rsqrt(var + LN_EPS) * g + b).astype(x.dtype)

def rope(x, pos):
    half = x.shape[-1] // 2
    inv = ROPE_THETA ** (-jnp.arange(half, dtype=jnp.float32) / half)
    ang = pos.astype(jnp.float32)[:, None] * inv[None, :]
    cos = jnp.cos(ang)[:, None, :]
    sin = jnp.sin(ang)[:, None, :]
    x1, x2 = x[..., :half], x[..., half:]
    return jnp.concatenate([x1 * cos - x2 * sin, x1 * sin + x2 * cos], -1).astype(x.dtype)

def masked_softmax(s, mask):
    s = jnp.where(mask, s.astype(jnp.float32), -jnp.inf)
    m = jnp.max(s, -1, keepdims=True)
    m = jnp.where(jnp.isfinite(m), m, 0.0)
    e = jnp.where(mask, jnp.exp(s - m), 0.0)
    return e / jnp.maximum(jnp.sum(e, -1, keepdims=True), 1e-30)

def stack_blocks(out):
    nb, B, T, H, D = out.shape
    return out.transpose(1, 0, 2, 3, 4).reshape(B, nb * T, H, D)

def dsa_mixer(q, k, v, iq, ik, iw):
    B, S, H, D = q.shape
    topk = min(DSA_TOPK, S // 4)
    kpos = jnp.arange(S)
    scale = D ** -0.5
    gather = jax.vmap(lambda kb, ib: kb[ib])

    def block(i):
        t0 = i * Q_BLOCK
        tpos = t0 + jnp.arange(Q_BLOCK)
        qb = lax.dynamic_slice_in_dim(q, t0, Q_BLOCK, 1)
        iqb = lax.dynamic_slice_in_dim(iq, t0, Q_BLOCK, 1)
        iwb = lax.dynamic_slice_in_dim(iw, t0, Q_BLOCK, 1).astype(jnp.float32)
        isc = jnp.einsum("bthd,bsd->bths", iqb, ik).astype(jnp.float32)
        isc = jnp.einsum("bth,bths->bts", iwb, jax.nn.relu(isc))
        causal = kpos[None, :] <= tpos[:, None]
        isc = jnp.where(causal[None], isc, -jnp.inf)
        _, idx = lax.top_k(isc, topk)
        kg = gather(k, idx)
        vg = gather(v, idx)
        valid = idx <= tpos[None, :, None]
        s = jnp.einsum("bthd,btkd->bthk", qb, kg) * scale
        p = masked_softmax(s, valid[:, :, None, :])
        return jnp.einsum("bthk,btkd->bthd", p.astype(v.dtype), vg)

    return stack_blocks(lax.map(block, jnp.arange(S // Q_BLOCK)))

def fox_mixer(q, k, v, logf):
    B, S, H, D = q.shape
    cum = jnp.cumsum(logf.astype(jnp.float32), axis=1).transpose(0, 2, 1)
    kpos = jnp.arange(S)
    scale = D ** -0.5

    def block(i):
        t0 = i * Q_BLOCK
        tpos = t0 + jnp.arange(Q_BLOCK)
        qb = lax.dynamic_slice_in_dim(q, t0, Q_BLOCK, 1)
        cb = lax.dynamic_slice_in_dim(cum, t0, Q_BLOCK, 2)
        s = jnp.einsum("bthd,bshd->bhts", qb, k).astype(jnp.float32) * scale
        s = s + cb[:, :, :, None] - cum[:, :, None, :]
        causal = kpos[None, :] <= tpos[:, None]
        p = masked_softmax(s, causal)
        return jnp.einsum("bhts,bshd->bthd", p.astype(v.dtype), v)

    return stack_blocks(lax.map(block, jnp.arange(S // Q_BLOCK)))

def nsa_compress(kv, pe, w1, w2):
    B, S, G, D = kv.shape
    n_c = (S - NSA_CMP_LEN) // NSA_CMP_STRIDE + 1
    idx = jnp.arange(n_c)[:, None] * NSA_CMP_STRIDE + jnp.arange(NSA_CMP_LEN)[None, :]
    blocks = kv[:, idx] + pe[None, None, :, None, :]
    blocks = blocks.transpose(0, 1, 3, 2, 4).reshape(B, n_c, G, NSA_CMP_LEN * D)
    return jax.nn.silu(blocks @ w1) @ w2

def nsa_mixer(q, q_rot, kc, vc, ks, vs, kw, vw, gates):
    B, S, G, J, D = q.shape
    n_c = kc.shape[1]
    nsb = S // NSA_SEL_BLOCK
    n_sel = min(NSA_SEL_N, nsb)
    scale = D ** -0.5
    cstart = jnp.arange(n_c) * NSA_CMP_STRIDE
    cend = cstart + NSA_CMP_LEN - 1
    bstart = jnp.arange(nsb) * NSA_SEL_BLOCK
    overlap = ((cstart[:, None] < bstart[None, :] + NSA_SEL_BLOCK)
               & (cstart[:, None] + NSA_CMP_LEN > bstart[None, :])).astype(jnp.float32)
    ks_t = ks.transpose(0, 2, 1, 3)
    vs_t = vs.transpose(0, 2, 1, 3)
    pad = ((0, 0), (NSA_WINDOW, 0), (0, 0), (0, 0))
    kw_pad = jnp.pad(kw, pad)
    vw_pad = jnp.pad(vw, pad)
    gather = jax.vmap(jax.vmap(lambda kk, ii: kk[ii]))
    jb = jnp.arange(nsb)
    tok_off = jnp.arange(NSA_SEL_BLOCK)

    def block(i):
        T = NSA_Q_BLOCK
        t0 = i * T
        tpos = t0 + jnp.arange(T)
        qb = lax.dynamic_slice_in_dim(q, t0, T, 1)
        qrb = lax.dynamic_slice_in_dim(q_rot, t0, T, 1)
        gb = lax.dynamic_slice_in_dim(gates, t0, T, 1)
        s = jnp.einsum("btgjd,bcgd->bgjtc", qb, kc) * scale
        p_cmp = masked_softmax(s, cend[None, :] <= tpos[:, None])
        o_cmp = jnp.einsum("bgjtc,bcgd->btgjd", p_cmp.astype(vc.dtype), vc)
        score = jnp.einsum("bgjtc,cn->bgtn", p_cmp, overlap)
        cur = tpos // NSA_SEL_BLOCK
        forced = (jb[None, :] == 0) | (jb[None, :] == cur[:, None]) | (jb[None, :] == cur[:, None] - 1)
        future = bstart[None, :] > tpos[:, None]
        score = jnp.where(forced, jnp.inf, jnp.where(future, -jnp.inf, score))
        _, blk = lax.top_k(score, n_sel)
        tok = (blk[..., None] * NSA_SEL_BLOCK + tok_off).reshape(B, G, T, n_sel * NSA_SEL_BLOCK)
        kg = gather(ks_t, tok)
        vg = gather(vs_t, tok)
        s = jnp.einsum("btgjd,bgtnd->bgjtn", qrb, kg) * scale
        p = masked_softmax(s, (tok <= tpos[None, None, :, None])[:, :, None])
        o_slc = jnp.einsum("bgjtn,bgtnd->btgjd", p.astype(vs.dtype), vg)
        kwb = lax.dynamic_slice_in_dim(kw_pad, t0, NSA_WINDOW + T, 1)
        vwb = lax.dynamic_slice_in_dim(vw_pad, t0, NSA_WINDOW + T, 1)
        kpos = t0 - NSA_WINDOW + jnp.arange(NSA_WINDOW + T)
        wmask = ((kpos[None, :] <= tpos[:, None]) & (kpos[None, :] > tpos[:, None] - NSA_WINDOW)
                 & (kpos[None, :] >= 0))
        s = jnp.einsum("btgjd,bkgd->bgjtk", qrb, kwb) * scale
        p = masked_softmax(s, wmask)
        o_win = jnp.einsum("bgjtk,bkgd->btgjd", p.astype(vw.dtype), vwb)
        o = (gb[:, :, 0, :, :, None] * o_cmp + gb[:, :, 1, :, :, None] * o_slc
             + gb[:, :, 2, :, :, None] * o_win)
        return o.reshape(B, T, G * J, D)

    return stack_blocks(lax.map(block, jnp.arange(S // NSA_Q_BLOCK)))

def hybrid_layer(x, c, w_ada, b_ada, w_in, b_f, cmp_pe, cmp_w1, cmp_w2, w_out, ln_g, ln_b):
    B, S, _ = x.shape
    pos = jnp.arange(S)
    shift, scale, gate = jnp.split(c @ w_ada + b_ada, 3, axis=-1)
    u = x * (1.0 + scale[:, None, :]) + shift[:, None, :]
    h = split_cols(u @ w_in)

    dq = rope(h["dsa_q"].reshape(B, S, DSA_HEADS, HEAD_DIM), pos)
    dk = rope(h["dsa_k"][:, :, None, :], pos)[:, :, 0]
    iq = rope(h["idx_q"].reshape(B, S, IDX_HEADS, IDX_DIM), pos)
    ik = rope(h["idx_k"][:, :, None, :], pos)[:, :, 0]
    iw = h["idx_w"] * (IDX_HEADS ** -0.5)
    o_dsa = dsa_mixer(dq, dk, h["dsa_v"], iq, ik, iw)

    fq = h["fox_q"].reshape(B, S, FOX_HEADS, HEAD_DIM)
    fk = h["fox_k"].reshape(B, S, FOX_HEADS, HEAD_DIM)
    fv = h["fox_v"].reshape(B, S, FOX_HEADS, HEAD_DIM)
    logf = jax.nn.log_sigmoid(h["fox_f"].astype(jnp.float32) + b_f)
    o_fox = fox_mixer(fq, fk, fv, logf)

    kvs = lambda name: h[name].reshape(B, S, NSA_KV_GROUPS, HEAD_DIM)
    nq = h["nsa_q"].reshape(B, S, NSA_HEADS, HEAD_DIM)
    nq_rot = rope(nq, pos)
    kc = nsa_compress(kvs("nsa_kc"), cmp_pe[0], cmp_w1[0], cmp_w2[0])
    vc = nsa_compress(kvs("nsa_vc"), cmp_pe[1], cmp_w1[1], cmp_w2[1])
    ks = rope(kvs("nsa_ks"), pos)
    kw = rope(kvs("nsa_kw"), pos)
    gates = jax.nn.sigmoid(h["nsa_g"].reshape(B, S, 3, NSA_KV_GROUPS, NSA_HPG))
    grp = lambda t: t.reshape(B, S, NSA_KV_GROUPS, NSA_HPG, HEAD_DIM)
    o_nsa = nsa_mixer(grp(nq), grp(nq_rot), kc, vc, ks, kvs("nsa_vs"), kw, kvs("nsa_vw"), gates)

    mix = jnp.concatenate([o_dsa.reshape(B, S, DSA_W), o_fox.reshape(B, S, FOX_W),
                           o_nsa.reshape(B, S, NSA_W)], axis=-1)
    y = (mix * jax.nn.silu(h["gate"])) @ w_out
    return layer_norm(ALPHA * x + (1.0 + gate[:, None, :]) * y, ln_g, ln_b)

def second_inputs(seed: int = 0) -> dict:
    key = jax.random.key(seed)
    ks = jax.random.split(key, 12)
    D = D_MODEL
    L = NSA_CMP_LEN
    nrm = lambda k, shape, s: jax.random.normal(k, shape, jnp.float32) * s
    return {
        "x": nrm(ks[0], (BATCH, SEQ, D), 1.0),
        "c": nrm(ks[1], (BATCH, D), 1.0),
        "w_ada": nrm(ks[2], (DEPTH, D, 3 * D), 0.1 * D ** -0.5),
        "b_ada": nrm(ks[3], (DEPTH, 3 * D), 0.01),
        "w_in": nrm(ks[4], (DEPTH, D, IN_WIDTH), D ** -0.5),
        "b_f": jax.random.uniform(ks[5], (DEPTH, FOX_HEADS), jnp.float32, 1.0, 4.0),
        "cmp_pe": nrm(ks[6], (DEPTH, 2, L, HEAD_DIM), 0.1),
        "cmp_w1": nrm(ks[7], (DEPTH, 2, L * HEAD_DIM, HEAD_DIM), (L * HEAD_DIM) ** -0.5),
        "cmp_w2": nrm(ks[8], (DEPTH, 2, HEAD_DIM, HEAD_DIM), HEAD_DIM ** -0.5),
        "w_out": nrm(ks[9], (DEPTH, MIX_W, D), BETA * MIX_W ** -0.5),
        "ln_g": 1.0 + nrm(ks[10], (DEPTH, D), 0.01),
        "ln_b": nrm(ks[11], (DEPTH, D), 0.01),
    }

def second_block(x, c, w_ada, b_ada, w_in, b_f, cmp_pe, cmp_w1, cmp_w2, w_out, ln_g, ln_b):
    for l in range(DEPTH):
        x = hybrid_layer(x, c, w_ada[l], b_ada[l], w_in[l], b_f[l], cmp_pe[l], cmp_w1[l],
                         cmp_w2[l], w_out[l], ln_g[l], ln_b[l])
    return x


def setup_inputs(seed=0):
    out = dict(first_inputs(seed))
    for name, value in second_inputs(seed + 1).items():
        if name != "x":
            out[name + "_2"] = value
    return out


def reference(
    x, c, ctx, c_ctx, l0_mod_w, l0_mod_b, l0_mix_pre_g, l0_mix_post_g, l0_w_in, l0_mlstm_gate_b,
    l0_mlstm_conv_w, l0_mlstm_norm_g, l0_lambda_q1, l0_lambda_k1, l0_lambda_q2, l0_lambda_k2,
    l0_diff_norm_g, l0_w_out, l0_ffn_pre_g, l0_ffn_post_g, l0_ffn_w1, l0_ffn_w3, l0_ffn_w2,
    l1_mod_w, l1_mod_b, l1_mix_pre_g, l1_mix_post_g, l1_conv_pw1_w, l1_conv_pw1_b, l1_conv_dw_w,
    l1_conv_dw_b, l1_conv_ln_g, l1_conv_ln_b, l1_conv_pw2_w, l1_conv_pw2_b, l1_ffn_pre_g,
    l1_ffn_post_g, l1_router_w, l1_moe_w1, l1_moe_w3, l1_moe_w2, c_2, w_ada_2, b_ada_2, w_in_2,
    b_f_2, cmp_pe_2, cmp_w1_2, cmp_w2_2, w_out_2, ln_g_2, ln_b_2,
):
    x = first_block(
        x, c, ctx, c_ctx, l0_mod_w, l0_mod_b, l0_mix_pre_g, l0_mix_post_g, l0_w_in,
        l0_mlstm_gate_b, l0_mlstm_conv_w, l0_mlstm_norm_g, l0_lambda_q1, l0_lambda_k1,
        l0_lambda_q2, l0_lambda_k2, l0_diff_norm_g, l0_w_out, l0_ffn_pre_g, l0_ffn_post_g,
        l0_ffn_w1, l0_ffn_w3, l0_ffn_w2, l1_mod_w, l1_mod_b, l1_mix_pre_g, l1_mix_post_g,
        l1_conv_pw1_w, l1_conv_pw1_b, l1_conv_dw_w, l1_conv_dw_b, l1_conv_ln_g, l1_conv_ln_b,
        l1_conv_pw2_w, l1_conv_pw2_b, l1_ffn_pre_g, l1_ffn_post_g, l1_router_w, l1_moe_w1,
        l1_moe_w3, l1_moe_w2,
    )
    return second_block(
        x, c_2, w_ada_2, b_ada_2, w_in_2, b_f_2, cmp_pe_2, cmp_w1_2, cmp_w2_2, w_out_2, ln_g_2,
        ln_b_2,
    )


_drawn_inputs = setup_inputs


def setup_inputs(seed=0):
    import zlib

    import numpy as np

    out = dict(_drawn_inputs(seed))
    spreads = {}
    factors = {'l0_mlstm_norm_g': 3.632,
     'l0_lambda_q2': 2.957,
     'l1_conv_pw1_b': 4.3,
     'l1_conv_dw_b': 3.715,
     'l1_conv_ln_b': 3.53,
     'l1_conv_pw2_b': 3.745,
     'l1_ffn_post_g': 4.037,
     'b_ada_2': 8.0,
     'cmp_pe_2': 8.0,
     'ln_g_2': 3.985,
     'ln_b_2': 3.884}
    for name, (base, spread) in spreads.items():
        noise = np.random.default_rng([zlib.crc32(name.encode()), seed]).standard_normal(out[name].shape)
        drawn = base * np.exp(spread * noise) if base else spread * noise
        out[name] = jnp.asarray(drawn.astype(out[name].dtype))
    for name, factor in factors.items():
        out[name] = (out[name] * factor).astype(out[name].dtype)
    return out
```

```python
from contextlib import ExitStack
import math

import numpy as np

import concourse.bass as bass
from concourse import mybir

F32 = mybir.dt.float32
ALU = mybir.AluOpType
ACT = mybir.ActivationFunctionType
AX = mybir.AxisListType.X

P = 128
D = 1024
KT = D // P
T = 256
C = 256
TT = T // P
FF = 2816
FT = FF // P
NE = 8
BLOCKS = 16
CH = BLOCKS * P
RING = 11
NEG = -1e30
FLOOR = -1e20
EPS = 1e-6
LN_EPS = 1e-5
ALPHA = (2.0 * 2) ** 0.25
LAM_INIT = 0.8 - 0.6 * math.exp(-0.3 * 0)
NC = 15
TOPK = 64
CAP = 96
LAYERS = 2

MOD_CH = 6 * D // P // 2
IN0_CH = 15
OUT_CH = KT * KT // BLOCKS
FFN_CH = 3 * KT * FT // BLOCKS
PW1_CH = 2 * OUT_CH
ADA_CH = 3 * D // P // 2
IN2_CH = 17
CMP_CH = 4
L2_CH = ADA_CH + IN2_CH + CMP_CH + OUT_CH



def const_table():
    i = np.arange(P)
    r, c = i[:, None], i[None, :]
    t = {}
    t["ones"] = np.ones((P, P))
    t["ident"] = (r == c) * 1.0

    def rot(half, period):
        m = np.zeros((P, P))
        for o in range(P):
            k = o % period
            if k < half:
                m[o + half, o] = -1.0
            else:
                m[o - half, o] = 1.0
        return m

    t["rot_ax"] = rot(16, 32)
    t["rot64"] = rot(32, 64)
    t["rot32"] = rot(16, 32)
    tok = np.arange(T, dtype=np.float32)
    row, col = np.floor(tok / 64).astype(np.float32), (tok % 64).astype(np.float32)
    inv_ax = (np.float32(10000.0) ** (-np.arange(0, 32, 2, dtype=np.float32) / 32)).astype(np.float32)
    ang = np.zeros((P, T), np.float32)
    for o in range(P):
        ang[o] = (row if (o % 64) < 32 else col) * inv_ax[o % 16]
    t["cos_ax"], t["sin_ax"] = np.cos(ang), np.sin(ang)
    for name, half in (("64", 32), ("32", 16)):
        inv = (np.float32(10000.0) ** (-np.arange(half, dtype=np.float32) / half)).astype(np.float32)
        ang = inv[i % half][:, None] * tok[None, :]
        t["cos" + name], t["sin" + name] = np.cos(ang), np.sin(ang)
    s = np.arange(T)[None, :]
    t["ncum"] = np.concatenate([-1.0 * (r + P * k <= s) for k in range(TT)], 1)
    cd = np.where(c > r, NEG, 0.0)
    t["cmask"] = np.concatenate([cd, np.zeros((P, P)), cd], 1)
    t["fmask"] = np.concatenate([np.where(c < r, NEG, 0.0)] * 2, 1)
    t["bmask"] = np.concatenate([np.where(c > r, NEG, 0.0)] * 2, 1)
    cend = 16 * np.arange(16)[None, :] + 31
    t["cmpmask"] = np.concatenate([np.where((cend <= r + P * k) & (np.arange(16)[None, :] < NC), 0.0, NEG)
                                   for k in range(TT)], 1)
    t["iota"] = np.broadcast_to(np.arange(CAP)[None, :], (P, CAP))
    return t


def offsets(widths):
    at, out = 0, {}
    for n, w in widths:
        out[n] = (at, w)
        at += w
    return out, at


CONST_W = [("ones", P), ("ident", P), ("rot_ax", P), ("rot64", P), ("rot32", P), ("cos_ax", T), ("sin_ax", T),
           ("cos64", T), ("sin64", T), ("cos32", T), ("sin32", T), ("ncum", TT * T), ("cmask", 3 * P),
           ("fmask", T), ("bmask", T), ("cmpmask", TT * 16), ("iota", CAP)]
CONST_AT, CONST_N = offsets(CONST_W)

SMALL_W = [("c", 8), ("c_ctx", 8), ("mod_b0", 48), ("pre0", 8), ("post0", 8), ("gate_b", 4), ("conv_w", 24),
           ("mnorm", 4), ("lam", 4), ("dnorm", 4), ("fpre0", 8), ("fpost0", 8), ("mod_b1", 48), ("pre1", 8),
           ("post1", 8), ("pw1_b", 16), ("dw_w", 31 * 8), ("dw_b", 8), ("ln_g", 8), ("ln_b", 8), ("pw2_b", 8),
           ("fpre1", 8), ("fpost1", 8), ("router", 64), ("c2", 8)]
SMALL_AT, SMALL_N = offsets(SMALL_W)
LAYER_W = [("b_ada", 24), ("pe_k", 32), ("pe_v", 32), ("ln_g2", 8), ("ln_b2", 8), ("b_f", 6)]
LAYER_AT, LAYER_N = offsets(LAYER_W)



class Stream:

    def __init__(self, nc, ring, dram, sems):
        self.nc, self.ring, self.dram, self.landed = nc, ring, dram, sems
        self.used = self.issued = 0
        self.total = 0
        self.base = 0

    def begin(self, base, total):
        self.used = self.issued = 0
        self.total, self.base = total, base

    def chunk(self, g):
        return self.ring[:, (g % RING) * CH:(g % RING + 1) * CH]

    def wait(self, eng, g):
        eng.wait_ge(self.landed[g % RING], 16 * (g // RING + 1))

    def load(self, sp, first, n, freed):
        last = min(first + n + RING, self.total)
        for g in range(self.issued, last):
            old = g - RING
            if old >= first and old - first < n:
                sp.wait_ge(*freed[old - first])
            sp.dma_start(self.chunk(g), self.dram[self.base + g]).then_inc(self.landed[g % RING], 16)
        self.issued = max(self.issued, last)
        self.used = first + n

    def clear(self):
        for s in self.landed:
            self.nc.gpsimd.sem_clear(s)
        self.nc.all_engine_barrier()


class Stage:

    def __init__(self, nc, name, sems):
        self.nc, self.name, self.names = nc, name, sems

    def __enter__(self):
        self.stack = ExitStack()
        self.sems = {n: self.stack.enter_context(self.nc.semaphore(f"{self.name}_{n}")) for n in self.names}
        self.inner = ExitStack()
        self.block = self.inner.enter_context(self.nc.Block())
        return self.block, [self.sems[n] for n in self.names]

    def __exit__(self, *a):
        self.inner.close()
        for s in self.sems.values():
            self.nc.gpsimd.sem_clear(s)
        self.nc.all_engine_barrier()
        self.stack.close()


class Chain:

    def __init__(self, eng, sem):
        self.eng, self.sem, self.n = eng, sem, 0

    def __call__(self, ins):
        self.n += 1
        ins.then_inc(self.sem, 1)
        self.eng.wait_ge(self.sem, self.n)


def build(nc, a):
    ctx = ExitStack()
    with ctx:
        def sb(name, n):
            return ctx.enter_context(nc.sbuf_tensor("sb_" + name, [P, n], F32))

        ring = sb("ring", RING * CH)
        consts = sb("consts", CONST_N)
        small = sb("small", SMALL_N)
        layer_small = sb("layer_small", LAYER_N)
        XT = sb("XT", KT * T)[:, :].rearrange("p (k t) -> p k t", k=KT)
        U2 = sb("U2", KT * 2 * T)[:, :].rearrange("p (k t) -> p k t", k=KT)
        YT = sb("YT", KT * T)[:, :].rearrange("p (k t) -> p k t", k=KT)
        mod = sb("mod", 48)
        modc = sb("modc", 16)
        coef = sb("coef", 16)
        cs = sb("cs", 24)
        rstd = sb("rstd", T)
        mean = sb("mean", T)
        lam = sb("lam", 8)
        arena = sb("arena", 17440)
        full_flag = ctx.enter_context(nc.sbuf_tensor("full_flag", [P, NE], mybir.dt.int32))
        PS = ctx.enter_context(nc.psum_tensor("PS", [P, 8, 512], F32))
        UX = U2[:, :, C:C + T]
        UC = U2[:, :, 0:C]

        def const(name):
            at, w = CONST_AT[name]
            return consts[:, at:at + w]

        def sm(name, i=0, n=None):
            at, w = SMALL_AT[name]
            return small[:, at + i:at + (w if n is None else i + n)]

        def lsm(name, i=0, n=None):
            at, w = LAYER_AT[name]
            return layer_small[:, at + i:at + (w if n is None else i + n)]

        ones, ident = const("ones"), const("ident")

        def area(at, n):
            return arena[:, at:at + n]

        landed = [ctx.enter_context(nc.semaphore(f"landed{i}")) for i in range(RING)]
        ws = Stream(nc, ring, a["stream"], landed)

        def bc(ap2, k):
            return ap2.unsqueeze(1).broadcast_to([ap2.shape[0], k, ap2.shape[1]])


        def modulation(name, n, vec, bias, out, n_ctx=0, out_ctx=None, vec_ctx=None):
            acc = area(0, 4 * 256).rearrange("p (b n) -> p b n", b=4)
            first = ws.used
            jobs = []
            for k in range(n):
                jobs.append((k, vec, 2 * k))
                if k < n_ctx:
                    jobs.append((k, vec_ctx, 64 + 2 * k))
            last = {k: j + 1 for j, (k, _, _) in enumerate(jobs)}
            with Stage(nc, name, ["chain", "acc_ready", "acc_used", "done"]) as (block, (chain, acc_ready, acc_used, done)):
                @block.sync
                def _(sp):
                    ws.load(sp, first, n, [(acc_ready, last[k]) for k in range(n)])

                @block.vector
                def _(dve):
                    link = Chain(dve, chain)
                    for j, (k, v, _) in enumerate(jobs):
                        ws.wait(dve, first + k)
                        if j >= 4:
                            dve.wait_ge(acc_used, j - 3)
                        w = ws.chunk(first + k).rearrange("p (n k c) -> p n k c", n=2, k=KT)
                        o = acc[:, j % 4, :].rearrange("p (n c) -> p n c", n=2)
                        link(dve.tensor_scalar(o, w[:, :, 0, :], v[:, 0:1], None, ALU.mult))
                        for kt in range(1, KT):
                            ins = dve.scalar_tensor_tensor(out=o, in0=w[:, :, kt, :], scalar=v[:, kt:kt + 1], in1=o,
                                                           op0=ALU.mult, op1=ALU.add)
                            if kt < KT - 1:
                                link(ins)
                        ins.then_inc(acc_ready, 1)
                    dve.wait_ge(acc_used, len(jobs))
                    ins = dve.tensor_tensor(out[:, 0:2 * n], PS[:, 0, 0:2 * n], bias, ALU.add)
                    if n_ctx:
                        link(ins)
                        ins = dve.tensor_tensor(out_ctx[:, 0:2 * n_ctx], PS[:, 0, 64:64 + 2 * n_ctx],
                                                bias[:, 0:2 * n_ctx], ALU.add)
                    ins.then_inc(done, 1)

                @block.tensor
                def _(pe):
                    for j, (_, _, col) in enumerate(jobs):
                        pe.wait_ge(acc_ready, j + 1)
                        for h in range(2):
                            ins = pe.matmul(PS[:, 0, col + h:col + h + 1], acc[:, j % 4, h * P:(h + 1) * P],
                                            ones[:, 0:1], start=True, stop=True)
                        ins.then_inc(acc_used, 1)

        def norm(name, src, apply, center=False, eps=EPS):
            sq = area(0, KT * T).rearrange("p (k t) -> p k t", k=KT)
            with Stage(nc, name, ["chain", "sq_ready", "sum_ready", "mean_ready", "var_ready", "std_ready", "done"]) as (
                    block, (chain, sq_ready, sum_ready, mean_ready, var_ready, std_ready, done)):
                @block.scalar
                def _(act):
                    if center:
                        act.wait_ge(mean_ready, 1)
                    for k in range(KT):
                        nc.scalar.activation(sq[:, k, :], src[:, k, :], ACT.Square).then_inc(sq_ready, 1)
                    act.wait_ge(var_ready, 1)
                    nc.scalar.activation(rstd[:, :], rstd[:, :], ACT.Sqrt).then_inc(std_ready, 1)

                @block.tensor
                def _(pe):
                    if center:
                        for k in range(KT):
                            ins = pe.matmul(PS[:, 1, 0:T], ones, src[:, k, :], start=(k == 0), stop=(k == KT - 1))
                        ins.then_inc(sum_ready, 1)
                    for k in range(KT):
                        pe.wait_ge(sq_ready, k + 1)
                        ins = pe.matmul(PS[:, 0, 0:T], ones, sq[:, k, :], start=(k == 0), stop=(k == KT - 1))
                    ins.then_inc(sum_ready, 1)

                @block.vector
                def _(dve):
                    link = Chain(dve, chain)
                    if center:
                        dve.wait_ge(sum_ready, 1)
                        link(dve.tensor_scalar(mean[:, :], PS[:, 1, 0:T], 1.0 / D, None, ALU.mult))
                        dve.tensor_tensor(src, src, bc(mean[:, :], KT), ALU.subtract).then_inc(mean_ready, 1)
                        dve.wait_ge(mean_ready, 1)
                    dve.wait_ge(sum_ready, 2 if center else 1)
                    dve.tensor_scalar(rstd[:, :], PS[:, 0, 0:T], 1.0 / D, eps, ALU.mult, ALU.add).then_inc(var_ready, 1)
                    dve.wait_ge(std_ready, 1)
                    link(dve.reciprocal(rstd[:, :], rstd[:, :]))
                    apply(dve, link)

        def modulated(name, src, dst, g, shift, scale):
            tmp = area(KT * T, KT * T).rearrange("p (k t) -> p k t", k=KT)

            def apply(dve, link):
                link(dve.scalar_tensor_tensor(out=coef[:, 0:KT], in0=scale, scalar=1.0, in1=g, op0=ALU.add, op1=ALU.mult))
                link(dve.tensor_tensor(tmp, src, bc(rstd[:, :], KT), ALU.mult))
                for k in range(KT):
                    link(dve.tensor_scalar(dst[:, k, :], tmp[:, k, :], coef[:, k:k + 1], shift[:, k:k + 1],
                                           ALU.mult, ALU.add))
            norm(name, src, apply)

        def residual(name, src, g, gate):
            def apply(dve, link):
                link(dve.tensor_tensor(coef[:, 0:KT], gate, g, ALU.mult))
                link(dve.tensor_tensor(src, src, bc(rstd[:, :], KT), ALU.mult))
                for k in range(KT):
                    link(dve.scalar_tensor_tensor(out=XT[:, k, :], in0=src[:, k, :], scalar=coef[:, k:k + 1],
                                                  in1=XT[:, k, :], op0=ALU.mult, op1=ALU.add))
            norm(name, src, apply)

        def project(name, n, tasks):
            first = ws.used
            nb = 8
            count = {"act": 0, "dve": 0}
            emptied = []
            for t in tasks:
                count[t[2]] += 1
                emptied.append((t[2], count[t[2]]))
            last = {}
            for j, t in enumerate(tasks):
                last[t[0]] = j + 1
            with Stage(nc, name, ["chain_d", "chain_a", "bank_full", "act_emptied", "dve_emptied"]) as (
                    block, (chain_d, chain_a, bank_full, act_emptied, dve_emptied)):
                by = {"act": act_emptied, "dve": dve_emptied}

                @block.sync
                def _(sp):
                    ws.load(sp, first, n, [(bank_full, last[k]) for k in range(n)])

                @block.tensor
                def _(pe):
                    for j, (k, matmuls, _, _) in enumerate(tasks):
                        ws.wait(pe, first + k)
                        if j >= nb:
                            e, v = emptied[j - nb]
                            pe.wait_ge(by[e], v)
                        for o, l, r, s, e in matmuls(PS[:, j % nb, :], ws.chunk(first + k)):
                            ins = pe.matmul(o, l, r, start=s, stop=e)
                        ins.then_inc(bank_full, 1)

                def evacuate(eng, who, link):
                    for j, (_, _, e, f) in enumerate(tasks):
                        if e == who:
                            eng.wait_ge(bank_full, j + 1)
                            f(eng, PS[:, j % nb, :], link).then_inc(by[who], 1)

                @block.scalar
                def _(act):
                    evacuate(act, "act", Chain(act, chain_a))

                @block.vector
                def _(dve):
                    evacuate(dve, "dve", Chain(dve, chain_d))

        def tile_task(k, h, rhs, engine, evacuate, ncols=P, c0=0):
            def matmuls(bank, chunk):
                w = chunk.rearrange("p (n k c) -> p n k c", n=2, k=KT)
                N = rhs.shape[2]
                return [(bank[0:ncols, 0:N], w[:, h, kt, c0:c0 + ncols], rhs[:, kt, :], kt == 0, kt == KT - 1)
                        for kt in range(KT)]
            return (k, matmuls, engine, evacuate)

        def token_task(k, lhs, t0, engine, evacuate):
            def matmuls(bank, chunk):
                w = chunk.rearrange("p (n k c) -> p n k c", n=2, k=KT)
                o = bank[:, 0:2 * P].rearrange("p (n c) -> p n c", n=2)
                return [(o, lhs[:, kt, t0:t0 + P], w[:, :, kt, :], kt == 0, kt == KT - 1) for kt in range(KT)]
            return (k, matmuls, engine, evacuate)

        def copy_to(dst, n=None, scale=1.0):
            def f(act, bank, link):
                o = dst
                src = bank[0:dst.shape[0], 0:dst.shape[1]] if len(dst.shape) == 2 else \
                    bank[:, 0:dst.shape[1] * dst.shape[2]].rearrange("p (a b) -> p a b", a=dst.shape[1])
                return nc.scalar.activation(o, src, ACT.Copy, scale=scale)
            return f

        def copy_bias(dst, b):
            def f(act, bank, link):
                return nc.scalar.activation(dst, bank[:, 0:dst.shape[1]], ACT.Identity, bias=b)
            return f

        def pointwise(name, steps):
            with Stage(nc, name, ["step_done"]) as (block, (step_done,)):
                def run(eng, who):
                    for i, (w, f) in enumerate(steps):
                        if w == who:
                            if i:
                                eng.wait_ge(step_done, i)
                            f(eng).then_inc(step_done, 1)
                    eng.nop()

                @block.scalar
                def _(act):
                    run(act, "act")

                @block.vector
                def _(dve):
                    run(dve, "dve")

                @block.tensor
                def _(pe):
                    run(pe, "pe")

                @block.gpsimd
                def _(pool):
                    run(pool, "pool")

        def sigmoid_steps(src, dst):
            return [("act", lambda e: nc.scalar.activation(dst, src, ACT.Exp, scale=-1.0)),
                    ("dve", lambda e: e.tensor_scalar(dst, dst, 1.0, None, ALU.add)),
                    ("dve", lambda e: e.reciprocal(dst, dst))]

        def silu_steps(x, tmp, extra=1.0):
            return sigmoid_steps(x, tmp) + [
                ("dve", lambda e: e.scalar_tensor_tensor(out=x, in0=x, scalar=extra, in1=tmp, op0=ALU.mult, op1=ALU.mult))]

        def log_sigmoid_steps(z, t1, t2):
            return [("dve", lambda e: e.scalar_tensor_tensor(out=t1, in0=z, scalar=-1.0, in1=z, op0=ALU.mult, op1=ALU.max)),
                    ("act", lambda e: nc.scalar.activation(t1, t1, ACT.Exp, scale=-1.0)),
                    ("dve", lambda e: e.tensor_scalar(t1, t1, 1.0, None, ALU.add)),
                    ("act", lambda e: nc.scalar.activation(t2, t1, ACT.Ln)),
                    ("dve", lambda e: e.scalar_tensor_tensor(out=z, in0=z, scalar=0.0, in1=t2, op0=ALU.min, op1=ALU.subtract))]

        def rope(name, tiles, tmp_at):
            tmp = area(tmp_at, 2 * T).rearrange("p (b t) -> p b t", b=2)
            with Stage(nc, name, ["chain", "rotated", "done"]) as (block, (chain, rotated, done)):
                @block.tensor
                def _(pe):
                    for j, (x, m, _, _) in enumerate(tiles):
                        if j >= 4:
                            pe.wait_ge(done, j - 3)
                        pe.matmul(PS[:, j % 4, 0:T], const(m), x, start=True, stop=True).then_inc(rotated, 1)

                @block.vector
                def _(dve):
                    link = Chain(dve, chain)
                    for j, (x, _, c, s) in enumerate(tiles):
                        dve.wait_ge(rotated, j + 1)
                        link(dve.tensor_tensor(tmp[:, 0, :], PS[:, j % 4, 0:T], const(s), ALU.mult))
                        link(dve.tensor_tensor(tmp[:, 1, :], x, const(c), ALU.mult))
                        dve.tensor_tensor(x, tmp[:, 0, :], tmp[:, 1, :], ALU.add).then_inc(done, 1)
                        dve.wait_ge(done, j + 1)

        def ffn(name, src, expert=None, gates=None):
            H = area(0, FT * T).rearrange("p (k t) -> p k t", k=FT)
            EX = area(FT * T, 2 * T).rearrange("p (b t) -> p b t", b=2)
            TMP = area(FT * T + 2 * T, 2 * T).rearrange("p (b t) -> p b t", b=2)
            first = ws.used
            n2 = KT * FT // BLOCKS
            with Stage(nc, name, ["chain", "pair_ready", "exp_ready", "hidden_done", "w2_chunk", "y_ready", "y_done"]) as (
                    block, (chain, pair_ready, exp_ready, hidden_done, w2_chunk, y_ready, y_done)):
                @block.sync
                def _(sp):
                    ws.load(sp, first, FFN_CH, [(pair_ready, m + 1) for m in range(FT)] +
                            [(w2_chunk, q + 1) for q in range(n2 - 1)] + [(y_ready, KT)])

                @block.tensor
                def _(pe):
                    for m in range(FT):
                        ws.wait(pe, first + m)
                        if m >= 4:
                            pe.wait_ge(hidden_done, m - 3)
                        w = ws.chunk(first + m).rearrange("p (n k c) -> p n k c", n=2, k=KT)
                        for h in range(2):
                            for kt in range(KT):
                                ins = pe.matmul(PS[:, m % 4, h * T:(h + 1) * T], w[:, h, kt, :], src[:, kt, :],
                                                start=(kt == 0), stop=(kt == KT - 1))
                        ins.then_inc(pair_ready, 1)
                    b = 0
                    for o in range(KT):
                        if o >= 4:
                            pe.wait_ge(y_done, o - 3)
                        for m in range(FT):
                            if b % BLOCKS == 0:
                                ws.wait(pe, first + FT + b // BLOCKS)
                            if o == 0:
                                pe.wait_ge(hidden_done, m + 1)
                            w = ws.chunk(first + FT + b // BLOCKS)
                            ins = pe.matmul(PS[:, 4 + o % 4, 0:T], w[:, (b % BLOCKS) * P:(b % BLOCKS + 1) * P], H[:, m, :],
                                            start=(m == 0), stop=(m == FT - 1))
                            if m == FT - 1:
                                ins.then_inc(y_ready, 1)
                            elif b % BLOCKS == BLOCKS - 1:
                                ins.then_inc(w2_chunk, 1)
                            b += 1

                @block.scalar
                def _(act):
                    for m in range(FT):
                        act.wait_ge(pair_ready, m + 1)
                        if m >= 2:
                            act.wait_ge(hidden_done, m - 1)
                        nc.scalar.activation(EX[:, m % 2, :], PS[:, m % 4, 0:T], ACT.Exp, scale=-1.0).then_inc(exp_ready, 1)
                    if expert is None:
                        for o in range(KT):
                            act.wait_ge(y_ready, o + 1)
                            nc.scalar.activation(YT[:, o, :], PS[:, 4 + o % 4, 0:T], ACT.Copy).then_inc(y_done, 1)

                @block.vector
                def _(dve):
                    link = Chain(dve, chain)
                    for m in range(FT):
                        e = EX[:, m % 2, :]
                        dve.wait_ge(exp_ready, m + 1)
                        link(dve.tensor_scalar(e, e, 1.0, None, ALU.add))
                        link(dve.reciprocal(e, e))
                        link(dve.tensor_tensor(e, PS[:, m % 4, 0:T], e, ALU.mult))
                        dve.tensor_tensor(H[:, m, :], PS[:, m % 4, T:2 * T], e, ALU.mult).then_inc(hidden_done, 1)
                    if expert is not None:
                        for o in range(KT):
                            dve.wait_ge(y_ready, o + 1)
                            link(dve.tensor_tensor(TMP[:, o % 2, :], PS[:, 4 + o % 4, 0:T], gates[:, expert, :], ALU.mult))
                            dve.tensor_tensor(YT[:, o, :], YT[:, o, :], TMP[:, o % 2, :], ALU.add).then_inc(y_done, 1)
                    dve.nop()

        def attention(name, jobs, scale, at):
            SB = area(at, 2 * 1024).rearrange("p (j b n) -> p j b n", j=2, b=2)
            PB = area(at + 2048, 2 * 1024).rearrange("p (j b n) -> p j b n", j=2, b=2)
            PT = area(at + 4096, 2 * 640).rearrange("p (j n) -> p j n", j=2)
            ST = mean[:, 0:32].rearrange("p (j n) -> p j n", j=2)
            n = len(jobs)
            nbr = [len(j["branches"]) for j in jobs]
            cum = [sum(nbr[:i + 1]) for i in range(n)]
            with Stage(nc, name, ["chain", "scores", "negmax", "exps", "probs", "turned", "turned_used", "out_ready", "out_done"]) as (
                    block, (chain, scores, negmax, exps, probs, turned, copied, out_ready, out_done)):
                def sc_ps(i, br):
                    return PS[:, 2 * (i % 2) + br["bank"], br["off"]:br["off"] + br["n"]]

                def pieces(job):
                    out = []
                    at_ = 0
                    for bi, br in enumerate(job["branches"]):
                        if br.get("minus"):
                            continue
                        k0 = 0
                        for v in br["v"]:
                            rows = v.shape[0]
                            out.append((bi, k0, rows, at_, v))
                            k0 += rows
                            at_ += P
                    return out

                def turned_ps(i, at_):
                    return PS[:, 4 + i % 2, at_:at_ + P] if at_ < 512 else PS[:, 2 * (i % 2) + 1, P:2 * P]

                @block.tensor
                def _(pe):
                    for i in range(n + 2):
                        if i < n:
                            if i >= 2:
                                pe.wait_ge(exps, cum[i - 2])
                                if len(pieces(jobs[i - 2])) > 4:
                                    pe.wait_ge(copied, i - 1)
                            for br in jobs[i]["branches"]:
                                ins = pe.matmul(sc_ps(i, br), br["q"], br["k"], start=True, stop=True)
                            ins.then_inc(scores, 1)
                        if 0 <= i - 1 < n:
                            q = i - 1
                            pe.wait_ge(probs, q + 1)
                            if q >= 2:
                                pe.wait_ge(copied, q - 1)
                            for bi, k0, rows, at_, _v in pieces(jobs[q]):
                                br = jobs[q]["branches"][bi]
                                src = PB[:, q % 2, br["bank"], br["off"] + k0:br["off"] + k0 + rows]
                                ins = pe.transpose(turned_ps(q, at_)[0:rows, :], src, ident)
                            ins.then_inc(turned, 1)
                        if 0 <= i - 2 < n:
                            q = i - 2
                            pe.wait_ge(copied, q + 1)
                            if q >= 2:
                                pe.wait_ge(out_done, q - 1)
                            ps = pieces(jobs[q])
                            for z, (bi, k0, rows, at_, v) in enumerate(ps):
                                p_ = PT[0:rows, q % 2, at_:at_ + P]
                                if jobs[q].get("token_major"):
                                    o, l, r = PS[:, 6 + q % 2, 0:v.shape[1]], p_, v
                                else:
                                    b0 = jobs[q]["base"]
                                    o, l, r = PS[b0:b0 + v.shape[1], 6 + q % 2, 0:P], v, p_
                                ins = pe.matmul(o, l, r, start=(z == 0), stop=(z == len(ps) - 1))
                            ins.then_inc(out_ready, 1)

                @block.vector
                def _(dve):
                    link = Chain(dve, chain)
                    for i in range(n + 1):
                        if i < n:
                            dve.wait_ge(scores, i + 1)
                            if i >= 2:
                                dve.wait_ge(exps, cum[i - 2])
                            brs = jobs[i]["branches"]
                            for bi, br in enumerate(brs):
                                m = ST[:, i % 2, bi:bi + 1]
                                if br["bias"] is not None:
                                    s = SB[:, i % 2, br["bank"], br["off"]:br["off"] + br["n"]]
                                    link(dve.scalar_tensor_tensor(out=s, in0=sc_ps(i, br), scalar=scale, in1=br["bias"],
                                                                  op0=ALU.mult, op1=ALU.add))
                                    f = -1.0
                                else:
                                    s, f = sc_ps(i, br), -scale
                                link(dve.reduce_max(m, s, AX))
                                dve.tensor_scalar(ST[:, i % 2, 4 + bi:5 + bi], m, FLOOR, f, ALU.max, ALU.mult).then_inc(negmax, 1)
                        if i >= 1:
                            q = i - 1
                            dve.wait_ge(exps, cum[q])
                            if q >= 2:
                                dve.wait_ge(turned, q - 1)
                            brs = jobs[q]["branches"]
                            nb_ = len(brs)
                            S_ = ST[:, q % 2, :]
                            link(dve.tensor_scalar(S_[:, 8:8 + nb_], S_[:, 8:8 + nb_], 1e-30, None, ALU.max))
                            link(dve.reciprocal(S_[:, 12:12 + nb_], S_[:, 8:8 + nb_]))
                            for bi, br in enumerate(brs):
                                r_ = S_[:, 12 + bi:13 + bi]
                                if br["coef"] is not None:
                                    link(dve.tensor_tensor(r_, r_, br["coef"], ALU.mult))
                                p_ = PB[:, q % 2, br["bank"], br["off"]:br["off"] + br["n"]]
                                if br.get("minus"):
                                    o_ = PB[:, q % 2, 0, 0:br["n"]]
                                    ins = dve.scalar_tensor_tensor(out=o_, in0=p_, scalar=r_, in1=o_, op0=ALU.mult, op1=ALU.add)
                                else:
                                    ins = dve.tensor_scalar(p_, p_, r_, None, ALU.mult)
                                if bi < nb_ - 1:
                                    link(ins)
                            ins.then_inc(probs, 1)

                @block.scalar
                def _(act):
                    ne = 0
                    for i in range(n + 2):
                        if i < n:
                            if i >= 2:
                                act.wait_ge(turned, i - 1)
                            for bi, br in enumerate(jobs[i]["branches"]):
                                ne += 1
                                act.wait_ge(negmax, ne)
                                p_ = PB[:, i % 2, br["bank"], br["off"]:br["off"] + br["n"]]
                                if br["bias"] is not None:
                                    s, f = SB[:, i % 2, br["bank"], br["off"]:br["off"] + br["n"]], 1.0
                                else:
                                    s, f = sc_ps(i, br), scale
                                nc.scalar.activation(p_, s, ACT.Exp, bias=ST[:, i % 2, 4 + bi:5 + bi], scale=f,
                                                     accum_out=ST[:, i % 2, 8 + bi:9 + bi]).then_inc(exps, 1)
                        if 0 <= i - 1 < n:
                            q = i - 1
                            act.wait_ge(turned, q + 1)
                            if q >= 2:
                                act.wait_ge(out_ready, q - 1)
                            ps = pieces(jobs[q])
                            full = [x for x in ps if x[3] < 512]
                            w_ = P * len(full)
                            rows = full[0][2]
                            ins = nc.scalar.activation(PT[0:rows, q % 2, 0:w_], PS[0:rows, 4 + q % 2, 0:w_], ACT.Copy)
                            if len(ps) > len(full):
                                rows = ps[-1][2]
                                ins = nc.scalar.activation(PT[0:rows, q % 2, 512:512 + P],
                                                           turned_ps(q, 512)[0:rows, :], ACT.Copy)
                            ins.then_inc(copied, 1)
                        if 0 <= i - 2 < n:
                            q = i - 2
                            act.wait_ge(out_ready, q + 1)
                            o = jobs[q]["out"]
                            if jobs[q].get("token_major"):
                                s = PS[:, 6 + q % 2, 0:o.shape[1]]
                            else:
                                b0 = jobs[q]["base"]
                                s = PS[b0:b0 + o.shape[0], 6 + q % 2, 0:P]
                            nc.scalar.activation(o, s, ACT.Copy).then_inc(out_done, 1)


        with Stage(nc, "load", ["loaded", "step"]) as (block, (loaded, step)):
            @block.sync
            def _(sp):
                for dst, src in ((consts[:, :], a["consts"]), (small[:, :], a["small"]),
                                 (XT, a["xT"]), (UC, a["ctxT"])):
                    sp.dma_start(dst, src).then_inc(loaded, 16)

            @block.vector
            def _(dve):
                dve.wait_ge(loaded, 64)
                dve.memset(mod[:, :], 0.0).then_inc(step, 1)
                dve.wait_ge(step, 1)
                dve.nop()

        silu_in = small[:, SMALL_AT["c"][0]:SMALL_AT["c"][0] + 16]
        lq = sm("lam")
        pointwise("silu_c", sigmoid_steps(silu_in, cs[:, 0:16]) + [
            ("dve", lambda e: e.tensor_tensor(cs[:, 0:16], cs[:, 0:16], silu_in, ALU.mult)),
            ("dve", lambda e: e.tensor_tensor(lam[:, 0:2], lq[:, 0:2], lq[:, 2:4], ALU.mult)),
            ("pe", lambda e: e.matmul(PS[:, 0, 0:2], ones[0:64, :], lam[0:64, 0:2], start=True, stop=True)),
            ("act", lambda e: nc.scalar.activation(lam[:, 2:4], PS[:, 0, 0:2], ACT.Exp)),
            ("dve", lambda e: e.tensor_tensor(lam[:, 4:5], lam[:, 3:4], lam[:, 2:3], ALU.subtract)),
            ("dve", lambda e: e.tensor_scalar(lam[:, 5:6], lam[:, 4:5], -LAM_INIT, None, ALU.add))])

        ws.begin(0, MOD_CH + IN0_CH + OUT_CH + FFN_CH + MOD_CH + PW1_CH + OUT_CH)
        modulation("mod0", MOD_CH, cs[:, 0:8], sm("mod_b0"), mod, 8, modc, cs[:, 8:16])

        def mpart(i):
            return mod[:, KT * i:KT * (i + 1)]

        modulated("norm_ctx", UC, UC, sm("pre0"), modc[:, 0:8], modc[:, 8:16])
        modulated("norm_x", XT, UX, sm("pre0"), mpart(0), mpart(1))

        qm = area(0, 1024).rearrange("p (k t) -> p k t", k=4)
        km = area(1024, 2048).rearrange("p (k t) -> p k t", k=4)
        vm = area(3072, 2080).rearrange("p (s h d) -> p s h d", s=4, h=8)
        om = area(5152, 1024).rearrange("p (k t) -> p k t", k=4)
        gt = area(6176, 2048).rearrange("p (g t) -> p g t", g=4)
        dq = area(8224, 1024).rearrange("p (k t) -> p k t", k=4)
        dk = area(9248, 2048).rearrange("p (k t) -> p k t", k=4)
        dv = area(11296, 2048).rearrange("p (s n) -> p s n", s=4)
        SCR = 13344
        mixT = YT
        cw = sm("conv_w")

        def conv3(dst, col, segs):
            def f(dve, bank, link):
                for z, (s0, d0) in enumerate(segs):
                    x, y = bank[:, s0:s0 + T], dst[:, d0:d0 + T]
                    link(dve.tensor_scalar(y, x, cw[:, 3 * col + 1:3 * col + 2], None, ALU.mult))
                    link(dve.scalar_tensor_tensor(out=y[:, 1:T], in0=x[:, 0:T - 1], scalar=cw[:, 3 * col:3 * col + 1],
                                                  in1=y[:, 1:T], op0=ALU.mult, op1=ALU.add))
                    ins = dve.scalar_tensor_tensor(out=y[:, 0:T - 1], in0=x[:, 1:T], scalar=cw[:, 3 * col + 2:3 * col + 3],
                                                   in1=y[:, 0:T - 1], op0=ALU.mult, op1=ALU.add)
                    if z < len(segs) - 1:
                        link(ins)
                return ins
            return f

        tasks = []
        for m in range(4):
            tasks.append(tile_task(m // 2, m % 2, UX, "dve", conv3(qm[:, m, :], m, [(0, 0)])))
        for m in range(4):
            tasks.append(tile_task(2 + m // 2, m % 2, U2, "dve", conv3(km[:, m, :], 4 + m, [(0, 0), (C, C)])))

        def copy_v(s, h0):
            def f(act, bank, link):
                return nc.scalar.activation(vm[:, s, h0:h0 + 4, 0:64], bank[:, 0:256].rearrange("p (h d) -> p h d", h=4),
                                            ACT.Copy)
            return f
        for c_ in range(2):
            for s in range(4):
                tasks.append(token_task(4 + c_, U2, s * P, "act", copy_v(s, 4 * c_)))
        for m in range(4):
            tasks.append(tile_task(6 + m // 2, m % 2, UX, "act", copy_to(om[:, m, :])))
        for g in range(4):
            def gate_copy(g):
                def f(act, bank, link):
                    return nc.scalar.activation(gt[0:8, g, :], bank[0:8, 0:512], ACT.Identity, bias=sm("gate_b", g, 1)[0:8, :])
                return f
            tasks.append(tile_task(8, 0, U2, "act", gate_copy(g), ncols=8, c0=8 * g))
        for m in range(4):
            tasks.append(tile_task(9 + m // 2, m % 2, UX, "act", copy_to(dq[:, m, :])))
        for m in range(4):
            tasks.append(tile_task(11 + m // 2, m % 2, U2, "act", copy_to(dk[:, m, :])))
        for c_ in range(2):
            for s in range(4):
                tasks.append(token_task(13 + c_, U2, s * P, "act", copy_to(dv[:, s, 256 * c_:256 * (c_ + 1)])))
        project("in0", IN0_CH, tasks)

        gB = area(SCR, 1024).rearrange("p (d t) -> p d t", d=2)
        gM = area(SCR + 1024, 1024).rearrange("p (d t) -> p d t", d=2)
        gN = area(SCR + 2048, 1024).rearrange("p (d e t) -> p d e t", d=2, e=2)
        tA = area(SCR + 3072, 64).rearrange("p (d s h) -> p d s h", d=2, s=4)
        tM = area(SCR + 3072 + 64, 32).rearrange("p (d s h) -> p d s h", d=2, s=2)
        lf, ig = gt[0:8, 1:4:2, :], gt[0:8, 0:4:2, :]
        o512 = ones[0:8, 0:1].broadcast_to([8, 512])
        B8, M8, A8 = gB[0:8], gM[0:8], gt[0:8, 0:4:2, :]
        steps = log_sigmoid_steps(lf, B8, M8)
        steps += [
            ("dve", lambda e: e.tensor_tensor_scan(B8[:, 0, :], o512, gt[0:8, 1, :], 0.0, ALU.mult, ALU.add)),
            ("dve", lambda e: e.tensor_tensor_scan(B8[:, 1, C - 1::-1], o512[:, 0:C], gt[0:8, 3, C - 1::-1], 0.0, ALU.mult, ALU.add)),
            ("dve", lambda e: e.tensor_tensor_scan(B8[:, 1, 511:C - 1:-1], o512[:, 0:T], gt[0:8, 3, 511:C - 1:-1], B8[:, 1, 0:1], ALU.mult, ALU.add)),
            ("dve", lambda e: e.tensor_tensor(A8, ig, B8, ALU.subtract)),
            ("dve", lambda e: e.tensor_tensor_scan(M8[:, 0, :], gt[0:8, 0, :], gt[0:8, 0, :], NEG, ALU.max, ALU.max)),
            ("dve", lambda e: e.tensor_tensor_scan(M8[:, 1, C - 1::-1], gt[0:8, 2, C - 1::-1], gt[0:8, 2, C - 1::-1], NEG, ALU.max, ALU.max)),
            ("dve", lambda e: e.tensor_tensor_scan(M8[:, 1, 511:C - 1:-1], gt[0:8, 2, 511:C - 1:-1], gt[0:8, 2, 511:C - 1:-1], M8[:, 1, 0:1], ALU.max, ALU.max)),
            ("dve", lambda e: e.tensor_scalar(gN[0:8, :, 0, :], M8[:, :, C:], -1.0, None, ALU.mult)),
            ("dve", lambda e: e.tensor_tensor(B8[:, :, C:], B8[:, :, C:], M8[:, :, C:], ALU.add)),
            ("act", lambda e: nc.scalar.activation(gN[0:8, :, 1, :], B8[:, :, C:], ACT.Exp, scale=-1.0)),
            ("dve", lambda e: e.memset(vm[:, :, :, 64:65], 1.0)),
        ]
        for d in range(2):
            for s in range(4):
                steps.append(("pe", lambda e, d=d, s=s: e.transpose(PS[:, 0, (d * 4 + s) * 8:(d * 4 + s + 1) * 8],
                                                                    gt[0:8, 2 * d, s * P:(s + 1) * P], ident[0:8, 0:8])))
        for d in range(2):
            for s in range(2):
                steps.append(("pe", lambda e, d=d, s=s: e.transpose(PS[:, 0, 64 + (d * 2 + s) * 8:64 + (d * 2 + s + 1) * 8],
                                                                    gN[0:8, d, 1, s * P:(s + 1) * P], ident[0:8, 0:8])))
        steps.append(("act", lambda e: nc.scalar.activation(area(SCR + 3072, 96), PS[:, 0, 0:96], ACT.Copy)))
        steps += silu_steps(area(0, 1024), YT[:, 0:4, :].rearrange("p a b -> p (a b)"), 0.125)
        steps += silu_steps(area(1024, 2048), YT.rearrange("p a b -> p (a b)"))
        pointwise("gates0", steps)

        Hm = area(SCR, 1024).rearrange("p (t h d) -> p t h d", t=2, h=8)
        EE = U2.rearrange("p k t -> p (k t)").rearrange("p (j d s t) -> p j d s t", j=2, d=2, s=4)
        dn = mean[:, 0:16].rearrange("p (j n) -> p j n", j=2)
        NH = 8
        with Stage(nc, "mlstm", ["chain", "kq", "mrow", "e_done", "s_done", "num", "h_done"]) as (
                block, (chain, kq, mrow, e_done, s_done, num, h_done)):
            def base(h):
                return 64 * (h % 2)

            def scores_of(h):
                return PS[:, 2 * (h % 2):2 * (h % 2) + 2, :].rearrange("p b (s t) -> p (b s) t", s=2)

            @block.tensor
            def _(pe):
                for i in range(NH + 1):
                    if i < NH:
                        h = i
                        b0 = base(h)
                        if h >= 2:
                            pe.wait_ge(s_done, 6 * (h - 1))
                        for s in range(4):
                            ins = pe.matmul(scores_of(h)[:, s, :], km[b0:b0 + 64, h // 2, s * P:(s + 1) * P],
                                            qm[b0:b0 + 64, h // 2, :], start=True, stop=True)
                        ins.then_inc(kq, 1)
                        if h >= 1:
                            pe.wait_ge(e_done, 10 * h)
                        for d in range(2):
                            lhs = ident[0:8, h:h + 1].broadcast_to([8, P])
                            pe.matmul(PS[:, 4 + d, 0:T], lhs, gN[0:8, d, 0, :], start=True, stop=True)
                            pe.matmul(PS[:, 4 + d, T:2 * T], lhs, gN[0:8, d, 0, :], start=True, stop=False)
                            ins = pe.matmul(PS[:, 4 + d, T:2 * T], ident, const("bmask" if d else "fmask"), start=False, stop=True)
                            ins.then_inc(mrow, 1)
                    if i >= 1:
                        h = i - 1
                        pe.wait_ge(s_done, 6 * (h + 1))
                        if h >= 1:
                            pe.wait_ge(h_done, h)
                        for d in range(2):
                            for t in range(2):
                                keys = [0, 1] + ([2] if (d, t) == (0, 0) else [3] if (d, t) == (1, 1) else [2, 3])
                                o = PS[:, 6 + d, t * 65:(t + 1) * 65]
                                for z, s in enumerate(keys):
                                    ins = pe.matmul(o, EE[:, h % 2, d, s, t * P:(t + 1) * P], vm[:, s, h, :],
                                                    start=(z == 0), stop=(z == len(keys) - 1))
                        ins.then_inc(num, 1)

            def regions(d):
                return [(2, 0, P, 1), (2, P, P, 0), (3, P, P, 1)] if d == 0 else [(3, 0, P, 0), (3, P, P, 1), (2, 0, P, 1)]

            @block.scalar
            def _(act):
                for h in range(NH):
                    if h >= 2:
                        act.wait_ge(num, h - 1)
                    for d in range(2):
                        act.wait_ge(mrow, 2 * h + d + 1)
                        for s in range(2):
                            nc.scalar.activation(EE[:, h % 2, d, s, :], PS[:, 4 + d, 0:T], ACT.Exp,
                                                 bias=tA[:, d, s, h:h + 1]).then_inc(e_done, 1)
                        for s, q0, nq, masked in regions(d):
                            nc.scalar.activation(EE[:, h % 2, d, s, q0:q0 + nq], PS[:, 4 + d, masked * T + q0:masked * T + q0 + nq],
                                                 ACT.Exp, bias=tA[:, d, s, h:h + 1]).then_inc(e_done, 1)

            @block.vector
            def _(dve):
                link = Chain(dve, chain)
                for i in range(NH + 1):
                    if i < NH:
                        h = i
                        dve.wait_ge(kq, h + 1)
                        for d in range(2):
                            dve.wait_ge(e_done, 10 * h + 5 * d + 5)
                            sc = scores_of(h)
                            full, half, q0 = (2, 3, P) if d == 0 else (3, 2, 0)
                            e_ = EE[:, h % 2, d]
                            dve.tensor_tensor(e_[:, 0:2, :], e_[:, 0:2, :], sc[:, 0:2, :], ALU.mult).then_inc(s_done, 1)
                            dve.tensor_tensor(e_[:, full, :], e_[:, full, :], sc[:, full, :], ALU.mult).then_inc(s_done, 1)
                            dve.tensor_tensor(e_[:, half, q0:q0 + P], e_[:, half, q0:q0 + P], sc[:, half, q0:q0 + P],
                                              ALU.mult).then_inc(s_done, 1)
                    if i >= 1:
                        h = i - 1
                        dve.wait_ge(num, h + 1)
                        nm = PS[:, 6:8, 0:130].rearrange("p d (t n) -> p d t n", t=2)
                        den = nm[:, :, :, 64]
                        r = dn[:, h % 2, 0:4].rearrange("p (d t) -> p d t", d=2)
                        r2 = dn[:, h % 2, 4:8].rearrange("p (d t) -> p d t", d=2)
                        link(dve.tensor_scalar(r2, den, -1.0, None, ALU.mult))
                        link(dve.tensor_tensor(r, den, r2, ALU.max))
                        link(dve.tensor_tensor(r, r, tM[:, :, :, h], ALU.max))
                        link(dve.reciprocal(r2, r))
                        for t in range(2):
                            link(dve.tensor_scalar(Hm[:, t, h, :], nm[:, 0, t, 0:64], r2[:, 0, t:t + 1], None, ALU.mult))
                        for t in range(2):
                            ins = dve.scalar_tensor_tensor(out=Hm[:, t, h, :], in0=nm[:, 1, t, 0:64], scalar=r2[:, 1, t:t + 1],
                                                           in1=Hm[:, t, h, :], op0=ALU.mult, op1=ALU.add)
                            if t == 0:
                                link(ins)
                        ins.then_inc(h_done, 1)

        def turn_heads(name, src_of, dst_of, n_tiles):
            with Stage(nc, name, ["turned", "copied"]) as (block, (turned, copied)):
                @block.tensor
                def _(pe):
                    for m in range(n_tiles):
                        if m >= 4:
                            pe.wait_ge(copied, m - 3)
                        for t in range(2):
                            ins = pe.transpose(PS[:, m % 4, t * P:(t + 1) * P], src_of(m, t), ident)
                        ins.then_inc(turned, 1)

                @block.vector
                def _(dve):
                    for m in range(n_tiles):
                        dve.wait_ge(turned, m + 1)
                        dst_of(dve, m, PS[:, m % 4, 0:T]).then_inc(copied, 1)
                    dve.wait_ge(copied, n_tiles)
                    dve.nop()

        def head_norm_steps(H, n_heads, dim, sq, st, factor=1.0):
            G = 2 * n_heads
            Hf = H.rearrange("p t h d -> p (t h) d")
            sqf = sq.rearrange("p (g d) -> p g d", g=G)
            return [("act", lambda e: nc.scalar.activation(sqf, Hf, ACT.Square)),
                    ("dve", lambda e: e.reduce_sum(st[:, 0:G], sqf, AX)),
                    ("dve", lambda e: e.tensor_scalar(st[:, 0:G], st[:, 0:G], 1.0 / dim, EPS, ALU.mult, ALU.add)),
                    ("act", lambda e: nc.scalar.activation(st[:, G:2 * G], st[:, 0:G], ACT.Sqrt)),
                    ("dve", lambda e: e.reciprocal(st[:, 0:G], st[:, G:2 * G])),
                    ("dve", lambda e: e.tensor_scalar(st[:, 0:G], st[:, 0:G], factor, None, ALU.mult)),
                    ("dve", lambda e: e.tensor_tensor(Hf, Hf, st[:, 0:G].unsqueeze(2).broadcast_to([P, G, dim]), ALU.mult))]

        st0 = rstd[:, 0:32]
        pointwise("mnorm", head_norm_steps(Hm, 8, 64, area(0, 1024), st0)
                  + sigmoid_steps(om, area(1024, 1024).rearrange("p (k t) -> p k t", k=4)))
        sig_o = area(1024, 1024).rearrange("p (k t) -> p k t", k=4)
        turn_heads("mturn", lambda m, t: Hm[:, t, 2 * m:2 * m + 2, :].rearrange("p h d -> p (h d)"),
                   lambda dve, m, ps: dve.scalar_tensor_tensor(out=mixT[:, m, :], in0=ps, scalar=sm("mnorm", m, 1),
                                                               in1=sig_o[:, m, :], op0=ALU.mult, op1=ALU.mult), 4)

        rope("rope0", [(dq[:, m, :], "rot_ax", "cos_ax", "sin_ax") for m in range(4)]
             + [(dk[:, m, C:], "rot_ax", "cos_ax", "sin_ax") for m in range(4)], 0)
        Hd = area(SCR, 1024).rearrange("p (t h d) -> p t h d", t=2, h=4)
        jobs = []
        for h in range(4):
            for t in range(2):
                brs = [dict(bank=b, off=0, n=512, q=dq[64 * b:64 * b + 64, h, t * P:(t + 1) * P],
                            k=dk[64 * b:64 * b + 64, h, :], bias=None, coef=lam[:, 5:6] if b else None, minus=bool(b),
                            v=[dv[:, s, h * P:(h + 1) * P] for s in range(4)]) for b in range(2)]
                jobs.append(dict(branches=brs, token_major=True, out=Hd[:, t, h, :]))
        attention("diff", jobs, 0.125, 0)
        pointwise("dnorm", head_norm_steps(Hd, 4, 128, area(0, 1024), st0, 1.0 - LAM_INIT))
        turn_heads("dturn", lambda m, t: Hd[:, t, m, :],
                   lambda dve, m, ps: dve.tensor_scalar(mixT[:, 4 + m, :], ps, sm("dnorm", m, 1), None, ALU.mult), 4)

        def out_proj(name, src, dst, bias=None):
            project(name, OUT_CH, [tile_task(m // 2, m % 2, src, "act",
                                             copy_to(dst[:, m, :]) if bias is None else copy_bias(dst[:, m, :], bias[:, m:m + 1]))
                                   for m in range(KT)])

        big = area(4096, KT * T).rearrange("p (k t) -> p k t", k=KT)
        out_proj("out0", mixT, big)
        residual("res0", big, sm("post0"), mpart(2))
        modulated("norm_f0", XT, UX, sm("fpre0"), mpart(3), mpart(4))
        ffn("ffn0", UX)
        residual("res_f0", YT, sm("fpost0"), mpart(5))

        modulation("mod1", MOD_CH, cs[:, 0:8], sm("mod_b1"), mod)
        modulated("norm_c1", XT, UX, sm("pre1"), mpart(0), mpart(1))
        W = 31
        PADL = (W - 1) // 2
        TW = T + W - 1
        glu_a = area(0, 2048).rearrange("p (k t) -> p k t", k=KT)
        glu_g = area(2048, 2048).rearrange("p (k t) -> p k t", k=KT)
        hp = area(4096, KT * TW).rearrange("p (k t) -> p k t", k=KT)
        tasks = [tile_task(m // 2, m % 2, UX, "act", copy_bias((glu_a if m < 8 else glu_g)[:, m % 8, :], sm("pw1_b", m, 1)))
                 for m in range(16)]
        project("pw1", PW1_CH, tasks)
        pointwise("glu", sigmoid_steps(glu_g, glu_g) + [
            ("dve", lambda e: e.memset(hp, 0.0)),
            ("dve", lambda e: e.tensor_tensor(hp[:, :, PADL:PADL + T], glu_a, glu_g, ALU.mult))])
        dw = sm("dw_w").rearrange("p (k w) -> p k w", k=KT)
        with Stage(nc, "dwconv", ["tap"]) as (block, (tap,)):
            @block.vector
            def _(dve):
                n = 0
                for k in range(KT):
                    for w in range(W):
                        if w == 0:
                            ins = dve.tensor_scalar(YT[:, k, :], hp[:, k, 0:T], dw[:, k, 0:1], sm("dw_b", k, 1), ALU.mult, ALU.add)
                        else:
                            dve.wait_ge(tap, n)
                            ins = dve.scalar_tensor_tensor(out=YT[:, k, :], in0=hp[:, k, w:w + T], scalar=dw[:, k, w:w + 1],
                                                           in1=YT[:, k, :], op0=ALU.mult, op1=ALU.add)
                        ins.then_inc(tap, 1)
                        n += 1

        def ln_apply(g, b, src, dst):
            def apply(dve, link):
                link(dve.tensor_tensor(src, src, bc(rstd[:, :], KT), ALU.mult))
                for k in range(KT):
                    link(dve.tensor_scalar(dst[:, k, :], src[:, k, :], g[:, k:k + 1], b[:, k:k + 1], ALU.mult, ALU.add))
            return apply
        norm("ln1", YT, ln_apply(sm("ln_g"), sm("ln_b"), YT, YT), center=True)
        pointwise("silu1", silu_steps(YT, area(4096, 2048).rearrange("p (k t) -> p k t", k=KT)))
        out_proj("pw2", YT, big, sm("pw2_b"))
        residual("res1", big, sm("post1"), mpart(2))
        modulated("norm_m1", XT, UX, sm("fpre1"), mpart(3), mpart(4))

        H = area(0, FT * T).rearrange("p (k t) -> p k t", k=FT)
        EX = area(FT * T, 2 * T).rearrange("p (b t) -> p b t", b=2)
        UTM = area(6144, 2048).rearrange("p (t n) -> p t n", t=2)
        YTM = area(8192, 2048).rearrange("p (t n) -> p t n", t=2)
        UCT = area(10240, KT * CAP).rearrange("p (k c) -> p k c", k=KT)
        S1 = area(11008, 2 * CAP).rearrange("p (t c) -> p t c", t=2)
        SG = area(11200, 2 * CAP).rearrange("p (t c) -> p t c", t=2)
        PL = area(11392, T)
        YC = area(11648, D)
        rt = area(12672, 208)
        ro = sm("router").rearrange("p (k e) -> p k e", k=KT)

        def rv(i, n=16):
            return rt[:, i:i + n]
        steps = []
        for t in range(2):
            for kt in range(KT):
                steps.append(("pe", lambda e, t=t, kt=kt: e.matmul(PS[:, 0, 8 * t:8 * t + 8], UX[:, kt, t * P:(t + 1) * P], ro[:, kt, :],
                                                                   start=(kt == 0), stop=(kt == KT - 1))))
        L = rv(0).rearrange("p (t e) -> p t e", t=2)
        EQ = rv(16).rearrange("p (t e) -> p t e", t=2)
        CU = rv(32).rearrange("p (t e) -> p t e", t=2)
        F1 = rv(48).rearrange("p (t e) -> p t e", t=2)
        F2 = rv(64).rearrange("p (t e) -> p t e", t=2)
        V1, V2, G1, G2 = rv(80, 2), rv(82, 2), rv(84, 2), rv(86, 2)

        def b8(v):
            return v.unsqueeze(2).broadcast_to([P, 2, 8])
        steps.append(("dve", lambda e: e.tensor_copy(rv(0), PS[:, 0, 0:16])))
        for Fx, Vx in ((F1, V1), (F2, V2)):
            steps += [("dve", lambda e, Vx=Vx: e.reduce_max(Vx, L, AX)),
                      ("dve", lambda e, Vx=Vx: e.tensor_tensor(EQ, L, b8(Vx), ALU.is_equal))]
            for t in range(2):
                steps.append(("dve", lambda e, t=t: e.tensor_tensor_scan(CU[:, t, :], ones[:, 0:8], EQ[:, t, :], 0.0, ALU.mult, ALU.add)))
            steps += [("dve", lambda e, Fx=Fx: e.scalar_tensor_tensor(out=Fx, in0=CU, scalar=1.0, in1=EQ, op0=ALU.is_equal, op1=ALU.mult)),
                      ("dve", lambda e, Fx=Fx: e.scalar_tensor_tensor(out=L, in0=Fx, scalar=NEG, in1=L, op0=ALU.mult, op1=ALU.add))]
        steps += [("dve", lambda e: e.tensor_tensor(G2, V2, V1, ALU.subtract)),
                  ("act", lambda e: nc.scalar.activation(G2, G2, ACT.Exp)),
                  ("dve", lambda e: e.tensor_scalar(G1, G2, 1.0, None, ALU.add)),
                  ("dve", lambda e: e.reciprocal(G1, G1)),
                  ("dve", lambda e: e.tensor_tensor(G2, G2, G1, ALU.mult)),
                  ("dve", lambda e: e.tensor_tensor(F1, F1, b8(G1), ALU.mult)),
                  ("dve", lambda e: e.tensor_tensor(F2, F2, b8(G2), ALU.mult)),
                  ("dve", lambda e: e.tensor_tensor(F1, F1, F2, ALU.add)),
                  ("dve", lambda e: e.memset(YT, 0.0))][:-1]
        MK = rt[:, 128:146].rearrange("p (t e) -> p t e", t=2)
        POS = rt[:, 146:164].rearrange("p (t e) -> p t e", t=2)
        GA = rt[:, 164:182].rearrange("p (t e) -> p t e", t=2)
        GC = rt[:, 182:200].rearrange("p (t e) -> p t e", t=2)
        FIT = rt[:, 200:208]
        steps.insert(-6, ("dve", lambda e: e.memset(rt[:, 128:200], 0.0)))
        steps.insert(-6, ("dve", lambda e: e.tensor_tensor(MK[:, :, 0:8], F1, F2, ALU.add)))
        steps.append(("dve", lambda e: e.tensor_copy(GA[:, :, 0:8], F1)))
        ncum_ = const("ncum").rearrange("p (k s) -> p k s", k=2)
        for t in range(2):
            for k in range(2):
                steps.append(("pe", lambda e, t=t, k=k: e.matmul(PS[:, 1, 8 * t:8 * t + 8], ncum_[:, k, t * P:(t + 1) * P],
                                                                 MK[:, k, 0:8], start=(k == 0), stop=(k == 1))))
        for k in range(2):
            steps.append(("pe", lambda e, k=k: e.matmul(PS[:, 2, 0:8], ones, MK[:, k, 0:8], start=(k == 0), stop=(k == 1))))
        steps += [("dve", lambda e: e.tensor_scalar(POS[:, :, 0:8], PS[:, 1, 0:16].rearrange("p (t e) -> p t e", t=2), -1.0, -1.0,
                                                    ALU.mult, ALU.add)),
                  ("dve", lambda e: e.tensor_scalar(full_flag[:, :], PS[:, 2, 0:8], float(CAP), None, ALU.is_gt)),
                  ("dve", lambda e: e.tensor_scalar(FIT, PS[:, 2, 0:8], float(CAP), None, ALU.is_le)),
                  ("dve", lambda e: e.tensor_tensor(GC[:, :, 0:8], GA[:, :, 0:8], FIT.unsqueeze(1).broadcast_to([P, 2, 8]), ALU.mult))]
        pointwise("router", steps)
        with Stage(nc, "uturn", ["turned", "copied"]) as (block, (turned, copied)):
            @block.tensor
            def _(pe):
                for j in range(4):
                    t, half = j // 2, j % 2
                    for k in range(4):
                        ins = pe.transpose(PS[:, j, k * P:(k + 1) * P], UX[:, 4 * half + k, t * P:(t + 1) * P], ident)
                    ins.then_inc(turned, 1)

            @block.scalar
            def _(act):
                for j in range(4):
                    act.wait_ge(turned, j + 1)
                    nc.scalar.activation(UTM[:, j // 2, (j % 2) * 512:(j % 2 + 1) * 512], PS[:, j, :], ACT.Copy)

            @block.vector
            def _(dve):
                dve.memset(YTM, 0.0)
        ws.clear()
        moe_base = MOD_CH + IN0_CH + OUT_CH + FFN_CH + MOD_CH + PW1_CH + OUT_CH
        W13 = FT
        USES = FFN_CH // RING

        with Stage(nc, "experts", ["chain", "built", "chunk_done", "exp_ready", "hidden", "place_turned", "gathered", "act_copied",
                                   "y_copied", "y_ready", "y_added"]) as (
                block, (chain, built, chunk_done, exp_ready, hidden, place_turned, gathered, act_copied, y_copied, y_ready, y_added)):
            @block.sync
            def _(sp):
                for k in range(RING):
                    sp.dma_start(ws.chunk(k), a["stream"][moe_base + k]).then_inc(landed[k], 16)
                with sp.Fori(0, NE - 1) as e:
                    for k in range(FFN_CH):
                        sp.wait_ge(chunk_done, e * FFN_CH + k + 1)
                        sp.dma_start(ws.chunk(k), a["stream"][e * FFN_CH + (moe_base + k + RING)]).then_inc(landed[k % RING], 16)
                for k in range(FFN_CH - RING):
                    g = (NE - 1) * FFN_CH + k
                    sp.wait_ge(chunk_done, g + 1)
                    sp.dma_start(ws.chunk(k), a["stream"][moe_base + g + RING]).then_inc(landed[k % RING], 16)

            def here(eng, e, k):
                eng.wait_ge(landed[k % RING], e * (16 * USES) + 16 * (k // RING + 1))

            @block.tensor
            def _(pe):
                def gather(e):
                    for k in range(KT):
                        for t in range(2):
                            ins = pe.matmul(PS[:, 6 + k // 4, (k % 4) * CAP:(k % 4 + 1) * CAP], UTM[:, t, k * P:(k + 1) * P], S1[:, t, :],
                                            start=(t == 0), stop=(t == 1))
                    ins.then_inc(gathered, 1)

                def hidden_products(e, src, n):
                    for m in range(W13):
                        here(pe, e, m)
                        if m >= 4:
                            pe.wait_ge(hidden, e * FT + m - 3)
                        else:
                            pe.wait_ge(y_added, e * 4)
                        w = ws.chunk(m).rearrange("p (n k c) -> p n k c", n=2, k=KT)
                        for h in range(2):
                            for kt in range(KT):
                                ins = pe.matmul(PS[:, m % 4, h * T:h * T + n], w[:, h, kt, :], src[:, kt, 0:n],
                                                start=(kt == 0), stop=(kt == KT - 1))
                        ins.then_inc(chunk_done, 1)

                pe.wait_ge(built, 2)
                gather(0)
                with pe.Fori(0, NE) as e:
                    full = pe.value_load(full_flag[0:1, bass.ds(e, 1)], min_val=0, max_val=1)
                    pe.wait_ge(act_copied, e * 3 + 2)
                    with pe.If(full < 1):
                        hidden_products(e, UCT, CAP)
                    with pe.Else():
                        hidden_products(e, UX, T)
                    pe.wait_ge(built, e * 4 + 6)
                    pe.wait_ge(hidden, e * FT + FT - 3)
                    for t in range(2):
                        ins = pe.transpose(PS[0:CAP, 2, t * P:(t + 1) * P], SG[:, t, :], ident)
                    ins.then_inc(place_turned, 1)
                    gather(e)
                    pe.wait_ge(act_copied, e * 3 + 5)
                    pe.wait_ge(hidden, e * FT + FT)
                    with pe.If(full < 1):
                        for q in range(FFN_CH - W13):
                            here(pe, e, W13 + q)
                            for m in range(2):
                                for half in range(2):
                                    ins = pe.matmul(PS[0:CAP, 4 + half, :], H[:, 2 * q + m, 0:CAP],
                                                    ws.chunk(W13 + q)[:, m * D + half * 512:m * D + (half + 1) * 512],
                                                    start=(q + m == 0), stop=(2 * q + m == FT - 1))
                            ins.then_inc(chunk_done, 1)
                        pe.wait_ge(y_copied, e * 2 + 2)
                        for j in range(4):
                            pe.matmul(PS[:, j, :], PL[0:CAP, (j // 2) * P:(j // 2 + 1) * P], YC[0:CAP, (j % 2) * 512:(j % 2 + 1) * 512],
                                      start=True, stop=True).then_inc(y_ready, 1)
                    with pe.Else():
                        for q in range(FFN_CH - W13):
                            here(pe, e, W13 + q)
                            for m in range(2):
                                for j in range(4):
                                    ins = pe.matmul(PS[:, 4 + j, :], H[:, 2 * q + m, (j // 2) * P:(j // 2 + 1) * P],
                                                    ws.chunk(W13 + q)[:, m * D + (j % 2) * 512:m * D + (j % 2 + 1) * 512],
                                                    start=(q + m == 0), stop=(2 * q + m == FT - 1))
                            ins.then_inc(chunk_done, 1)
                        for j in range(4):
                            ins = pe.matmul(PS[:, 0, 0:1], ident, ident[:, 0:1], start=True, stop=True)
                            ins.then_inc(y_ready, 1)
                    pe.nop()

            @block.scalar
            def _(act):
                def exps(e, n):
                    act.wait_ge(hidden, e * FT)
                    for m in range(FT):
                        act.wait_ge(chunk_done, e * FFN_CH + m + 1)
                        if m >= 2:
                            act.wait_ge(hidden, e * FT + m - 1)
                        nc.scalar.activation(EX[:, m % 2, 0:n], PS[:, m % 4, 0:n], ACT.Exp, scale=-1.0).then_inc(exp_ready, 1)

                def copy_gathered():
                    for b in range(2):
                        nc.scalar.activation(UCT[:, 4 * b:4 * b + 4, :], PS[:, 6 + b, 0:4 * CAP].rearrange("p (k c) -> p k c", k=4),
                                             ACT.Copy).then_inc(act_copied, 1)
                act.wait_ge(gathered, 1)
                copy_gathered()
                with act.Fori(0, NE) as e:
                    full = act.value_load(full_flag[0:1, bass.ds(e, 1)], min_val=0, max_val=1)
                    with act.If(full < 1):
                        exps(e, CAP)
                    with act.Else():
                        exps(e, T)
                    act.wait_ge(place_turned, e + 1)
                    nc.scalar.activation(PL[0:CAP, :], PS[0:CAP, 2, 0:T], ACT.Copy).then_inc(act_copied, 1)
                    act.wait_ge(gathered, e + 2)
                    copy_gathered()
                    with act.If(full < 1):
                        act.wait_ge(chunk_done, e * FFN_CH + FFN_CH)
                        for b in range(2):
                            nc.scalar.activation(YC[0:CAP, b * 512:(b + 1) * 512], PS[0:CAP, 4 + b, :], ACT.Copy).then_inc(y_copied, 1)
                    with act.Else():
                        for b in range(2):
                            act.nop().then_inc(y_copied, 1)
                    act.nop()

            @block.vector
            def _(dve):
                def build(e, which):
                    dst, val = (S1, MK) if which == 0 else (SG, GC)
                    for t in range(2):
                        dve.tensor_scalar(dst[:, t, :], const("iota"), POS[:, t, bass.ds(e, 1)], val[:, t, bass.ds(e, 1)],
                                          ALU.is_equal, ALU.mult).then_inc(built, 1)

                def hiddens(e, n):
                    for m in range(FT):
                        x = EX[:, m % 2, 0:n]
                        dve.wait_ge(exp_ready, e * FT + m + 1)
                        dve.tensor_scalar(x, x, 1.0, None, ALU.add).then_inc(chain, 1)
                        dve.wait_ge(chain, e * (3 * FT) + 3 * m + 1)
                        dve.reciprocal(x, x).then_inc(chain, 1)
                        dve.wait_ge(chain, e * (3 * FT) + 3 * m + 2)
                        dve.tensor_tensor(x, PS[:, m % 4, 0:n], x, ALU.mult).then_inc(chain, 1)
                        dve.wait_ge(chain, e * (3 * FT) + 3 * m + 3)
                        dve.tensor_tensor(H[:, m, 0:n], PS[:, m % 4, T:T + n], x, ALU.mult).then_inc(hidden, 1)

                build(0, 0)
                with dve.Fori(0, NE) as e:
                    full = dve.value_load(full_flag[0:1, bass.ds(e, 1)], min_val=0, max_val=1)
                    dve.wait_ge(gathered, e + 1)
                    build(e + 1, 0)
                    dve.wait_ge(place_turned, e)
                    build(e, 1)
                    with dve.If(full < 1):
                        hiddens(e, CAP)
                    with dve.Else():
                        hiddens(e, T)
                    with dve.If(full < 1):
                        for j in range(4):
                            dve.wait_ge(y_ready, e * 4 + j + 1)
                            y = YTM[:, j // 2, (j % 2) * 512:(j % 2 + 1) * 512]
                            dve.tensor_tensor(y, y, PS[:, j, :], ALU.add).then_inc(y_added, 1)
                    with dve.Else():
                        for j in range(4):
                            dve.wait_ge(y_ready, e * 4 + 4)
                            y = YTM[:, j // 2, (j % 2) * 512:(j % 2 + 1) * 512]
                            dve.scalar_tensor_tensor(out=y, in0=PS[:, 4 + j, :], scalar=GA[:, j // 2, bass.ds(e, 1)], in1=y,
                                                     op0=ALU.mult, op1=ALU.add).then_inc(y_added, 1)
                    dve.nop()
        ws.clear()
        turn_heads("yturn", lambda m, t: YTM[:, t, m * P:(m + 1) * P], lambda dve, m, ps: dve.tensor_copy(YT[:, m, :], ps), KT)
        residual("res_m1", YT, sm("fpost1"), mpart(5))

        q_dsa = area(0, 512).rearrange("p (k t) -> p k t", k=2)
        k_dsa = area(512, 256)
        q_idx = area(768, 512).rearrange("p (k t) -> p k t", k=2)
        k_idx = area(1280, 256)
        q_fox = area(1536, 768).rearrange("p (k t) -> p k t", k=3)
        k_fox = area(2304, 768).rearrange("p (k t) -> p k t", k=3)
        q_nsa = area(3072, 768).rearrange("p (k t) -> p k t", k=3)
        qr_nsa = area(3840, 768).rearrange("p (k t) -> p k t", k=3)
        kc_in = area(4608, 256)
        vc_in = area(4864, 256)
        k_slc = area(5120, 256)
        k_win = area(5376, 256)
        sgate = area(5632, 2048).rearrange("p (k t) -> p k t", k=KT)
        tokm = area(7680, 2 * 768).rearrange("p (t n) -> p t n", t=2)
        V_FOX, V_SLC, V_WIN, V_DSA, I_W, N_G, F_F = 0, 384, 512, 640, 704, 712, 730
        kcT = area(9216, 16)
        vcn = area(9232, 128)
        foxb = area(9360, 6 * 384).rearrange("p (h n) -> p h n", h=6)
        dsab = area(11664, 384)
        SCR2 = 12048
        with nc.Fori(0, LAYERS) as ly:
            with Stage(nc, "lload", ["loaded"]) as (block, (loaded,)):
                @block.sync
                def _(sp):
                    sp.dma_start(layer_small[:, :], a["layer_small"][ly]).then_inc(loaded, 16)
                    sp.wait_ge(loaded, 16)
                    sp.nop()
            ws.begin(moe_base + NE * FFN_CH + ly * L2_CH, L2_CH)
            modulation("ada", ADA_CH, sm("c2"), lsm("b_ada"), mod)

            def u_apply():
                st = [("dve", lambda e: e.tensor_scalar(coef[:, 0:8], mod[:, 8:16], 1.0, None, ALU.add)),
                      ("dve", lambda e: e.tensor_scalar(coef[:, 8:16], mod[:, 16:24], 1.0, None, ALU.add))]
                for k in range(KT):
                    st.append(("dve", lambda e, k=k: e.tensor_scalar(UX[:, k, :], XT[:, k, :], coef[:, k:k + 1], mod[:, k:k + 1],
                                                                     ALU.mult, ALU.add)))
                return st
            pointwise("u2", u_apply())

            tiles = [q_dsa[:, 0, :], q_dsa[:, 1, :], k_dsa, q_idx[:, 0, :], q_idx[:, 1, :], k_idx,
                     q_fox[:, 0, :], q_fox[:, 1, :], q_fox[:, 2, :], k_fox[:, 0, :], k_fox[:, 1, :], k_fox[:, 2, :],
                     q_nsa[:, 0, :], q_nsa[:, 1, :], q_nsa[:, 2, :], kc_in, vc_in, k_slc, k_win] + \
                    [sgate[:, m, :] for m in range(KT)]
            tasks = [tile_task(m // 2, m % 2, UX, "act", copy_to(dst)) for m, dst in enumerate(tiles)]
            W2 = area(SCR2, 256)

            def keep_w2(bank, chunk):
                return [(bank[:, 0:256], ident, chunk[:, 8 * P:10 * P], True, True)]
            tasks.append((13, keep_w2, "act", copy_to(W2)))
            for c_ in range(3):
                for t in range(2):
                    tasks.append(token_task(14 + c_, UX, t * P, "act", copy_to(tokm[:, t, 256 * c_:256 * (c_ + 1)])))
            project("in2", IN2_CH, tasks)

            kb = area(SCR2 + 256, 2 * 480).rearrange("p (z l c) -> p z l c", z=2, l=32)
            hc = area(SCR2 + 1216, 32)
            hs = area(SCR2 + 1248, 32)
            fr = ws.used
            with Stage(nc, "compress", ["built", "wchunk", "summed", "chain", "turn", "done"]) as (
                    block, (built, wchunk, summed, chain, turn, done)):
                @block.sync
                def _(sp):
                    ws.load(sp, fr, CMP_CH, [(wchunk, k + 1) for k in range(CMP_CH)])

                @block.vector
                def _(dve):
                    link = Chain(dve, chain)
                    for z, (src, pe_) in enumerate(((kc_in, "pe_k"), (vc_in, "pe_v"))):
                        for c_ in range(NC):
                            ins = dve.tensor_tensor(kb[:, z, :, c_], src[:, 16 * c_:16 * c_ + 32], lsm(pe_), ALU.add)
                            ins.then_inc(built, 1)
                    dve.wait_ge(turn, 1)
                    link(dve.tensor_scalar(hs[:, 0:2 * NC], hs[:, 0:2 * NC], 1.0, None, ALU.add))
                    link(dve.reciprocal(hs[:, 0:2 * NC], hs[:, 0:2 * NC]))
                    dve.tensor_tensor(hc[:, 0:2 * NC], hs[:, 0:2 * NC], PS[:, 0, 0:2 * NC], ALU.mult).then_inc(done, 1)

                @block.scalar
                def _(act):
                    act.wait_ge(summed, 1)
                    nc.scalar.activation(hs[:, 0:2 * NC], PS[:, 0, 0:2 * NC], ACT.Exp, scale=-1.0).then_inc(turn, 1)
                    act.wait_ge(summed, 2)
                    nc.scalar.activation(kcT[:, 0:NC], PS[:, 1, 0:NC], ACT.Copy)
                    nc.scalar.activation(vcn[0:NC, :], PS[0:NC, 2, 0:P], ACT.Copy)

                @block.tensor
                def _(pe):
                    for z in range(2):
                        pe.wait_ge(built, NC * (z + 1))
                        for l in range(32):
                            k = 2 * z + l // 16
                            if l % 16 == 0:
                                ws.wait(pe, fr + k)
                            ins = pe.matmul(PS[:, 0, NC * z:NC * (z + 1)], ws.chunk(fr + k)[:, (l % 16) * P:(l % 16 + 1) * P],
                                            kb[:, z, l, :], start=(l == 0), stop=(l == 31))
                            if l % 16 == 15:
                                ins.then_inc(wchunk, 1)
                    ins = pe.transpose(PS[:, 3, 0:P], ident, ident)
                    ins.then_inc(summed, 1)
                    pe.wait_ge(done, 1)
                    pe.matmul(PS[:, 1, 0:NC], W2[:, 0:P], hc[:, 0:NC], start=True, stop=True)
                    pe.matmul(PS[0:NC, 2, 0:P], hc[:, NC:2 * NC], W2[:, P:2 * P], start=True, stop=True).then_inc(summed, 1)

            steps = [("dve", lambda e: e.tensor_copy(qr_nsa, q_nsa)),
                     ("dve", lambda e: e.tensor_scalar(tokm[:, :, I_W:I_W + 8], tokm[:, :, I_W:I_W + 8], 8.0 ** -0.5, None, ALU.mult))]
            ng = tokm[:, :, N_G:N_G + 18]
            steps += sigmoid_steps(ng, ng)
            ffg = tokm[:, :, F_F:F_F + 6]
            fb = lsm("b_f").unsqueeze(1).broadcast_to([P, 2, 6])
            s12 = area(SCR2, 12).rearrange("p (t n) -> p t n", t=2)
            s12b = area(SCR2 + 12, 12).rearrange("p (t n) -> p t n", t=2)
            steps.append(("dve", lambda e: e.tensor_tensor(ffg, ffg, fb, ALU.add)))
            steps += log_sigmoid_steps(ffg, s12, s12b)
            ncum = const("ncum").rearrange("p (k s) -> p k s", k=2)
            for h in range(6):
                for t in range(2):
                    steps.append(("pe", lambda e, h=h, t=t: e.matmul(PS[:, h, 0:T], ffg[:, t, h:h + 1].broadcast_to([P, P]), ncum[:, t, :],
                                                                     start=(t == 0), stop=(t == 1))))
                steps.append(("dve", lambda e, h=h: e.tensor_tensor(foxb[:, h, 0:P], PS[:, h, 0:P], const("cmask")[:, 0:P], ALU.add)))
                steps.append(("dve", lambda e, h=h: e.tensor_tensor(foxb[:, h, P:3 * P], PS[:, h, 0:T], const("cmask")[:, P:3 * P], ALU.add)))
            steps += silu_steps(sgate, UX)
            pointwise("gates2", steps)
            rope("rope2", [(q_dsa[:, 0, :], "rot64", "cos64", "sin64"), (q_dsa[:, 1, :], "rot64", "cos64", "sin64"),
                           (k_dsa, "rot64", "cos64", "sin64"), (k_slc, "rot64", "cos64", "sin64"), (k_win, "rot64", "cos64", "sin64"),
                           (q_idx[:, 0, :], "rot32", "cos32", "sin32"), (q_idx[:, 1, :], "rot32", "cos32", "sin32"),
                           (k_idx, "rot32", "cos32", "sin32")]
                 + [(qr_nsa[:, m, :], "rot64", "cos64", "sin64") for m in range(3)], SCR2)

            isc = area(SCR2, 384)
            wk = area(SCR2 + 384, 2 * 256).rearrange("p (j n) -> p j n", j=2)
            m8 = area(SCR2 + 896, 8)
            rel = area(SCR2 + 1024, 4 * 256).rearrange("p (j n) -> p j n", j=4)
            SEL = -3.0e38
            LOW = -2.0e38
            with Stage(nc, "index", ["chain", "raw", "relu", "summed", "masked", "selected"]) as (
                    block, (chain, raw, relu, summed, masked, selected)):
                rows = [(0, 0, P), (1, P, 2 * P)]

                @block.tensor
                def _(pe):
                    j = 0
                    for t, at_, n_ in rows:
                        for h in range(8):
                            if j >= 4:
                                pe.wait_ge(relu, j - 3)
                            b0 = 32 * (h % 4)
                            pe.matmul(PS[:, j % 4, 0:n_], q_idx[b0:b0 + 32, h // 4, t * P:(t + 1) * P], k_idx[b0:b0 + 32, 0:n_],
                                      start=True, stop=True).then_inc(raw, 1)
                            j += 1

                @block.scalar
                def _(act):
                    j = 0
                    for t, at_, n_ in rows:
                        for h in range(8):
                            act.wait_ge(raw, j + 1)
                            if j >= 4:
                                act.wait_ge(summed, j - 3)
                            nc.scalar.activation(rel[:, j % 4, 0:n_], PS[:, j % 4, 0:n_], ACT.Relu).then_inc(relu, 1)
                            j += 1

                @block.vector
                def _(dve):
                    link = Chain(dve, chain)
                    j = 0
                    for t, at_, n_ in rows:
                        for h in range(8):
                            dve.wait_ge(relu, j + 1)
                            w = tokm[:, t, I_W + h:I_W + h + 1]
                            o = isc[:, at_:at_ + n_]
                            if h == 0:
                                ins = dve.tensor_scalar(o, rel[:, j % 4, 0:n_], w, None, ALU.mult)
                            else:
                                ins = dve.scalar_tensor_tensor(out=o, in0=rel[:, j % 4, 0:n_], scalar=w, in1=o, op0=ALU.mult, op1=ALU.add)
                            ins.then_inc(summed, 1)
                            j += 1
                            dve.wait_ge(summed, j)
                    for t, at_, n_ in rows:
                        dve.wait_ge(masked, t + 1)
                        cur = isc[:, at_:at_ + n_]
                        for r in range(TOPK // 8):
                            nxt = wk[:, r % 2, 0:n_]
                            link(dve.max(m8, cur))
                            link(dve.match_replace(nxt, m8, cur, SEL))
                            cur = nxt
                        link(dve.tensor_scalar(cur, cur, SEL, NEG, ALU.not_equal, ALU.mult))
                        dve.tensor_tensor(dsab[:, at_:at_ + n_], cur, const("cmask")[:, at_:at_ + n_], ALU.add).then_inc(selected, 1)
                        dve.wait_ge(selected, t + 1)
                    dve.nop()

                @block.gpsimd
                def _(pool):
                    for t, at_, n_ in rows:
                        pool.wait_ge(summed, 8 * (t + 1))
                        nc.gpsimd.affine_select(out=isc[:, at_:at_ + n_], in_=isc[:, at_:at_ + n_], compare_op=ALU.is_ge, fill=LOW,
                                                base=t * P, pattern=[[-1, n_]], channel_multiplier=1).then_inc(masked, 1)

            jobs = []

            def mask_of(t):
                return const("cmask")[:, 0:P] if t == 0 else const("cmask")[:, P:3 * P]

            def nk(t):
                return P * (t + 1)

            def vals(c0, t):
                return [tokm[:, s, c0:c0 + 64] for s in range(t + 1)]
            for h in range(4):
                b0 = 64 * (h % 2)
                for t in range(2):
                    jobs.append(dict(base=b0, out=YT[b0:b0 + 64, h // 2, t * P:(t + 1) * P], branches=[dict(
                        bank=0, off=0, n=nk(t), q=q_dsa[b0:b0 + 64, h // 2, t * P:(t + 1) * P], k=k_dsa[b0:b0 + 64, 0:nk(t)],
                        bias=dsab[:, 0:P] if t == 0 else dsab[:, P:3 * P], coef=None, v=vals(V_DSA, t))]))
            for h in range(6):
                b0 = 64 * (h % 2)
                for t in range(2):
                    jobs.append(dict(base=b0, out=YT[b0:b0 + 64, 2 + h // 2, t * P:(t + 1) * P], branches=[dict(
                        bank=0, off=0, n=nk(t), q=q_fox[b0:b0 + 64, h // 2, t * P:(t + 1) * P], k=k_fox[b0:b0 + 64, h // 2, 0:nk(t)],
                        bias=foxb[:, h, 0:P] if t == 0 else foxb[:, h, P:3 * P], coef=None, v=vals(V_FOX + 64 * h, t))]))
            for h in range(6):
                g, j_ = h // 3, h % 3
                bq, bo = 64 * g, 64 * (h % 2)
                for t in range(2):
                    def gate(z):
                        return tokm[:, t, N_G + 6 * z + h:N_G + 6 * z + h + 1]
                    q_, qr_ = (x[bq:bq + 64, j_, t * P:(t + 1) * P] for x in (q_nsa, qr_nsa))
                    brs = [dict(bank=0, off=0, n=nk(t), q=qr_, k=k_slc[bq:bq + 64, 0:nk(t)], bias=mask_of(t), coef=gate(1),
                                v=vals(V_SLC + 64 * g, t)),
                           dict(bank=0, off=256, n=nk(t), q=qr_, k=k_win[bq:bq + 64, 0:nk(t)], bias=mask_of(t), coef=gate(2),
                                v=vals(V_WIN + 64 * g, t)),
                           dict(bank=1, off=0, n=NC, q=q_, k=kcT[bq:bq + 64, 0:NC], bias=const("cmpmask")[:, 16 * t:16 * t + NC],
                                coef=gate(0), v=[vcn[0:NC, 64 * g:64 * g + 64]])]
                    jobs.append(dict(base=bo, out=YT[bo:bo + 64, 5 + h // 2, t * P:(t + 1) * P], branches=brs))
            attention("attn2", jobs, 0.125, SCR2)
            pointwise("gate_mix", [("dve", lambda e: e.tensor_tensor(YT, YT, sgate, ALU.mult))])
            out2 = area(0, KT * T).rearrange("p (k t) -> p k t", k=KT)
            rs = area(2048, KT * T).rearrange("p (k t) -> p k t", k=KT)
            out_proj("out2", YT, rs)
            steps = []
            for k in range(KT):
                steps.append(("dve", lambda e, k=k: e.tensor_scalar(rs[:, k, :], rs[:, k, :], coef[:, 8 + k:9 + k], None, ALU.mult)))
            steps.append(("dve", lambda e: e.scalar_tensor_tensor(out=rs, in0=XT, scalar=ALPHA, in1=rs, op0=ALU.mult, op1=ALU.add)))
            pointwise("resid2", steps)
            norm("ln2", rs, ln_apply(lsm("ln_g2"), lsm("ln_b2"), rs, XT), center=True, eps=LN_EPS)
            ws.clear()

        with Stage(nc, "store", ["stored"]) as (block, (stored,)):
            @block.sync
            def _(sp):
                sp.dma_start(a["out"], XT).then_inc(stored, 16)
                sp.wait_ge(stored, 16)
                sp.nop()



def cols(v):
    v = np.asarray(v)
    return v.reshape(-1, P).T


def blocks(w):
    w = np.asarray(w)
    k, n = w.shape
    return w.reshape(k // P, P, n // P, P).transpose(2, 0, 1, 3)


def to_chunks(b):
    return b.reshape(-1, BLOCKS, P, P).transpose(0, 2, 1, 3).reshape(-1, P, CH)


def chunks(w):
    return to_chunks(blocks(w).reshape(-1, P, P))


def padded(w, n):
    out = np.zeros((w.shape[0], n), w.dtype)
    out[:, :w.shape[1]] = w
    return out


def ffn_chunks(w1, w3, w2):
    pair = np.stack([blocks(w1), blocks(w3)], 1)
    return [to_chunks(pair.reshape(-1, P, P)), chunks(w2)]


def expert_chunks(w1, w3, w2):
    pair = np.stack([blocks(w1), blocks(w3)], 1)
    return [to_chunks(pair.reshape(-1, P, P)), to_chunks(blocks(w2).transpose(1, 0, 2, 3).reshape(-1, P, P))]


def two(w):
    out = np.zeros((P, P), w.dtype)
    out[0:64, 0:64] = w
    out[64:, 64:] = w
    return out


def layer_chunks(w_ada, w_in, cmp_w1, cmp_w2, w_out):
    at, s = 0, {}
    for name, w in (("dsa_q", 256), ("dsa_k", 64), ("dsa_v", 64), ("idx_q", 256), ("idx_k", 32), ("idx_w", 8),
                    ("fox_q", 384), ("fox_k", 384), ("fox_v", 384), ("fox_f", 6), ("nsa_q", 384), ("kc", 128),
                    ("vc", 128), ("ks", 128), ("vs", 128), ("kw", 128), ("vw", 128), ("nsa_g", 18), ("gate", 1024)):
        s[name] = w_in[:, at:at + w]
        at += w
    q = s["nsa_q"].reshape(D, 2, 3, 64).transpose(0, 2, 1, 3).reshape(D, 384)
    feat = np.concatenate([s["dsa_q"], s["dsa_k"], s["dsa_k"], s["idx_q"]] + [s["idx_k"]] * 4 +
                          [s["fox_q"], s["fox_k"], q, s["kc"], s["vc"], s["ks"], s["kw"], s["gate"]], 1)
    tok = padded(np.concatenate([s["fox_v"], s["vs"], s["vw"], s["dsa_v"], s["idx_w"], s["nsa_g"], s["fox_f"]], 1), 768)
    small = np.zeros((8, P, P), w_in.dtype)
    small[0], small[1] = two(cmp_w2[0]), two(cmp_w2[1])
    inp = np.concatenate([blocks(feat).reshape(-1, P, P), small, blocks(tok).reshape(-1, P, P)], 0)
    w1 = np.stack([two(cmp_w1[z].reshape(32, 64, 64)[l]) for z in range(2) for l in range(32)], 0)
    return [chunks(w_ada), to_chunks(inp), to_chunks(w1), chunks(w_out)]


def lay_out(i):
    i = {k: np.asarray(v) for k, v in i.items()}
    f = np.float32
    win = i["l0_w_in"]
    g0 = 4 * 512
    in0 = np.concatenate([win[:, :g0], padded(win[:, g0:g0 + 32], 256), win[:, g0 + 32:]], 1)
    parts = [chunks(i["l0_mod_w"]), chunks(in0), chunks(i["l0_w_out"])]
    parts += ffn_chunks(i["l0_ffn_w1"], i["l0_ffn_w3"], i["l0_ffn_w2"])
    parts += [chunks(i["l1_mod_w"]), chunks(i["l1_conv_pw1_w"]), chunks(i["l1_conv_pw2_w"])]
    for e in range(NE):
        parts += expert_chunks(i["l1_moe_w1"][e], i["l1_moe_w3"][e], i["l1_moe_w2"][e])
    for l in range(LAYERS):
        parts += layer_chunks(i["w_ada_2"][l], i["w_in_2"][l], i["cmp_w1_2"][l], i["cmp_w2_2"][l], i["w_out_2"][l])
    stream = np.concatenate(parts, 0)

    def rows(m):
        out = np.zeros((P, m.shape[1]), m.dtype)
        out[:m.shape[0]] = m
        return out
    sm = {
        "c": cols(i["c"][0]), "c_ctx": cols(i["c_ctx"]), "mod_b0": cols(i["l0_mod_b"]), "pre0": cols(i["l0_mix_pre_g"]),
        "post0": cols(i["l0_mix_post_g"]), "gate_b": rows(i["l0_mlstm_gate_b"].reshape(4, 8).T),
        "conv_w": i["l0_mlstm_conv_w"].reshape(3, 8, P).transpose(2, 1, 0).reshape(P, 24),
        "mnorm": cols(i["l0_mlstm_norm_g"]),
        "lam": rows(np.stack([i["l0_lambda_q1"], i["l0_lambda_q2"], i["l0_lambda_k1"], i["l0_lambda_k2"]], 1)),
        "dnorm": cols(i["l0_diff_norm_g"]), "fpre0": cols(i["l0_ffn_pre_g"]), "fpost0": cols(i["l0_ffn_post_g"]),
        "mod_b1": cols(i["l1_mod_b"]), "pre1": cols(i["l1_mix_pre_g"]), "post1": cols(i["l1_mix_post_g"]),
        "pw1_b": cols(i["l1_conv_pw1_b"]), "dw_w": i["l1_conv_dw_w"].reshape(31, 8, P).transpose(2, 1, 0).reshape(P, 248),
        "dw_b": cols(i["l1_conv_dw_b"]), "ln_g": cols(i["l1_conv_ln_g"]), "ln_b": cols(i["l1_conv_ln_b"]),
        "pw2_b": cols(i["l1_conv_pw2_b"]), "fpre1": cols(i["l1_ffn_pre_g"]), "fpost1": cols(i["l1_ffn_post_g"]),
        "router": i["l1_router_w"].reshape(8, P, 8).transpose(1, 0, 2).reshape(P, 64), "c2": cols(i["c_2"][0]),
    }
    small = np.concatenate([sm[n] for n, _ in SMALL_W], 1).astype(f, copy=False)
    layer = []
    for l in range(LAYERS):
        pe = i["cmp_pe_2"][l]
        lm = {"b_ada": cols(i["b_ada_2"][l]), "pe_k": np.concatenate([pe[0].T] * 2, 0), "pe_v": np.concatenate([pe[1].T] * 2, 0),
              "ln_g2": cols(i["ln_g_2"][l]), "ln_b2": cols(i["ln_b_2"][l]), "b_f": np.stack([i["b_f_2"][l]] * P, 0)}
        layer.append(np.concatenate([lm[n] for n, _ in LAYER_W], 1))
    t = const_table()
    const = np.concatenate([t[n] for n, _ in CONST_W], 1).astype(f)

    def feature_major(x):
        return np.ascontiguousarray(x[0].T.reshape(KT, P, -1).transpose(1, 0, 2))
    return {"stream": stream, "small": np.ascontiguousarray(small), "layer_small": np.ascontiguousarray(np.stack(layer, 0)),
            "consts": const, "xT": feature_major(i["x"]), "ctxT": feature_major(i["ctx"])}


def kernel(**inputs):
    import concourse.bacc as _bacc
    from concourse.bass_utils import run_bass_kernel_spmd as _run

    arrays = lay_out(inputs)
    nc = _bacc.Bacc("TRN2", target_bir_lowering=False, num_devices=1)
    a = {n: nc.dram_tensor(n, v.shape, F32, kind="ExternalInput").ap() for n, v in arrays.items()}
    a["out"] = nc.dram_tensor("out", (P, KT, T), F32, kind="ExternalOutput").ap()
    build(nc, a)
    r = _run(nc, [arrays], core_ids=[0])
    y = r.results[0]["out"]
    return np.ascontiguousarray(y.transpose(1, 0, 2).reshape(D, T).T).reshape(1, T, D)
```

```python
from contextlib import ExitStack
import math

import numpy as np

import concourse.bass as bass
from concourse import mybir

F32 = mybir.dt.float32
ALU = mybir.AluOpType
ACT = mybir.ActivationFunctionType
AX = mybir.AxisListType.X

P = 128
D = 1024
KT = D // P
T = 256
C = 256
TT = T // P
FF = 2816
FT = FF // P
NE = 8
BLOCKS = 16
CH = BLOCKS * P
RING = 9
NEG = -1e30
FLOOR = -1e20
EPS = 1e-6
LN_EPS = 1e-5
ALPHA = (2.0 * 2) ** 0.25
LAM_INIT = 0.8 - 0.6 * math.exp(-0.3 * 0)
NC = 15
TOPK = 64
CAP = 112
LAYERS = 2

MOD_CH = 6 * D // P // 2
MOD_FIRST = 8
IN0_CH = 15
OUT_CH = KT * KT // BLOCKS
FFN_CH = 3 * KT * FT // BLOCKS
PW1_CH = 2 * OUT_CH
ADA_CH = 3 * D // P // 2
EXPERT_SIDE = LAYERS * ADA_CH // NE
EXPERT_CH = FFN_CH + EXPERT_SIDE
IN2_CH = 17
CMP_CH = 4
L2_CH = IN2_CH + CMP_CH + OUT_CH



def const_table():
    i = np.arange(P)
    r, c = i[:, None], i[None, :]
    t = {}
    t["ones"] = np.ones((P, P))
    t["ident"] = (r == c) * 1.0

    def rot(half, period):
        m = np.zeros((P, P))
        for o in range(P):
            k = o % period
            if k < half:
                m[o + half, o] = -1.0
            else:
                m[o - half, o] = 1.0
        return m

    t["rot_ax"] = rot(16, 32)
    t["rot64"] = rot(32, 64)
    t["rot32"] = rot(16, 32)
    tok = np.arange(T, dtype=np.float32)
    row, col = np.floor(tok / 64).astype(np.float32), (tok % 64).astype(np.float32)
    inv_ax = (np.float32(10000.0) ** (-np.arange(0, 32, 2, dtype=np.float32) / 32)).astype(np.float32)
    ang = np.zeros((P, T), np.float32)
    for o in range(P):
        ang[o] = (row if (o % 64) < 32 else col) * inv_ax[o % 16]
    t["cos_ax"], t["sin_ax"] = np.cos(ang), np.sin(ang)
    for name, half in (("64", 32), ("32", 16)):
        inv = (np.float32(10000.0) ** (-np.arange(half, dtype=np.float32) / half)).astype(np.float32)
        ang = inv[i % half][:, None] * tok[None, :]
        t["cos" + name], t["sin" + name] = np.cos(ang), np.sin(ang)
    s = np.arange(T)[None, :]
    t["ncum"] = np.concatenate([-1.0 * (r + P * k <= s) for k in range(TT)], 1)
    cd = np.where(c > r, NEG, 0.0)
    t["cmask"] = np.concatenate([cd, np.zeros((P, P)), cd], 1)
    t["fmask"] = np.concatenate([np.where(c < r, NEG, 0.0)] * 2, 1)
    t["bmask"] = np.concatenate([np.where(c > r, NEG, 0.0)] * 2, 1)
    cend = 16 * np.arange(16)[None, :] + 31
    t["cmpmask"] = np.concatenate([np.where((cend <= r + P * k) & (np.arange(16)[None, :] < NC), 0.0, NEG)
                                   for k in range(TT)], 1)
    t["iota"] = np.broadcast_to(np.arange(CAP)[None, :], (P, CAP))
    return t


def offsets(widths):
    at, out = 0, {}
    for n, w in widths:
        out[n] = (at, w)
        at += w
    return out, at


CONST_W = [("ones", P), ("ident", P), ("rot_ax", P), ("rot64", P), ("rot32", P), ("cos_ax", T), ("sin_ax", T),
           ("cos64", T), ("sin64", T), ("cos32", T), ("sin32", T), ("ncum", TT * T), ("cmask", 3 * P),
           ("fmask", T), ("bmask", T), ("cmpmask", TT * 16), ("iota", CAP)]
CONST_AT, CONST_N = offsets(CONST_W)

SMALL_W = [("c", 8), ("c_ctx", 8), ("mod_b0", 48), ("pre0", 8), ("post0", 8), ("gate_b", 4), ("conv_w", 24),
           ("mnorm", 4), ("lam", 4), ("dnorm", 4), ("fpre0", 8), ("fpost0", 8), ("mod_b1", 48), ("pre1", 8),
           ("post1", 8), ("pw1_b", 16), ("dw_w", 31 * 8), ("dw_b", 8), ("ln_g", 8), ("ln_b", 8), ("pw2_b", 8),
           ("fpre1", 8), ("fpost1", 8), ("router", 64), ("c2", 8)]
SMALL_AT, SMALL_N = offsets(SMALL_W)
LAYER_W = [("b_ada", 24), ("pe_k", 32), ("pe_v", 32), ("ln_g2", 8), ("ln_b2", 8), ("b_f", 6)]
LAYER_AT, LAYER_N = offsets(LAYER_W)



def interleave(n, m):
    main, side, at = [], [], 0
    for k in range(max(n, m)):
        if k < n:
            main.append(at)
            at += 1
        if k < m:
            side.append(at)
            at += 1
    return main, side


EXPERT_AFTER = [5, 11, 17]
EXPERT_MAIN = [k + sum(k > a for a in EXPERT_AFTER) for k in range(FFN_CH)]
EXPERT_SIDES = [a + 1 + z for z, a in enumerate(EXPERT_AFTER)]
assert sorted(EXPERT_MAIN + EXPERT_SIDES) == list(range(EXPERT_CH)) and EXPERT_CH % RING == 0


class Stream:

    def __init__(self, nc, ring, dram, sems):
        self.nc, self.ring, self.dram, self.landed = nc, ring, dram, sems
        self.used = self.issued = 0
        self.total = 0
        self.base = 0

    def begin(self, base, total):
        self.used = self.issued = 0
        self.total, self.base = total, base

    def chunk(self, g):
        return self.ring[:, (g % RING) * CH:(g % RING + 1) * CH]

    def wait(self, eng, g):
        eng.wait_ge(self.landed[g % RING], 16 * (g // RING + 1))

    def load(self, sp, first, n, freed):
        last = min(first + n + RING, self.total)
        for g in range(self.issued, last):
            old = g - RING
            if old >= first and old - first < n:
                sp.wait_ge(*freed[old - first])
            sp.dma_start(self.chunk(g), self.dram[self.base + g]).then_inc(self.landed[g % RING], 16)
        self.issued = max(self.issued, last)
        self.used = first + n

    def clear(self):
        for s in self.landed:
            self.nc.gpsimd.sem_clear(s)
        self.nc.all_engine_barrier()


class Stage:

    def __init__(self, nc, name, sems):
        self.nc, self.name, self.names = nc, name, sems

    def __enter__(self):
        self.stack = ExitStack()
        self.sems = {n: self.stack.enter_context(self.nc.semaphore(f"{self.name}_{n}")) for n in self.names}
        self.inner = ExitStack()
        self.block = self.inner.enter_context(self.nc.Block())
        return self.block, [self.sems[n] for n in self.names]

    def __exit__(self, *a):
        self.inner.close()
        for s in self.sems.values():
            self.nc.gpsimd.sem_clear(s)
        self.nc.all_engine_barrier()
        self.stack.close()


class Chain:

    def __init__(self, eng, sem):
        self.eng, self.sem, self.n = eng, sem, 0

    def __call__(self, ins):
        self.go(ins)
        self.sync()

    def go(self, ins):
        self.n += 1
        ins.then_inc(self.sem, 1)

    def sync(self):
        self.eng.wait_ge(self.sem, self.n)


def build(nc, a):
    ctx = ExitStack()
    with ctx:
        def sb(name, n):
            return ctx.enter_context(nc.sbuf_tensor("sb_" + name, [P, n], F32))

        ring = sb("ring", RING * CH)
        consts = sb("consts", CONST_N)
        small = sb("small", SMALL_N)
        layer_small = sb("layer_small", LAYER_N)
        XT = sb("XT", KT * T)[:, :].rearrange("p (k t) -> p k t", k=KT)
        U2 = sb("U2", KT * 2 * T)[:, :].rearrange("p (k t) -> p k t", k=KT)
        YT = sb("YT", KT * T)[:, :].rearrange("p (k t) -> p k t", k=KT)
        mod = sb("mod", 48)
        mod1 = sb("mod1", 48)
        modc = sb("modc", 16)
        adac = sb("adac", LAYERS * 24)
        coef = sb("coef", 16)
        cs = sb("cs", 24)
        rstd = sb("rstd", T)
        mean = sb("mean", T)
        lam = sb("lam", 8)
        arena = sb("arena", 18448)
        full_flag = ctx.enter_context(nc.sbuf_tensor("full_flag", [P, NE], mybir.dt.int32))
        PS = ctx.enter_context(nc.psum_tensor("PS", [P, 8, 512], F32))
        UX = U2[:, :, C:C + T]
        UC = U2[:, :, 0:C]

        def const(name):
            at, w = CONST_AT[name]
            return consts[:, at:at + w]

        def sm(name, i=0, n=None):
            at, w = SMALL_AT[name]
            return small[:, at + i:at + (w if n is None else i + n)]

        def lsm(name, i=0, n=None):
            at, w = LAYER_AT[name]
            return layer_small[:, at + i:at + (w if n is None else i + n)]

        ones, ident = const("ones"), const("ident")

        def area(at, n):
            return arena[:, at:at + n]

        landed = [ctx.enter_context(nc.semaphore(f"landed{i}")) for i in range(RING)]
        ws = Stream(nc, ring, a["stream"], landed)

        def bc(ap2, k):
            return ap2.unsqueeze(1).broadcast_to([ap2.shape[0], k, ap2.shape[1]])


        def modulation(name, n, vec, bias, out, n_ctx=0, out_ctx=None, vec_ctx=None):
            acc = area(0, 4 * 256).rearrange("p (b n) -> p b n", b=4)
            first = ws.used
            jobs = []
            for k in range(n):
                jobs.append((k, vec, 2 * k))
                if k < n_ctx:
                    jobs.append((k, vec_ctx, 64 + 2 * k))
            last = {k: j + 1 for j, (k, _, _) in enumerate(jobs)}
            with Stage(nc, name, ["chain", "acc_ready", "acc_used", "done"]) as (block, (chain, acc_ready, acc_used, done)):
                @block.sync
                def _(sp):
                    ws.load(sp, first, n, [(acc_ready, last[k]) for k in range(n)])

                @block.vector
                def _(dve):
                    link = Chain(dve, chain)
                    for j, (k, v, _) in enumerate(jobs):
                        ws.wait(dve, first + k)
                        if j >= 4:
                            dve.wait_ge(acc_used, j - 3)
                        w = ws.chunk(first + k).rearrange("p (n k c) -> p n k c", n=2, k=KT)
                        o = acc[:, j % 4, :].rearrange("p (n c) -> p n c", n=2)
                        link(dve.tensor_scalar(o, w[:, :, 0, :], v[:, 0:1], None, ALU.mult))
                        for kt in range(1, KT):
                            ins = dve.scalar_tensor_tensor(out=o, in0=w[:, :, kt, :], scalar=v[:, kt:kt + 1], in1=o,
                                                           op0=ALU.mult, op1=ALU.add)
                            if kt < KT - 1:
                                link(ins)
                        ins.then_inc(acc_ready, 1)
                    dve.wait_ge(acc_used, len(jobs))
                    ins = dve.tensor_tensor(out[:, 0:2 * n], PS[:, 0, 0:2 * n], bias, ALU.add)
                    if n_ctx:
                        link(ins)
                        ins = dve.tensor_tensor(out_ctx[:, 0:2 * n_ctx], PS[:, 0, 64:64 + 2 * n_ctx],
                                                bias[:, 0:2 * n_ctx], ALU.add)
                    ins.then_inc(done, 1)

                @block.tensor
                def _(pe):
                    for j, (_, _, col) in enumerate(jobs):
                        pe.wait_ge(acc_ready, j + 1)
                        for h in range(2):
                            ins = pe.matmul(PS[:, 0, col + h:col + h + 1], acc[:, j % 4, h * P:(h + 1) * P],
                                            ones[:, 0:1], start=True, stop=True)
                        ins.then_inc(acc_used, 1)

        def norm(name, src, scale_of, finish, center=False, eps=EPS, prepare=None):
            sq = area(0, KT * T).rearrange("p (k t) -> p k t", k=KT)
            tmp = area(KT * T, KT * T).rearrange("p (k t) -> p k t", k=KT)
            with Stage(nc, name, ["chain", "sq_ready", "sum_ready", "centred", "var_ready", "std_ready", "scaled", "done"]) as (
                    block, (chain, sq_ready, sum_ready, centred, var_ready, std_ready, scaled, done)):
                def finishing(eng, who):
                    for k in range(KT):
                        if finish[0](k) == who:
                            eng.wait_ge(scaled, k + 1)
                            finish[1](eng, k, tmp[:, k, :]).then_inc(done, 1)

                @block.scalar
                def _(act):
                    for k in range(KT):
                        if center:
                            act.wait_ge(centred, k + 1)
                        nc.scalar.activation(sq[:, k, :], src[:, k, :], ACT.Square).then_inc(sq_ready, 1)
                    act.wait_ge(var_ready, 1)
                    nc.scalar.activation(rstd[:, :], rstd[:, :], ACT.Sqrt).then_inc(std_ready, 1)
                    finishing(act, "act")

                @block.tensor
                def _(pe):
                    if center:
                        for k in range(KT):
                            ins = pe.matmul(PS[:, 1, 0:T], ones, src[:, k, :], start=(k == 0), stop=(k == KT - 1))
                        ins.then_inc(sum_ready, 1)
                    for k in range(KT):
                        pe.wait_ge(sq_ready, k + 1)
                        ins = pe.matmul(PS[:, 0, 0:T], ones, sq[:, k, :], start=(k == 0), stop=(k == KT - 1))
                    ins.then_inc(sum_ready, 1)

                @block.gpsimd
                def _(pool):
                    finishing(pool, "pool")

                @block.vector
                def _(dve):
                    link = Chain(dve, chain)
                    if prepare:
                        prepare(dve, link)
                    if center:
                        dve.wait_ge(sum_ready, 1)
                        link(dve.tensor_scalar(mean[:, :], PS[:, 1, 0:T], 1.0 / D, None, ALU.mult))
                        for k in range(KT):
                            dve.tensor_tensor(src[:, k, :], src[:, k, :], mean[:, :], ALU.subtract).then_inc(centred, 1)
                    dve.wait_ge(sum_ready, 2 if center else 1)
                    dve.tensor_scalar(rstd[:, :], PS[:, 0, 0:T], 1.0 / D, eps, ALU.mult, ALU.add).then_inc(var_ready, 1)
                    dve.wait_ge(std_ready, 1)
                    link(dve.reciprocal(rstd[:, :], rstd[:, :]))
                    if center:
                        dve.wait_ge(centred, KT)
                    for k in range(KT):
                        dve.scalar_tensor_tensor(out=tmp[:, k, :], in0=src[:, k, :], scalar=scale_of(k), in1=rstd[:, :],
                                                 op0=ALU.mult, op1=ALU.mult).then_inc(scaled, 1)
                    finishing(dve, "dve")

        def plus_bias(dst, b):
            return (lambda k: "act",
                    lambda act, k, tmp: nc.scalar.activation(dst[:, k, :], tmp, ACT.Identity, bias=b[:, k:k + 1]))

        def modulated(name, src, dst, g, shift, scale):
            norm(name, src, lambda k: coef[:, k:k + 1], plus_bias(dst, shift),
                 prepare=lambda dve, link: link(dve.scalar_tensor_tensor(out=coef[:, 0:KT], in0=scale, scalar=1.0, in1=g,
                                                                         op0=ALU.add, op1=ALU.mult)))

        def residual(name, src, g, gate):
            norm(name, src, lambda k: coef[:, k:k + 1],
                 (lambda k: "pool" if k < 4 else "dve",
                  lambda eng, k, tmp: eng.tensor_tensor(XT[:, k, :], XT[:, k, :], tmp, ALU.add)),
                 prepare=lambda dve, link: link(dve.tensor_tensor(coef[:, 0:KT], gate, g, ALU.mult)))

        class Side:

            def __init__(self, places, vec, bias, out, col, acc_at):
                self.places, self.vec, self.bias, self.out, self.col = places, vec, bias, out, col
                self.acc = area(acc_at, 512).rearrange("p (b n) -> p b n", b=2)

            def sum_rows(self, dve, link, z, acc_ready, acc_used):
                ws.wait(dve, self.places[z])
                if z >= 2:
                    dve.wait_ge(acc_used, z - 1)
                w = ws.chunk(self.places[z]).rearrange("p (n k c) -> p n k c", n=2, k=KT)
                o = self.acc[:, z % 2, :].rearrange("p (n c) -> p n c", n=2)
                link(dve.tensor_scalar(o, w[:, :, 0, :], self.vec[:, 0:1], None, ALU.mult))
                for kt in range(1, KT):
                    ins = dve.scalar_tensor_tensor(out=o, in0=w[:, :, kt, :], scalar=self.vec[:, kt:kt + 1], in1=o,
                                                   op0=ALU.mult, op1=ALU.add)
                    if kt < KT - 1:
                        link(ins)
                ins.then_inc(acc_ready, 1)

            def sum_partitions(self, pe, z, acc_ready, acc_used):
                pe.wait_ge(acc_ready, z + 1)
                for h in range(2):
                    ins = pe.matmul(PS[:, 7, 2 * z + h:2 * z + h + 1], self.acc[:, z % 2, h * P:(h + 1) * P], ones[:, 0:1],
                                    start=True, stop=True)
                ins.then_inc(acc_used, 1)

            def finish(self, dve, acc_used):
                n = len(self.places)
                dve.wait_ge(acc_used, n)
                c = self.col
                return dve.tensor_tensor(self.out[:, c:c + 2 * n], PS[:, 7, 0:2 * n], self.bias[:, c:c + 2 * n], ALU.add)

        def project(name, n, tasks, side=None):
            first = ws.used
            nb = 7 if side else 8
            n_side = side[0] if side else 0
            main, places = interleave(n, n_side)
            sd = Side([first + p for p in places], *side[1:]) if side else None
            count = {"act": 0, "dve": 0}
            emptied = []
            for t in tasks:
                count[t[2]] += 1
                emptied.append((t[2], count[t[2]]))
            last = {}
            for j, t in enumerate(tasks):
                last[t[0]] = j + 1
            with Stage(nc, name, ["chain_d", "chain_a", "bank_full", "act_emptied", "dve_emptied", "acc_ready", "acc_used", "side_done"]) as (
                    block, (chain_d, chain_a, bank_full, act_emptied, dve_emptied, acc_ready, acc_used, side_done)):
                by = {"act": act_emptied, "dve": dve_emptied}

                @block.sync
                def _(sp):
                    freed = {main[k]: (bank_full, last[k]) for k in range(n)}
                    freed.update({p: (acc_ready, z + 1) for z, p in enumerate(places)})
                    ws.load(sp, first, n + n_side, [freed[p] for p in range(n + n_side)])

                @block.tensor
                def _(pe):
                    z = 0
                    for j, (k, matmuls, _, _) in enumerate(tasks):
                        ws.wait(pe, first + main[k])
                        if j >= nb:
                            e, v = emptied[j - nb]
                            pe.wait_ge(by[e], v)
                        for o, l, r, s, e in matmuls(PS[:, j % nb, :], ws.chunk(first + main[k])):
                            ins = pe.matmul(o, l, r, start=s, stop=e)
                        ins.then_inc(bank_full, 1)
                        if last[k] == j + 1 and z < k and z < n_side:
                            sd.sum_partitions(pe, z, acc_ready, acc_used)
                            z += 1
                    for z in range(z, n_side):
                        sd.sum_partitions(pe, z, acc_ready, acc_used)

                def evacuate(eng, who, link):
                    z = 0
                    for j, (k, _, e, f) in enumerate(tasks):
                        if e == who:
                            eng.wait_ge(bank_full, j + 1)
                            f(eng, PS[:, j % nb, :], link).then_inc(by[who], 1)
                        if who == "dve" and last[k] == j + 1 and z < n_side:
                            sd.sum_rows(eng, link, z, acc_ready, acc_used)
                            z += 1
                    if who == "dve" and n_side:
                        for z in range(z, n_side):
                            sd.sum_rows(eng, link, z, acc_ready, acc_used)
                        sd.finish(eng, acc_used).then_inc(side_done, 1)

                @block.scalar
                def _(act):
                    evacuate(act, "act", Chain(act, chain_a))

                @block.vector
                def _(dve):
                    evacuate(dve, "dve", Chain(dve, chain_d))

        def tile_task(k, h, rhs, engine, evacuate, ncols=P, c0=0):
            def matmuls(bank, chunk):
                w = chunk.rearrange("p (n k c) -> p n k c", n=2, k=KT)
                N = rhs.shape[2]
                return [(bank[0:ncols, 0:N], w[:, h, kt, c0:c0 + ncols], rhs[:, kt, :], kt == 0, kt == KT - 1)
                        for kt in range(KT)]
            return (k, matmuls, engine, evacuate)

        def token_task(k, lhs, t0, engine, evacuate):
            def matmuls(bank, chunk):
                w = chunk.rearrange("p (n k c) -> p n k c", n=2, k=KT)
                o = bank[:, 0:2 * P].rearrange("p (n c) -> p n c", n=2)
                return [(o, lhs[:, kt, t0:t0 + P], w[:, :, kt, :], kt == 0, kt == KT - 1) for kt in range(KT)]
            return (k, matmuls, engine, evacuate)

        def copy_to(dst, n=None, scale=1.0):
            def f(act, bank, link):
                o = dst
                src = bank[0:dst.shape[0], 0:dst.shape[1]] if len(dst.shape) == 2 else \
                    bank[:, 0:dst.shape[1] * dst.shape[2]].rearrange("p (a b) -> p a b", a=dst.shape[1])
                return nc.scalar.activation(o, src, ACT.Copy, scale=scale)
            return f

        def copy_bias(dst, b):
            def f(act, bank, link):
                return nc.scalar.activation(dst, bank[:, 0:dst.shape[1]], ACT.Identity, bias=b)
            return f

        def pointwise(name, steps):
            with Stage(nc, name, ["step_done"]) as (block, (step_done,)):
                def run(eng, who):
                    for i, (w, f) in enumerate(steps):
                        if w.rstrip("!") == who:
                            assert w == who or steps[i - 1][0].rstrip("!") == who
                            if i and w == who:
                                eng.wait_ge(step_done, i)
                            f(eng).then_inc(step_done, 1)
                    eng.nop()

                @block.scalar
                def _(act):
                    run(act, "act")

                @block.vector
                def _(dve):
                    run(dve, "dve")

                @block.tensor
                def _(pe):
                    run(pe, "pe")

                @block.gpsimd
                def _(pool):
                    run(pool, "pool")

        def sigmoid_steps(src, dst):
            return [("act", lambda e: nc.scalar.activation(dst, src, ACT.Sigmoid))]

        def silu_steps(x):
            return [("act", lambda e: nc.scalar.activation(x, x, ACT.Silu))]

        def log_sigmoid_steps(z, t1, t2):
            return [("dve", lambda e: e.scalar_tensor_tensor(out=t1, in0=z, scalar=-1.0, in1=z, op0=ALU.mult, op1=ALU.max)),
                    ("act", lambda e: nc.scalar.activation(t1, t1, ACT.Exp, scale=-1.0)),
                    ("dve", lambda e: e.tensor_scalar(t1, t1, 1.0, None, ALU.add)),
                    ("act", lambda e: nc.scalar.activation(t2, t1, ACT.Ln)),
                    ("dve", lambda e: e.scalar_tensor_tensor(out=z, in0=z, scalar=0.0, in1=t2, op0=ALU.min, op1=ALU.subtract))]

        def rope(name, tiles, tmp_at):
            tmp = area(tmp_at, 2 * T).rearrange("p (b t) -> p b t", b=2)
            with Stage(nc, name, ["chain", "rotated", "done"]) as (block, (chain, rotated, done)):
                @block.tensor
                def _(pe):
                    for j, (x, m, _, _) in enumerate(tiles):
                        if j >= 4:
                            pe.wait_ge(done, j - 3)
                        pe.matmul(PS[:, j % 4, 0:T], const(m), x, start=True, stop=True).then_inc(rotated, 1)

                @block.vector
                def _(dve):
                    link = Chain(dve, chain)
                    for j, (x, _, c, s) in enumerate(tiles):
                        dve.wait_ge(rotated, j + 1)
                        link(dve.tensor_tensor(tmp[:, 0, :], PS[:, j % 4, 0:T], const(s), ALU.mult))
                        link(dve.tensor_tensor(tmp[:, 1, :], x, const(c), ALU.mult))
                        dve.tensor_tensor(x, tmp[:, 0, :], tmp[:, 1, :], ALU.add).then_inc(done, 1)
                        dve.wait_ge(done, j + 1)

        def ffn(name, src, side):
            H = area(0, FT * T).rearrange("p (k t) -> p k t", k=FT)
            EX = area(FT * T, 2 * T).rearrange("p (b t) -> p b t", b=2)
            first = ws.used
            n2 = KT * FT // BLOCKS
            n_side = side[0]
            main, places = interleave(FFN_CH, n_side)
            sd = Side([first + p for p in places], *side[1:])
            with Stage(nc, name, ["chain", "pair_ready", "silu_ready", "hidden_done", "w2_chunk", "y_ready", "y_done",
                                  "acc_ready", "acc_used", "side_done"]) as (
                    block, (chain, pair_ready, silu_ready, hidden_done, w2_chunk, y_ready, y_done, acc_ready, acc_used, side_done)):
                @block.sync
                def _(sp):
                    own = [(pair_ready, m + 1) for m in range(FT)] + [(w2_chunk, q + 1) for q in range(n2 - 1)] + [(y_ready, KT)]
                    freed = dict(zip(main, own))
                    freed.update({p: (acc_ready, z + 1) for z, p in enumerate(places)})
                    ws.load(sp, first, FFN_CH + n_side, [freed[p] for p in range(FFN_CH + n_side)])

                @block.tensor
                def _(pe):
                    for m in range(FT):
                        ws.wait(pe, first + main[m])
                        if m >= 4:
                            pe.wait_ge(hidden_done, m - 3)
                        w = ws.chunk(first + main[m]).rearrange("p (n k c) -> p n k c", n=2, k=KT)
                        for h in range(2):
                            for kt in range(KT):
                                ins = pe.matmul(PS[:, m % 4, h * T:(h + 1) * T], w[:, h, kt, :], src[:, kt, :],
                                                start=(kt == 0), stop=(kt == KT - 1))
                        ins.then_inc(pair_ready, 1)
                        if m >= 1:
                            sd.sum_partitions(pe, m - 1, acc_ready, acc_used)
                    b = 0
                    for o in range(KT):
                        if o >= 3:
                            pe.wait_ge(y_done, o - 2)
                        for m in range(FT):
                            if b % BLOCKS == 0:
                                ws.wait(pe, first + main[FT + b // BLOCKS])
                            if o == 0:
                                pe.wait_ge(hidden_done, m + 1)
                            w = ws.chunk(first + main[FT + b // BLOCKS])
                            ins = pe.matmul(PS[:, 4 + o % 3, 0:T], w[:, (b % BLOCKS) * P:(b % BLOCKS + 1) * P], H[:, m, :],
                                            start=(m == 0), stop=(m == FT - 1))
                            if m == FT - 1:
                                ins.then_inc(y_ready, 1)
                            elif b % BLOCKS == BLOCKS - 1:
                                ins.then_inc(w2_chunk, 1)
                            b += 1
                        if o == 0:
                            for z in range(FT - 1, n_side):
                                sd.sum_partitions(pe, z, acc_ready, acc_used)

                @block.scalar
                def _(act):
                    for m in range(FT):
                        act.wait_ge(pair_ready, m + 1)
                        if m >= 2:
                            act.wait_ge(hidden_done, m - 1)
                        nc.scalar.activation(EX[:, m % 2, :], PS[:, m % 4, 0:T], ACT.Silu).then_inc(silu_ready, 1)
                    for o in range(KT):
                        act.wait_ge(y_ready, o + 1)
                        nc.scalar.activation(YT[:, o, :], PS[:, 4 + o % 3, 0:T], ACT.Copy).then_inc(y_done, 1)

                @block.vector
                def _(dve):
                    link = Chain(dve, chain)
                    for m in range(FT):
                        e = EX[:, m % 2, :]
                        dve.wait_ge(silu_ready, m + 1)
                        dve.tensor_tensor(H[:, m, :], PS[:, m % 4, T:2 * T], e, ALU.mult).then_inc(hidden_done, 1)
                        sd.sum_rows(dve, link, m, acc_ready, acc_used)
                    for z in range(FT, n_side):
                        sd.sum_rows(dve, link, z, acc_ready, acc_used)
                    sd.finish(dve, acc_used).then_inc(side_done, 1)

        def attention(name, jobs, scale, at):
            SB = area(at, 2 * 1024).rearrange("p (j b n) -> p j b n", j=2, b=2)
            PB = area(at + 2048, 3 * 1024).rearrange("p (j b n) -> p j b n", j=3, b=2)
            PT = area(at + 5120, 2 * 640).rearrange("p (j n) -> p j n", j=2)
            ST = mean[:, 0:48].rearrange("p (j n) -> p j n", j=3)
            n = len(jobs)
            cum = [sum(len(j["scores"]) for j in jobs[:i + 1]) for i in range(n)]

            def branch(buf, job, bi):
                for bank, b0, c, w, _ in job["groups"]:
                    if b0 <= bi < b0 + c:
                        return buf[:, bi, 0:w] if bank is None else buf[:, bank, 256 * (bi - b0):256 * (bi - b0) + w]

            def group(buf, g):
                bank, b0, c, w, _ = g
                if bank is None:
                    return buf[:, :, 0:w]
                return buf[:, bank, 0:w] if c == 1 else buf[:, bank, :].rearrange("p (c n) -> p c n", c=c)[:, :, 0:w]

            def scores_ps(i):
                return PS[:, 2 * (i % 2):2 * (i % 2) + 2, :]

            def pieces(job):
                out = []
                for base, brs in job["outs"]:
                    for bi, vs in brs:
                        for z, v in enumerate(vs):
                            out.append((base, bi, z * P, v.shape[0], v, len(out) * P))
                return out

            def turned_ps(q, at_):
                return PS[:, 4 + q % 2, at_:at_ + P] if at_ < 512 else PS[:, 6 + q % 2, 256:256 + P]

            with Stage(nc, name, ["chain", "scores", "negmax", "exps", "probs", "turned", "turned_copied", "out_ready", "out_done"]) as (
                    block, (chain, scores, negmax, exps, probs, turned, copied, out_ready, out_done)):
                @block.tensor
                def _(pe):
                    for i in range(n + 3):
                        if i < n:
                            job = jobs[i]
                            if i >= 2 and jobs[i - 2]["groups"][0][4] is None:
                                pe.wait_ge(exps, cum[i - 2])
                            elif i >= 2:
                                pe.wait_ge(negmax, i - 1)
                            for bi, (q_, k_) in enumerate(job["scores"]):
                                ins = pe.matmul(branch(scores_ps(i), job, bi), q_, k_, start=True, stop=True)
                            ins.then_inc(scores, 1)
                        q = i - 2
                        if 0 <= q < n:
                            pe.wait_ge(probs, q + 1)
                            if q >= 2:
                                pe.wait_ge(copied, q - 1)
                                if len(pieces(jobs[q])) > 4:
                                    pe.wait_ge(out_done, q - 1)
                            for _b, bi, k0, rows, _v, at_ in pieces(jobs[q]):
                                src = branch(PB[:, q % 3], jobs[q], bi)[:, k0:k0 + rows]
                                ins = pe.transpose(turned_ps(q, at_)[0:rows, :], src, ident)
                            ins.then_inc(turned, 1)
                        q = i - 3
                        if 0 <= q < n:
                            pe.wait_ge(copied, q + 1)
                            if q >= 2:
                                pe.wait_ge(out_done, q - 1)
                            ps = pieces(jobs[q])
                            for z, (base, bi, k0, rows, v, at_) in enumerate(ps):
                                p_ = PT[0:rows, q % 2, at_:at_ + P]
                                if jobs[q].get("token_major"):
                                    o, l, r = PS[:, 6 + q % 2, 0:v.shape[1]], p_, v
                                else:
                                    o, l, r = PS[base:base + v.shape[1], 6 + q % 2, 0:P], v, p_
                                ins = pe.matmul(o, l, r, start=(z == 0 or ps[z - 1][0] != base),
                                                stop=(z == len(ps) - 1 or ps[z + 1][0] != base))
                            ins.then_inc(out_ready, 1)

                @block.vector
                def _(dve):
                    link = Chain(dve, chain)
                    for i in range(n + 1):
                        job, q = (jobs[i] if i < n else None), i - 1
                        S_, R_ = ST[:, i % 3, :], ST[:, q % 3, :]
                        if job:
                            dve.wait_ge(scores, i + 1)
                            for g in job["groups"]:
                                if g[4] is not None:
                                    if i >= 2:
                                        dve.wait_ge(exps, cum[i - 2])
                                    link.go(dve.scalar_tensor_tensor(out=group(SB[:, i % 2], g), in0=group(scores_ps(i), g), scalar=scale,
                                                                     in1=g[4], op0=ALU.mult, op1=ALU.add))
                        if q >= 0:
                            dve.wait_ge(exps, cum[q])
                            nb = len(jobs[q]["scores"])
                            link.go(dve.tensor_scalar(R_[:, 8:8 + nb], R_[:, 8:8 + nb], 1e-30, None, ALU.max))
                        link.sync()
                        if job:
                            for g in job["groups"]:
                                src = scores_ps(i) if g[4] is None else SB[:, i % 2]
                                link.go(dve.reduce_max(S_[:, g[1]:g[1] + g[2]], group(src, g), AX))
                        if q >= 0:
                            link.go(dve.reciprocal(R_[:, 12:12 + nb], R_[:, 8:8 + nb]))
                        link.sync()
                        if job:
                            c = len(job["scores"])
                            f = -scale if job["groups"][0][4] is None else -1.0
                            dve.tensor_scalar(S_[:, 4:4 + c], S_[:, 0:c], FLOOR, f, ALU.max, ALU.mult).then_inc(negmax, 1)
                        if q >= 0:
                            if jobs[q]["coef"] is not None:
                                b0, cf = jobs[q]["coef"]
                                link(dve.tensor_tensor(R_[:, 12 + b0:12 + nb], R_[:, 12 + b0:12 + nb], cf, ALU.mult))
                            for bi in range(nb):
                                r_, p_ = R_[:, 12 + bi:13 + bi], branch(PB[:, q % 3], jobs[q], bi)
                                if bi and jobs[q].get("minus"):
                                    link.sync()
                                    o_ = branch(PB[:, q % 3], jobs[q], 0)
                                    ins = dve.scalar_tensor_tensor(out=o_, in0=p_, scalar=r_, in1=o_, op0=ALU.mult, op1=ALU.add)
                                else:
                                    ins = dve.tensor_scalar(p_, p_, r_, None, ALU.mult)
                                if bi < nb - 1:
                                    link.go(ins)
                            link.sync()
                            ins.then_inc(probs, 1)

                @block.scalar
                def _(act):
                    for i in range(n + 3):
                        if i < n:
                            job = jobs[i]
                            act.wait_ge(negmax, i + 1)
                            if i >= 3:
                                act.wait_ge(turned, i - 2)
                            for bi in range(len(job["scores"])):
                                biased = job["groups"][0][4] is not None
                                s = branch(SB[:, i % 2] if biased else scores_ps(i), job, bi)
                                nc.scalar.activation(branch(PB[:, i % 3], job, bi), s, ACT.Exp, bias=ST[:, i % 3, 4 + bi:5 + bi],
                                                     scale=1.0 if biased else scale,
                                                     accum_out=ST[:, i % 3, 8 + bi:9 + bi]).then_inc(exps, 1)
                        q = i - 2
                        if 0 <= q < n:
                            act.wait_ge(turned, q + 1)
                            if q >= 2:
                                act.wait_ge(out_ready, q - 1)
                            ps = pieces(jobs[q])
                            z = 0
                            while z < len(ps):
                                e = z + 1
                                while e < min(len(ps), 4) and ps[e][3] == ps[z][3] and z < 4:
                                    e += 1
                                w_ = P * (e - z)
                                rows, at_ = ps[z][3], ps[z][5]
                                src = PS[0:rows, 4 + q % 2, at_:at_ + w_] if at_ < 512 else turned_ps(q, at_)[0:rows, :]
                                ins = nc.scalar.activation(PT[0:rows, q % 2, at_:at_ + w_], src, ACT.Copy)
                                z = e
                            ins.then_inc(copied, 1)
                        q = i - 3
                        if 0 <= q < n:
                            act.wait_ge(out_ready, q + 1)
                            o = jobs[q]["out"]
                            nc.scalar.activation(o, PS[:, 6 + q % 2, 0:o.shape[1]] if o.shape[0] == P else
                                                 PS[jobs[q]["outs"][0][0]:jobs[q]["outs"][0][0] + 64, 6 + q % 2, 0:P],
                                                 ACT.Copy).then_inc(out_done, 1)


        with Stage(nc, "load", ["loaded", "step"]) as (block, (loaded, step)):
            @block.sync
            def _(sp):
                for dst, src in ((consts[:, :], a["consts"]), (small[:, :], a["small"]),
                                 (XT, a["xT"]), (UC, a["ctxT"])):
                    sp.dma_start(dst, src).then_inc(loaded, 16)

            @block.vector
            def _(dve):
                dve.wait_ge(loaded, 64)
                dve.memset(mod[:, :], 0.0).then_inc(step, 1)
                dve.wait_ge(step, 1)
                dve.nop()

        silu_in = small[:, SMALL_AT["c"][0]:SMALL_AT["c"][0] + 16]
        lq = sm("lam")
        pointwise("silu_c", [
            ("act", lambda e: nc.scalar.activation(cs[:, 0:16], silu_in, ACT.Silu)),
            ("dve", lambda e: e.tensor_tensor(lam[:, 0:2], lq[:, 0:2], lq[:, 2:4], ALU.mult)),
            ("pe", lambda e: e.matmul(PS[:, 0, 0:2], ones[0:64, :], lam[0:64, 0:2], start=True, stop=True)),
            ("act", lambda e: nc.scalar.activation(lam[:, 2:4], PS[:, 0, 0:2], ACT.Exp)),
            ("dve", lambda e: e.tensor_tensor(lam[:, 4:5], lam[:, 3:4], lam[:, 2:3], ALU.subtract)),
            ("dve", lambda e: e.tensor_scalar(lam[:, 5:6], lam[:, 4:5], -LAM_INIT, None, ALU.add))])

        ws.begin(0, MOD_CH + IN0_CH + OUT_CH + FFN_CH + MOD_CH + PW1_CH + OUT_CH)
        modulation("mod0", MOD_FIRST, cs[:, 0:8], sm("mod_b0", 0, 2 * MOD_FIRST), mod, MOD_FIRST, modc, cs[:, 8:16])

        def mpart(i, m=None):
            return (mod if m is None else m)[:, KT * i:KT * (i + 1)]

        modulated("norm_ctx", UC, UC, sm("pre0"), modc[:, 0:8], modc[:, 8:16])
        modulated("norm_x", XT, UX, sm("pre0"), mpart(0), mpart(1))

        qm = area(0, 1024).rearrange("p (k t) -> p k t", k=4)
        km = area(1024, 2048).rearrange("p (k t) -> p k t", k=4)
        vm = area(3072, 2080).rearrange("p (s h d) -> p s h d", s=4, h=8)
        om = area(5152, 1024).rearrange("p (k t) -> p k t", k=4)
        gt = area(6176, 2048).rearrange("p (g t) -> p g t", g=4)
        dq = area(8224, 1024).rearrange("p (k t) -> p k t", k=4)
        dk = area(9248, 2048).rearrange("p (k t) -> p k t", k=4)
        dv = area(11296, 2048).rearrange("p (s n) -> p s n", s=4)
        SCR = 13344
        mixT = YT
        cw = sm("conv_w")

        def conv3(dst, col, segs):
            def f(dve, bank, link):
                for z, (s0, d0) in enumerate(segs):
                    x, y = bank[:, s0:s0 + T], dst[:, d0:d0 + T]
                    link(dve.tensor_scalar(y, x, cw[:, 3 * col + 1:3 * col + 2], None, ALU.mult))
                    link(dve.scalar_tensor_tensor(out=y[:, 1:T], in0=x[:, 0:T - 1], scalar=cw[:, 3 * col:3 * col + 1],
                                                  in1=y[:, 1:T], op0=ALU.mult, op1=ALU.add))
                    ins = dve.scalar_tensor_tensor(out=y[:, 0:T - 1], in0=x[:, 1:T], scalar=cw[:, 3 * col + 2:3 * col + 3],
                                                   in1=y[:, 0:T - 1], op0=ALU.mult, op1=ALU.add)
                    if z < len(segs) - 1:
                        link(ins)
                return ins
            return f

        tasks = []
        for m in range(4):
            tasks.append(tile_task(m // 2, m % 2, UX, "dve", conv3(qm[:, m, :], m, [(0, 0)])))
        for m in range(4):
            tasks.append(tile_task(2 + m // 2, m % 2, U2, "dve", conv3(km[:, m, :], 4 + m, [(0, 0), (C, C)])))

        def copy_v(s, h0):
            def f(act, bank, link):
                return nc.scalar.activation(vm[:, s, h0:h0 + 4, 0:64], bank[:, 0:256].rearrange("p (h d) -> p h d", h=4),
                                            ACT.Copy)
            return f
        for c_ in range(2):
            for s in range(4):
                tasks.append(token_task(4 + c_, U2, s * P, "act", copy_v(s, 4 * c_)))
        for m in range(4):
            tasks.append(tile_task(6 + m // 2, m % 2, UX, "act", copy_to(om[:, m, :])))
        for g in range(4):
            def gate_copy(g):
                def f(act, bank, link):
                    return nc.scalar.activation(gt[0:8, g, :], bank[0:8, 0:512], ACT.Identity, bias=sm("gate_b", g, 1)[0:8, :])
                return f
            tasks.append(tile_task(8, 0, U2, "act", gate_copy(g), ncols=8, c0=8 * g))
        for m in range(4):
            tasks.append(tile_task(9 + m // 2, m % 2, UX, "act", copy_to(dq[:, m, :])))
        for m in range(4):
            tasks.append(tile_task(11 + m // 2, m % 2, U2, "act", copy_to(dk[:, m, :])))
        for c_ in range(2):
            for s in range(4):
                tasks.append(token_task(13 + c_, U2, s * P, "act", copy_to(dv[:, s, 256 * c_:256 * (c_ + 1)])))
        side_bias = sm("mod_b0")
        project("in0", IN0_CH, tasks, (MOD_CH - MOD_FIRST, cs[:, 0:8], side_bias, mod, 2 * MOD_FIRST, SCR))

        gB = area(SCR, 1024).rearrange("p (d t) -> p d t", d=2)
        gM = area(SCR + 1024, 1024).rearrange("p (d t) -> p d t", d=2)
        gN = area(SCR + 2048, 1024).rearrange("p (d e t) -> p d e t", d=2, e=2)
        tA = area(SCR + 3072, 64).rearrange("p (d s h) -> p d s h", d=2, s=4)
        tM = area(SCR + 3072 + 64, 32).rearrange("p (d s h) -> p d s h", d=2, s=2)
        lf, ig = gt[0:8, 1:4:2, :], gt[0:8, 0:4:2, :]
        o512 = ones[0:8, 0:1].broadcast_to([8, 512])
        B8, M8, A8 = gB[0:8], gM[0:8], gt[0:8, 0:4:2, :]
        steps = log_sigmoid_steps(lf, B8, M8)
        steps += [
            ("dve", lambda e: e.tensor_tensor_scan(B8[:, 0, :], o512, gt[0:8, 1, :], 0.0, ALU.mult, ALU.add)),
            ("dve", lambda e: e.tensor_tensor_scan(B8[:, 1, C - 1::-1], o512[:, 0:C], gt[0:8, 3, C - 1::-1], 0.0, ALU.mult, ALU.add)),
            ("dve", lambda e: e.tensor_tensor_scan(B8[:, 1, 511:C - 1:-1], o512[:, 0:T], gt[0:8, 3, 511:C - 1:-1], B8[:, 1, 0:1], ALU.mult, ALU.add)),
            ("dve", lambda e: e.tensor_tensor(A8, ig, B8, ALU.subtract)),
            ("dve", lambda e: e.tensor_tensor_scan(M8[:, 0, :], gt[0:8, 0, :], gt[0:8, 0, :], NEG, ALU.max, ALU.max)),
            ("dve", lambda e: e.tensor_tensor_scan(M8[:, 1, C - 1::-1], gt[0:8, 2, C - 1::-1], gt[0:8, 2, C - 1::-1], NEG, ALU.max, ALU.max)),
            ("dve", lambda e: e.tensor_tensor_scan(M8[:, 1, 511:C - 1:-1], gt[0:8, 2, 511:C - 1:-1], gt[0:8, 2, 511:C - 1:-1], M8[:, 1, 0:1], ALU.max, ALU.max)),
            ("dve", lambda e: e.tensor_scalar(gN[0:8, :, 0, :], M8[:, :, C:], -1.0, None, ALU.mult)),
            ("dve", lambda e: e.tensor_tensor(B8[:, :, C:], B8[:, :, C:], M8[:, :, C:], ALU.add)),
            ("act", lambda e: nc.scalar.activation(gN[0:8, :, 1, :], B8[:, :, C:], ACT.Exp, scale=-1.0)),
            ("dve", lambda e: e.memset(vm[:, :, :, 64:65], 1.0)),
        ]
        for d in range(2):
            for s in range(4):
                steps.append(("pe!" if d + s else "pe", lambda e, d=d, s=s: e.transpose(PS[:, 0, (d * 4 + s) * 8:(d * 4 + s + 1) * 8],
                                                                    gt[0:8, 2 * d, s * P:(s + 1) * P], ident[0:8, 0:8])))
        for d in range(2):
            for s in range(2):
                steps.append(("pe!", lambda e, d=d, s=s: e.transpose(PS[:, 0, 64 + (d * 2 + s) * 8:64 + (d * 2 + s + 1) * 8],
                                                                    gN[0:8, d, 1, s * P:(s + 1) * P], ident[0:8, 0:8])))
        steps.append(("act", lambda e: nc.scalar.activation(area(SCR + 3072, 96), PS[:, 0, 0:96], ACT.Copy)))
        steps += silu_steps(area(0, 3072))
        pointwise("gates0", steps)

        Hm = area(SCR, 1024).rearrange("p (t h d) -> p t h d", t=2, h=8)
        EE = U2.rearrange("p k t -> p (k t)").rearrange("p (j d s t) -> p j d s t", j=2, d=2, s=4)
        dn = mean[:, 0:16].rearrange("p (j n) -> p j n", j=2)
        NH = 8
        with Stage(nc, "mlstm", ["chain", "kq", "mrow", "e_done", "s_done", "num", "h_done"]) as (
                block, (chain, kq, mrow, e_done, s_done, num, h_done)):
            def base(h):
                return 64 * (h % 2)

            def scores_of(h):
                return PS[:, 2 * (h % 2):2 * (h % 2) + 2, :].rearrange("p b (s t) -> p (b s) t", s=2)

            @block.tensor
            def _(pe):
                for i in range(NH + 1):
                    if i < NH:
                        h = i
                        b0 = base(h)
                        if h >= 2:
                            pe.wait_ge(s_done, 6 * (h - 1))
                        for s in range(4):
                            ins = pe.matmul(scores_of(h)[:, s, :], km[b0:b0 + 64, h // 2, s * P:(s + 1) * P],
                                            qm[b0:b0 + 64, h // 2, :], start=True, stop=True)
                        ins.then_inc(kq, 1)
                        if h >= 1:
                            pe.wait_ge(e_done, 10 * h)
                        for d in range(2):
                            lhs = ident[0:8, h:h + 1].broadcast_to([8, P])
                            pe.matmul(PS[:, 4 + d, 0:T], lhs, gN[0:8, d, 0, :], start=True, stop=True)
                            pe.matmul(PS[:, 4 + d, T:2 * T], lhs, gN[0:8, d, 0, :], start=True, stop=False)
                            ins = pe.matmul(PS[:, 4 + d, T:2 * T], ident, const("bmask" if d else "fmask"), start=False, stop=True)
                            ins.then_inc(mrow, 1)
                    if i >= 1:
                        h = i - 1
                        pe.wait_ge(s_done, 6 * (h + 1))
                        if h >= 1:
                            pe.wait_ge(h_done, h)
                        for d in range(2):
                            for t in range(2):
                                keys = [0, 1] + ([2] if (d, t) == (0, 0) else [3] if (d, t) == (1, 1) else [2, 3])
                                o = PS[:, 6 + d, t * 65:(t + 1) * 65]
                                for z, s in enumerate(keys):
                                    ins = pe.matmul(o, EE[:, h % 2, d, s, t * P:(t + 1) * P], vm[:, s, h, :],
                                                    start=(z == 0), stop=(z == len(keys) - 1))
                        ins.then_inc(num, 1)

            def regions(d):
                return [(2, 0, P, 1), (2, P, P, 0), (3, P, P, 1)] if d == 0 else [(3, 0, P, 0), (3, P, P, 1), (2, 0, P, 1)]

            @block.scalar
            def _(act):
                for h in range(NH):
                    if h >= 2:
                        act.wait_ge(num, h - 1)
                    for d in range(2):
                        act.wait_ge(mrow, 2 * h + d + 1)
                        for s in range(2):
                            nc.scalar.activation(EE[:, h % 2, d, s, :], PS[:, 4 + d, 0:T], ACT.Exp,
                                                 bias=tA[:, d, s, h:h + 1]).then_inc(e_done, 1)
                        for s, q0, nq, masked in regions(d):
                            nc.scalar.activation(EE[:, h % 2, d, s, q0:q0 + nq], PS[:, 4 + d, masked * T + q0:masked * T + q0 + nq],
                                                 ACT.Exp, bias=tA[:, d, s, h:h + 1]).then_inc(e_done, 1)

            @block.vector
            def _(dve):
                link = Chain(dve, chain)
                for i in range(NH + 1):
                    if i < NH:
                        h = i
                        dve.wait_ge(kq, h + 1)
                        for d in range(2):
                            dve.wait_ge(e_done, 10 * h + 5 * d + 5)
                            sc = scores_of(h)
                            full, half, q0 = (2, 3, P) if d == 0 else (3, 2, 0)
                            e_ = EE[:, h % 2, d]
                            for x, y in ((e_[:, 0:2, :], sc[:, 0:2, :]), (e_[:, full, :], sc[:, full, :]),
                                         (e_[:, half, q0:q0 + P], sc[:, half, q0:q0 + P])):
                                dve.scalar_tensor_tensor(out=x, in0=y, scalar=0.125, in1=x, op0=ALU.mult,
                                                         op1=ALU.mult).then_inc(s_done, 1)
                    if i >= 1:
                        h = i - 1
                        dve.wait_ge(num, h + 1)
                        nm = PS[:, 6:8, 0:130].rearrange("p d (t n) -> p d t n", t=2)
                        den = nm[:, :, :, 64]
                        r = dn[:, h % 2, 0:4].rearrange("p (d t) -> p d t", d=2)
                        r2 = dn[:, h % 2, 4:8].rearrange("p (d t) -> p d t", d=2)
                        link(dve.tensor_scalar(r2, den, -1.0, None, ALU.mult))
                        link(dve.tensor_tensor(r, den, r2, ALU.max))
                        link(dve.tensor_tensor(r, r, tM[:, :, :, h], ALU.max))
                        link(dve.reciprocal(r2, r))
                        for t in range(2):
                            link(dve.tensor_scalar(Hm[:, t, h, :], nm[:, 0, t, 0:64], r2[:, 0, t:t + 1], None, ALU.mult))
                        for t in range(2):
                            ins = dve.scalar_tensor_tensor(out=Hm[:, t, h, :], in0=nm[:, 1, t, 0:64], scalar=r2[:, 1, t:t + 1],
                                                           in1=Hm[:, t, h, :], op0=ALU.mult, op1=ALU.add)
                            if t == 0:
                                link(ins)
                        ins.then_inc(h_done, 1)

        def turn_heads(name, src_of, dst_of, n_tiles):
            with Stage(nc, name, ["turned", "copied"]) as (block, (turned, copied)):
                @block.tensor
                def _(pe):
                    for m in range(n_tiles):
                        if m >= 4:
                            pe.wait_ge(copied, m - 3)
                        for t in range(2):
                            ins = pe.transpose(PS[:, m % 4, t * P:(t + 1) * P], src_of(m, t), ident)
                        ins.then_inc(turned, 1)

                @block.vector
                def _(dve):
                    for m in range(n_tiles):
                        dve.wait_ge(turned, m + 1)
                        dst_of(dve, m, PS[:, m % 4, 0:T]).then_inc(copied, 1)
                    dve.wait_ge(copied, n_tiles)
                    dve.nop()

        def head_norm_steps(H, n_heads, dim, sq, st, factor=1.0):
            G = 2 * n_heads
            Hf = H.rearrange("p t h d -> p (t h) d")
            sqf = sq.rearrange("p (g d) -> p g d", g=G)
            return [("act", lambda e: nc.scalar.activation(sqf, Hf, ACT.Square)),
                    ("dve", lambda e: e.reduce_sum(st[:, 0:G], sqf, AX)),
                    ("dve", lambda e: e.tensor_scalar(st[:, 0:G], st[:, 0:G], 1.0 / dim, EPS, ALU.mult, ALU.add)),
                    ("act", lambda e: nc.scalar.activation(st[:, G:2 * G], st[:, 0:G], ACT.Sqrt)),
                    ("dve", lambda e: e.reciprocal(st[:, 0:G], st[:, G:2 * G])),
                    ("dve", lambda e: e.tensor_scalar(st[:, 0:G], st[:, 0:G], factor, None, ALU.mult)),
                    ("dve", lambda e: e.tensor_tensor(Hf, Hf, st[:, 0:G].unsqueeze(2).broadcast_to([P, G, dim]), ALU.mult))]

        st0 = rstd[:, 0:32]
        pointwise("mnorm", head_norm_steps(Hm, 8, 64, area(0, 1024), st0)
                  + sigmoid_steps(om, area(1024, 1024).rearrange("p (k t) -> p k t", k=4)))
        sig_o = area(1024, 1024).rearrange("p (k t) -> p k t", k=4)
        turn_heads("mturn", lambda m, t: Hm[:, t, 2 * m:2 * m + 2, :].rearrange("p h d -> p (h d)"),
                   lambda dve, m, ps: dve.scalar_tensor_tensor(out=mixT[:, m, :], in0=ps, scalar=sm("mnorm", m, 1),
                                                               in1=sig_o[:, m, :], op0=ALU.mult, op1=ALU.mult), 4)

        rope("rope0", [(dq[:, m, :], "rot_ax", "cos_ax", "sin_ax") for m in range(4)]
             + [(dk[:, m, C:], "rot_ax", "cos_ax", "sin_ax") for m in range(4)], 0)
        Hd = area(SCR, 1024).rearrange("p (t h d) -> p t h d", t=2, h=4)
        jobs = []
        for h in range(4):
            for t in range(2):
                sides = [slice(0, 64), slice(64, P)]
                jobs.append(dict(scores=[(dq[b, h, t * P:(t + 1) * P], dk[b, h, :]) for b in sides], groups=[(None, 0, 2, 512, None)],
                                 coef=(1, lam[:, 5:6]), minus=True, outs=[(0, [(0, [dv[:, s, h * P:(h + 1) * P] for s in range(4)])])],
                                 token_major=True, out=Hd[:, t, h, :]))
        attention("diff", jobs, 0.125, 0)
        pointwise("dnorm", head_norm_steps(Hd, 4, 128, area(0, 1024), st0, 1.0 - LAM_INIT))
        turn_heads("dturn", lambda m, t: Hd[:, t, m, :],
                   lambda dve, m, ps: dve.tensor_scalar(mixT[:, 4 + m, :], ps, sm("dnorm", m, 1), None, ALU.mult), 4)

        def out_proj(name, src, dst, bias=None):
            project(name, OUT_CH, [tile_task(m // 2, m % 2, src, "act",
                                             copy_to(dst[:, m, :]) if bias is None else copy_bias(dst[:, m, :], bias[:, m:m + 1]))
                                   for m in range(KT)])

        big = area(4096, KT * T).rearrange("p (k t) -> p k t", k=KT)
        out_proj("out0", mixT, big)
        residual("res0", big, sm("post0"), mpart(2))
        modulated("norm_f0", XT, UX, sm("fpre0"), mpart(3), mpart(4))
        ffn("ffn0", UX, (MOD_CH, cs[:, 0:8], sm("mod_b1"), mod1, 0, 8192))
        residual("res_f0", YT, sm("fpost0"), mpart(5))

        modulated("norm_c1", XT, UX, sm("pre1"), mpart(0, mod1), mpart(1, mod1))
        W = 31
        PADL = (W - 1) // 2
        TW = T + W - 1
        glu_a = area(0, 2048).rearrange("p (k t) -> p k t", k=KT)
        glu_g = area(2048, 2048).rearrange("p (k t) -> p k t", k=KT)
        hp = area(4096, KT * TW).rearrange("p (k t) -> p k t", k=KT)
        tasks = [tile_task(m // 2, m % 2, UX, "act", copy_bias((glu_a if m < 8 else glu_g)[:, m % 8, :], sm("pw1_b", m, 1)))
                 for m in range(16)]
        project("pw1", PW1_CH, tasks)
        pointwise("glu", sigmoid_steps(glu_g, glu_g) + [
            ("dve", lambda e: e.memset(hp, 0.0)),
            ("dve", lambda e: e.tensor_tensor(hp[:, :, PADL:PADL + T], glu_a, glu_g, ALU.mult))])
        dw = sm("dw_w").rearrange("p (k w) -> p k w", k=KT)
        ND = 4
        DG = area(6400, 8 * P).rearrange("p (b n) -> p b n", b=8)
        with Stage(nc, "dwconv", ["tap", "diag", "diag_used", "tile_done", "copied"]) as (
                block, (tap, diag, diag_used, tile_done, copied)):
            @block.vector
            def _(dve):
                n = 0
                for k0 in range(0, ND, 2):
                    for w in range(W):
                        for k in (k0, k0 + 1):
                            if w == 0:
                                ins = dve.tensor_scalar(YT[:, k, :], hp[:, k, 0:T], dw[:, k, 0:1], sm("dw_b", k, 1), ALU.mult, ALU.add)
                            else:
                                dve.wait_ge(tap, n - 1)
                                ins = dve.scalar_tensor_tensor(out=YT[:, k, :], in0=hp[:, k, w:w + T], scalar=dw[:, k, w:w + 1],
                                                               in1=YT[:, k, :], op0=ALU.mult, op1=ALU.add)
                            ins.then_inc(tap, 1)
                            n += 1

            @block.scalar
            def _(act):
                n = 0
                for k in range(ND, KT):
                    for w in range(W):
                        if n >= 8:
                            act.wait_ge(diag_used, n - 7)
                        nc.scalar.activation(DG[:, n % 8, :], ident, ACT.Copy, scale=dw[:, k, w:w + 1]).then_inc(diag, 1)
                        n += 1
                    if k > ND:
                        act.wait_ge(tile_done, k - ND)
                        nc.scalar.activation(YT[:, k - 1, :], PS[:, k - 1, 0:T], ACT.Identity, bias=sm("dw_b", k - 1, 1)).then_inc(copied, 1)
                act.wait_ge(tile_done, KT - ND)
                nc.scalar.activation(YT[:, KT - 1, :], PS[:, KT - 1, 0:T], ACT.Identity, bias=sm("dw_b", KT - 1, 1)).then_inc(copied, 1)

            @block.tensor
            def _(pe):
                n = 0
                for k in range(ND, KT):
                    for w in range(W):
                        pe.wait_ge(diag, n + 1)
                        pe.matmul(PS[:, k, 0:T], DG[:, n % 8, :], hp[:, k, w:w + T], start=(w == 0), stop=(w == W - 1)).then_inc(diag_used, 1)
                        n += 1
                    pe.matmul(PS[:, 0, 0:1], ident, ones[:, 0:1], start=True, stop=True).then_inc(tile_done, 1)

        norm("ln1", YT, lambda k: sm("ln_g", k, 1), plus_bias(YT, sm("ln_b")), center=True)
        pointwise("silu1", silu_steps(YT))
        out_proj("pw2", YT, big, sm("pw2_b"))
        residual("res1", big, sm("post1"), mpart(2, mod1))
        modulated("norm_m1", XT, UX, sm("fpre1"), mpart(3, mod1), mpart(4, mod1))

        H = area(0, FT * T).rearrange("p (k t) -> p k t", k=FT)
        EX = area(FT * T, 2 * T).rearrange("p (b t) -> p b t", b=2)
        UTM = area(6144, 2048).rearrange("p (t n) -> p t n", t=2)
        YTM = area(8192, 2048).rearrange("p (t n) -> p t n", t=2)
        UCT = area(10240, KT * CAP).rearrange("p (k c) -> p k c", k=KT)
        S1 = area(11136, 2 * CAP).rearrange("p (t c) -> p t c", t=2)
        SG = area(11360, 2 * CAP).rearrange("p (t c) -> p t c", t=2)
        PL = area(11584, T)
        YC = area(11840, D)
        rt = area(12864, 208)
        ACC = area(13072, 3 * 256).rearrange("p (z n) -> p z n", z=3)
        ro = sm("router").rearrange("p (k e) -> p k e", k=KT)

        def rv(i, n=16):
            return rt[:, i:i + n]
        steps = []
        for t in range(2):
            for kt in range(KT):
                steps.append(("pe!" if t + kt else "pe", lambda e, t=t, kt=kt: e.matmul(PS[:, 0, 8 * t:8 * t + 8], UX[:, kt, t * P:(t + 1) * P], ro[:, kt, :],
                                                                   start=(kt == 0), stop=(kt == KT - 1))))
        L = rv(0).rearrange("p (t e) -> p t e", t=2)
        EQ = rv(16).rearrange("p (t e) -> p t e", t=2)
        CU = rv(32).rearrange("p (t e) -> p t e", t=2)
        F1 = rv(48).rearrange("p (t e) -> p t e", t=2)
        F2 = rv(64).rearrange("p (t e) -> p t e", t=2)
        V1, V2, G1, G2 = rv(80, 2), rv(82, 2), rv(84, 2), rv(86, 2)

        def b8(v):
            return v.unsqueeze(2).broadcast_to([P, 2, 8])
        steps.append(("dve", lambda e: e.tensor_copy(rv(0), PS[:, 0, 0:16])))
        for Fx, Vx in ((F1, V1), (F2, V2)):
            steps += [("dve", lambda e, Vx=Vx: e.reduce_max(Vx, L, AX)),
                      ("dve", lambda e, Vx=Vx: e.tensor_tensor(EQ, L, b8(Vx), ALU.is_equal))]
            for t in range(2):
                steps.append(("dve", lambda e, t=t: e.tensor_tensor_scan(CU[:, t, :], ones[:, 0:8], EQ[:, t, :], 0.0, ALU.mult, ALU.add)))
            steps += [("dve", lambda e, Fx=Fx: e.scalar_tensor_tensor(out=Fx, in0=CU, scalar=1.0, in1=EQ, op0=ALU.is_equal, op1=ALU.mult)),
                      ("dve", lambda e, Fx=Fx: e.scalar_tensor_tensor(out=L, in0=Fx, scalar=NEG, in1=L, op0=ALU.mult, op1=ALU.add))]
        steps += [("dve", lambda e: e.tensor_tensor(G2, V2, V1, ALU.subtract)),
                  ("act", lambda e: nc.scalar.activation(G2, G2, ACT.Exp)),
                  ("dve", lambda e: e.tensor_scalar(G1, G2, 1.0, None, ALU.add)),
                  ("dve", lambda e: e.reciprocal(G1, G1)),
                  ("dve", lambda e: e.tensor_tensor(G2, G2, G1, ALU.mult)),
                  ("dve", lambda e: e.tensor_tensor(F1, F1, b8(G1), ALU.mult)),
                  ("dve", lambda e: e.tensor_tensor(F2, F2, b8(G2), ALU.mult)),
                  ("dve", lambda e: e.tensor_tensor(F1, F1, F2, ALU.add)),
                  ("dve", lambda e: e.memset(YT, 0.0))][:-1]
        MK = rt[:, 128:146].rearrange("p (t e) -> p t e", t=2)
        POS = rt[:, 146:164].rearrange("p (t e) -> p t e", t=2)
        GA = rt[:, 164:182].rearrange("p (t e) -> p t e", t=2)
        GC = rt[:, 182:200].rearrange("p (t e) -> p t e", t=2)
        FIT = rt[:, 200:208]
        steps.insert(-6, ("dve", lambda e: e.memset(rt[:, 128:200], 0.0)))
        steps.insert(-6, ("dve", lambda e: e.tensor_tensor(MK[:, :, 0:8], F1, F2, ALU.add)))
        steps.append(("dve", lambda e: e.tensor_copy(GA[:, :, 0:8], F1)))
        ncum_ = const("ncum").rearrange("p (k s) -> p k s", k=2)
        for t in range(2):
            for k in range(2):
                steps.append(("pe", lambda e, t=t, k=k: e.matmul(PS[:, 1, 8 * t:8 * t + 8], ncum_[:, k, t * P:(t + 1) * P],
                                                                 MK[:, k, 0:8], start=(k == 0), stop=(k == 1))))
        for k in range(2):
            steps.append(("pe", lambda e, k=k: e.matmul(PS[:, 2, 0:8], ones, MK[:, k, 0:8], start=(k == 0), stop=(k == 1))))
        steps += [("dve", lambda e: e.tensor_scalar(POS[:, :, 0:8], PS[:, 1, 0:16].rearrange("p (t e) -> p t e", t=2), -1.0, -1.0,
                                                    ALU.mult, ALU.add)),
                  ("dve", lambda e: e.tensor_scalar(full_flag[:, :], PS[:, 2, 0:8], float(CAP), None, ALU.is_gt)),
                  ("dve", lambda e: e.tensor_scalar(FIT, PS[:, 2, 0:8], float(CAP), None, ALU.is_le)),
                  ("dve", lambda e: e.tensor_tensor(GC[:, :, 0:8], GA[:, :, 0:8], FIT.unsqueeze(1).broadcast_to([P, 2, 8]), ALU.mult))]
        pointwise("router", steps)
        with Stage(nc, "uturn", ["turned", "copied"]) as (block, (turned, copied)):
            @block.tensor
            def _(pe):
                for j in range(4):
                    t, half = j // 2, j % 2
                    for k in range(4):
                        ins = pe.transpose(PS[:, j, k * P:(k + 1) * P], UX[:, 4 * half + k, t * P:(t + 1) * P], ident)
                    ins.then_inc(turned, 1)

            @block.scalar
            def _(act):
                for j in range(4):
                    act.wait_ge(turned, j + 1)
                    nc.scalar.activation(UTM[:, j // 2, (j % 2) * 512:(j % 2 + 1) * 512], PS[:, j, :], ACT.Copy)

            @block.vector
            def _(dve):
                dve.memset(YTM, 0.0)
        ws.clear()
        moe_base = ws.total
        W13 = FT
        USES = EXPERT_CH // RING

        with Stage(nc, "experts", ["built", "chunk_done", "silu_ready", "hidden", "place_turned", "gathered", "act_copied",
                                   "y_copied", "y_ready", "y_added", "acc_ready", "acc_chain"]) as (
                block, (built, chunk_done, silu_ready, hidden, place_turned, gathered, act_copied, y_copied, y_ready, y_added,
                        acc_ready, acc_chain)):
            @block.sync
            def _(sp):
                for k in range(RING):
                    sp.dma_start(ws.chunk(k), a["stream"][moe_base + k]).then_inc(landed[k], 16)

                def refill(e, k, source):
                    if k in EXPERT_SIDES:
                        sp.wait_ge(acc_ready, e * EXPERT_SIDE + EXPERT_SIDES.index(k) + 1)
                    else:
                        sp.wait_ge(chunk_done, e * FFN_CH + EXPERT_MAIN.index(k) + 1)
                    sp.dma_start(ws.chunk(k), source).then_inc(landed[k % RING], 16)

                with sp.Fori(0, NE - 1) as e:
                    for k in range(EXPERT_CH):
                        refill(e, k, a["stream"][e * EXPERT_CH + (moe_base + k + RING)])
                for k in range(EXPERT_CH - RING):
                    refill(NE - 1, k, a["stream"][moe_base + (NE - 1) * EXPERT_CH + k + RING])

            def here(eng, e, k):
                eng.wait_ge(landed[k % RING], e * (16 * USES) + 16 * (k // RING + 1))

            def main(k):
                return ws.chunk(EXPERT_MAIN[k])

            @block.tensor
            def _(pe):
                def gather(e):
                    for k in range(KT):
                        for t in range(2):
                            ins = pe.matmul(PS[:, 6 + k // 4, (k % 4) * CAP:(k % 4 + 1) * CAP], UTM[:, t, k * P:(k + 1) * P], S1[:, t, :],
                                            start=(t == 0), stop=(t == 1))
                    ins.then_inc(gathered, 1)

                def hidden_products(e, src, n):
                    for m in range(W13):
                        here(pe, e, EXPERT_MAIN[m])
                        if m >= 4:
                            pe.wait_ge(hidden, e * FT + m - 3)
                        else:
                            pe.wait_ge(y_added, e * 4)
                        w = main(m).rearrange("p (n k c) -> p n k c", n=2, k=KT)
                        for h in range(2):
                            for kt in range(KT):
                                ins = pe.matmul(PS[:, m % 4, h * T:h * T + n], w[:, h, kt, :], src[:, kt, 0:n],
                                                start=(kt == 0), stop=(kt == KT - 1))
                        ins.then_inc(chunk_done, 1)

                pe.wait_ge(built, 2)
                gather(0)
                with pe.Fori(0, NE) as e:
                    full = pe.value_load(full_flag[0:1, bass.ds(e, 1)], min_val=0, max_val=1)
                    pe.wait_ge(act_copied, e * 4 + 2)
                    with pe.If(full < 1):
                        hidden_products(e, UCT, CAP)
                    with pe.Else():
                        hidden_products(e, UX, T)
                    pe.wait_ge(built, e * 4 + 6)
                    pe.wait_ge(hidden, e * FT + FT - 3)
                    for t in range(2):
                        pe.transpose(PS[0:CAP, 2, t * P:(t + 1) * P], SG[:, t, :], ident)
                    pe.wait_ge(acc_ready, e * EXPERT_SIDE + EXPERT_SIDE)
                    for z in range(2 * EXPERT_SIDE):
                        ins = pe.matmul(PS[:, 2, T + z:T + z + 1], ACC[:, z // 2, (z % 2) * P:(z % 2 + 1) * P], ones[:, 0:1],
                                        start=True, stop=True)
                    ins.then_inc(place_turned, 1)
                    gather(e)
                    pe.wait_ge(act_copied, e * 4 + 6)
                    pe.wait_ge(hidden, e * FT + FT)
                    with pe.If(full < 1):
                        for q in range(FFN_CH - W13):
                            here(pe, e, EXPERT_MAIN[W13 + q])
                            for m in range(2):
                                for half in range(2):
                                    ins = pe.matmul(PS[0:CAP, 4 + half, :], H[:, 2 * q + m, 0:CAP],
                                                    main(W13 + q)[:, m * D + half * 512:m * D + (half + 1) * 512],
                                                    start=(q + m == 0), stop=(2 * q + m == FT - 1))
                            ins.then_inc(chunk_done, 1)
                        pe.wait_ge(y_copied, e * 2 + 2)
                        for j in range(4):
                            pe.matmul(PS[:, j, :], PL[0:CAP, (j // 2) * P:(j // 2 + 1) * P], YC[0:CAP, (j % 2) * 512:(j % 2 + 1) * 512],
                                      start=True, stop=True).then_inc(y_ready, 1)
                    with pe.Else():
                        for q in range(FFN_CH - W13):
                            here(pe, e, EXPERT_MAIN[W13 + q])
                            for m in range(2):
                                for j in range(4):
                                    ins = pe.matmul(PS[:, 4 + j, :], H[:, 2 * q + m, (j // 2) * P:(j // 2 + 1) * P],
                                                    main(W13 + q)[:, m * D + (j % 2) * 512:m * D + (j % 2 + 1) * 512],
                                                    start=(q + m == 0), stop=(2 * q + m == FT - 1))
                            ins.then_inc(chunk_done, 1)
                        for j in range(4):
                            ins = pe.matmul(PS[:, 0, 0:1], ident, ident[:, 0:1], start=True, stop=True)
                            ins.then_inc(y_ready, 1)
                    pe.nop()

            @block.scalar
            def _(act):
                def silus(e, n):
                    act.wait_ge(hidden, e * FT)
                    for m in range(FT):
                        act.wait_ge(chunk_done, e * FFN_CH + m + 1)
                        if m >= 2:
                            act.wait_ge(hidden, e * FT + m - 1)
                        nc.scalar.activation(EX[:, m % 2, 0:n], PS[:, m % 4, 0:n], ACT.Silu).then_inc(silu_ready, 1)

                def copy_gathered():
                    for b in range(2):
                        nc.scalar.activation(UCT[:, 4 * b:4 * b + 4, :], PS[:, 6 + b, 0:4 * CAP].rearrange("p (k c) -> p k c", k=4),
                                             ACT.Copy).then_inc(act_copied, 1)
                act.wait_ge(gathered, 1)
                copy_gathered()
                with act.Fori(0, NE) as e:
                    full = act.value_load(full_flag[0:1, bass.ds(e, 1)], min_val=0, max_val=1)
                    with act.If(full < 1):
                        silus(e, CAP)
                    with act.Else():
                        silus(e, T)
                    act.wait_ge(place_turned, e + 1)
                    nc.scalar.activation(PL[0:CAP, :], PS[0:CAP, 2, 0:T], ACT.Copy).then_inc(act_copied, 1)
                    nc.scalar.activation(adac[:, bass.ds(e * (2 * EXPERT_SIDE), 2 * EXPERT_SIDE)], PS[:, 2, T:T + 2 * EXPERT_SIDE],
                                         ACT.Copy).then_inc(act_copied, 1)
                    act.wait_ge(gathered, e + 2)
                    copy_gathered()
                    with act.If(full < 1):
                        act.wait_ge(chunk_done, e * FFN_CH + FFN_CH)
                        for b in range(2):
                            nc.scalar.activation(YC[0:CAP, b * 512:(b + 1) * 512], PS[0:CAP, 4 + b, :], ACT.Copy).then_inc(y_copied, 1)
                    with act.Else():
                        for b in range(2):
                            act.nop().then_inc(y_copied, 1)
                    act.nop()

            @block.vector
            def _(dve):
                def build(e, which):
                    dst, val = (S1, MK) if which == 0 else (SG, GC)
                    for t in range(2):
                        dve.tensor_scalar(dst[:, t, :], const("iota"), POS[:, t, bass.ds(e, 1)], val[:, t, bass.ds(e, 1)],
                                          ALU.is_equal, ALU.mult).then_inc(built, 1)

                def side(e, z):
                    here(dve, e, EXPERT_SIDES[z])
                    if z == 0:
                        dve.wait_ge(place_turned, e)
                    w = ws.chunk(EXPERT_SIDES[z]).rearrange("p (n k c) -> p n k c", n=2, k=KT)
                    o = ACC[:, z, :].rearrange("p (n c) -> p n c", n=2)
                    for kt in range(KT):
                        if kt == 0:
                            ins = dve.tensor_scalar(o, w[:, :, 0, :], sm("c2", 0, 1), None, ALU.mult)
                        else:
                            dve.wait_ge(acc_chain, (e * EXPERT_SIDE + z) * (KT - 1) + kt)
                            ins = dve.scalar_tensor_tensor(out=o, in0=w[:, :, kt, :], scalar=sm("c2", kt, 1), in1=o,
                                                           op0=ALU.mult, op1=ALU.add)
                        ins.then_inc(acc_chain if kt < KT - 1 else acc_ready, 1)

                def hiddens(e, n):
                    for m in range(FT):
                        x = EX[:, m % 2, 0:n]
                        dve.wait_ge(silu_ready, e * FT + m + 1)
                        dve.tensor_tensor(H[:, m, 0:n], PS[:, m % 4, T:T + n], x, ALU.mult).then_inc(hidden, 1)
                        if m in EXPERT_AFTER:
                            side(e, EXPERT_AFTER.index(m))

                build(0, 0)
                with dve.Fori(0, NE) as e:
                    full = dve.value_load(full_flag[0:1, bass.ds(e, 1)], min_val=0, max_val=1)
                    dve.wait_ge(gathered, e + 1)
                    build(e + 1, 0)
                    dve.wait_ge(place_turned, e)
                    build(e, 1)
                    with dve.If(full < 1):
                        hiddens(e, CAP)
                    with dve.Else():
                        hiddens(e, T)
                    with dve.If(full < 1):
                        for j in range(4):
                            dve.wait_ge(y_ready, e * 4 + j + 1)
                            y = YTM[:, j // 2, (j % 2) * 512:(j % 2 + 1) * 512]
                            dve.tensor_tensor(y, y, PS[:, j, :], ALU.add).then_inc(y_added, 1)
                    with dve.Else():
                        for j in range(4):
                            dve.wait_ge(y_ready, e * 4 + 4)
                            y = YTM[:, j // 2, (j % 2) * 512:(j % 2 + 1) * 512]
                            dve.scalar_tensor_tensor(out=y, in0=PS[:, 4 + j, :], scalar=GA[:, j // 2, bass.ds(e, 1)], in1=y,
                                                     op0=ALU.mult, op1=ALU.add).then_inc(y_added, 1)
                    dve.nop()
        ws.clear()
        turn_heads("yturn", lambda m, t: YTM[:, t, m * P:(m + 1) * P], lambda dve, m, ps: dve.tensor_copy(YT[:, m, :], ps), KT)
        residual("res_m1", YT, sm("fpost1"), mpart(5, mod1))

        q_dsa = area(0, 512).rearrange("p (k t) -> p k t", k=2)
        k_dsa = area(512, 256)
        q_idx = area(768, 512).rearrange("p (k t) -> p k t", k=2)
        k_idx = area(1280, 256)
        q_fox = area(1536, 768).rearrange("p (k t) -> p k t", k=3)
        k_fox = area(2304, 768).rearrange("p (k t) -> p k t", k=3)
        q_nsa = area(3072, 768).rearrange("p (k t) -> p k t", k=3)
        qr_nsa = area(3840, 768).rearrange("p (k t) -> p k t", k=3)
        kc_in = area(4608, 256)
        vc_in = area(4864, 256)
        k_slc = area(5120, 256)
        k_win = area(5376, 256)
        sgate = area(5632, 2048).rearrange("p (k t) -> p k t", k=KT)
        tokm = area(7680, 2 * 768).rearrange("p (t n) -> p t n", t=2)
        V_FOX, V_SLC, V_WIN, V_DSA, I_W, N_G, F_F = 0, 384, 512, 640, 704, 712, 730
        kcT = area(9216, 16)
        vcn = area(9232, 128)
        foxb = area(9360, 6 * 384).rearrange("p (h n) -> p h n", h=6)
        dsab = area(11664, 384)
        SCR2 = 12048
        with nc.Fori(0, LAYERS) as ly:
            with Stage(nc, "lload", ["loaded"]) as (block, (loaded,)):
                @block.sync
                def _(sp):
                    sp.dma_start(layer_small[:, :], a["layer_small"][ly]).then_inc(loaded, 16)
                    sp.wait_ge(loaded, 16)
                    sp.nop()
            ws.begin(moe_base + NE * EXPERT_CH + ly * L2_CH, L2_CH)

            def u_apply():
                st = [("dve", lambda e: e.tensor_tensor(mod[:, 0:24], adac[:, bass.ds(ly * 24, 24)], lsm("b_ada"), ALU.add)),
                      ("dve", lambda e: e.tensor_scalar(coef[:, 0:8], mod[:, 8:16], 1.0, None, ALU.add)),
                      ("dve", lambda e: e.tensor_scalar(coef[:, 8:16], mod[:, 16:24], 1.0, None, ALU.add))]
                for k in range(KT):
                    st.append(("dve!" if k else "dve", lambda e, k=k: e.tensor_scalar(UX[:, k, :], XT[:, k, :], coef[:, k:k + 1], mod[:, k:k + 1],
                                                                     ALU.mult, ALU.add)))
                return st
            pointwise("u2", u_apply())

            tiles = [q_dsa[:, 0, :], q_dsa[:, 1, :], k_dsa, q_idx[:, 0, :], q_idx[:, 1, :], k_idx,
                     q_fox[:, 0, :], q_fox[:, 1, :], q_fox[:, 2, :], k_fox[:, 0, :], k_fox[:, 1, :], k_fox[:, 2, :],
                     q_nsa[:, 0, :], q_nsa[:, 1, :], q_nsa[:, 2, :], kc_in, vc_in, k_slc, k_win] + \
                    [sgate[:, m, :] for m in range(KT)]
            tasks = [tile_task(m // 2, m % 2, UX, "act", copy_to(dst)) for m, dst in enumerate(tiles)]
            W2 = area(SCR2, 256)

            def keep_w2(bank, chunk):
                return [(bank[:, 0:256], ident, chunk[:, 8 * P:10 * P], True, True)]
            tasks.append((13, keep_w2, "act", copy_to(W2)))
            for c_ in range(3):
                for t in range(2):
                    tasks.append(token_task(14 + c_, UX, t * P, "act", copy_to(tokm[:, t, 256 * c_:256 * (c_ + 1)])))
            project("in2", IN2_CH, tasks)

            kb = area(SCR2 + 256, 2 * 480).rearrange("p (z l c) -> p z l c", z=2, l=32)
            hc = area(SCR2 + 1216, 32)
            fr = ws.used
            with Stage(nc, "compress", ["built", "wchunk", "summed", "done"]) as (
                    block, (built, wchunk, summed, done)):
                @block.sync
                def _(sp):
                    ws.load(sp, fr, CMP_CH, [(wchunk, k + 1) for k in range(CMP_CH)])

                @block.vector
                def _(dve):
                    for z, (src, pe_) in enumerate(((kc_in, "pe_k"), (vc_in, "pe_v"))):
                        for half in range(2):
                            tok = src[:, 16 * half:16 * half + 16 * NC].rearrange("p (c l) -> p l c", l=16)
                            pos = lsm(pe_, 16 * half, 16).unsqueeze(2).broadcast_to([P, 16, NC])
                            dve.tensor_tensor(kb[:, z, 16 * half:16 * half + 16, :], tok, pos, ALU.add).then_inc(built, 1)

                @block.scalar
                def _(act):
                    act.wait_ge(summed, 1)
                    nc.scalar.activation(hc[:, 0:2 * NC], PS[:, 0, 0:2 * NC], ACT.Silu).then_inc(done, 1)
                    act.wait_ge(summed, 2)
                    nc.scalar.activation(kcT[:, 0:NC], PS[:, 1, 0:NC], ACT.Copy)
                    nc.scalar.activation(vcn[0:NC, :], PS[0:NC, 2, 0:P], ACT.Copy)

                @block.tensor
                def _(pe):
                    for z in range(2):
                        pe.wait_ge(built, 2 * (z + 1))
                        for l in range(32):
                            k = 2 * z + l // 16
                            if l % 16 == 0:
                                ws.wait(pe, fr + k)
                            ins = pe.matmul(PS[:, 0, NC * z:NC * (z + 1)], ws.chunk(fr + k)[:, (l % 16) * P:(l % 16 + 1) * P],
                                            kb[:, z, l, :], start=(l == 0), stop=(l == 31))
                            if l % 16 == 15:
                                ins.then_inc(wchunk, 1)
                    ins = pe.transpose(PS[:, 3, 0:P], ident, ident)
                    ins.then_inc(summed, 1)
                    pe.wait_ge(done, 1)
                    pe.matmul(PS[:, 1, 0:NC], W2[:, 0:P], hc[:, 0:NC], start=True, stop=True)
                    pe.matmul(PS[0:NC, 2, 0:P], hc[:, NC:2 * NC], W2[:, P:2 * P], start=True, stop=True).then_inc(summed, 1)

            steps = [("dve", lambda e: e.tensor_copy(qr_nsa, q_nsa)),
                     ("dve", lambda e: e.tensor_scalar(tokm[:, :, I_W:I_W + 8], tokm[:, :, I_W:I_W + 8], 8.0 ** -0.5, None, ALU.mult))]
            ng = tokm[:, :, N_G:N_G + 18]
            steps += sigmoid_steps(ng, ng)
            ffg = tokm[:, :, F_F:F_F + 6]
            fb = lsm("b_f").unsqueeze(1).broadcast_to([P, 2, 6])
            s12 = area(SCR2, 12).rearrange("p (t n) -> p t n", t=2)
            s12b = area(SCR2 + 12, 12).rearrange("p (t n) -> p t n", t=2)
            steps.append(("dve", lambda e: e.tensor_tensor(ffg, ffg, fb, ALU.add)))
            steps += log_sigmoid_steps(ffg, s12, s12b)
            ncum = const("ncum").rearrange("p (k s) -> p k s", k=2)
            for h in range(6):
                for t in range(2):
                    steps.append(("pe" if h + t == 0 else "pe!", lambda e, h=h, t=t: e.matmul(PS[:, h, 0:T], ffg[:, t, h:h + 1].broadcast_to([P, P]), ncum[:, t, :],
                                                                     start=(t == 0), stop=(t == 1))))
            for h in range(6):
                steps.append(("dve!" if h else "dve", lambda e, h=h: e.tensor_tensor(foxb[:, h, 0:P], PS[:, h, 0:P], const("cmask")[:, 0:P], ALU.add)))
                steps.append(("dve!", lambda e, h=h: e.tensor_tensor(foxb[:, h, P:3 * P], PS[:, h, 0:T], const("cmask")[:, P:3 * P], ALU.add)))
            steps += silu_steps(sgate)
            pointwise("gates2", steps)
            rope("rope2", [(q_dsa[:, 0, :], "rot64", "cos64", "sin64"), (q_dsa[:, 1, :], "rot64", "cos64", "sin64"),
                           (k_dsa, "rot64", "cos64", "sin64"), (k_slc, "rot64", "cos64", "sin64"), (k_win, "rot64", "cos64", "sin64"),
                           (q_idx[:, 0, :], "rot32", "cos32", "sin32"), (q_idx[:, 1, :], "rot32", "cos32", "sin32"),
                           (k_idx, "rot32", "cos32", "sin32")]
                 + [(qr_nsa[:, m, :], "rot64", "cos64", "sin64") for m in range(3)], SCR2)

            isc = area(SCR2, 384)
            wk = area(SCR2 + 384, 2 * 256).rearrange("p (j n) -> p j n", j=2)
            m8 = area(SCR2 + 896, 8)
            rel = area(SCR2 + 1024, 4 * 256).rearrange("p (j n) -> p j n", j=4)
            SEL = -3.0e38
            LOW = -2.0e38
            with Stage(nc, "index", ["chain", "raw", "relu", "summed", "masked", "selected"]) as (
                    block, (chain, raw, relu, summed, masked, selected)):
                rows = [(0, 0, P), (1, P, 2 * P)]

                @block.tensor
                def _(pe):
                    j = 0
                    for t, at_, n_ in rows:
                        for h in range(8):
                            if j >= 4:
                                pe.wait_ge(relu, j - 3)
                            b0 = 32 * (h % 4)
                            pe.matmul(PS[:, j % 4, 0:n_], q_idx[b0:b0 + 32, h // 4, t * P:(t + 1) * P], k_idx[b0:b0 + 32, 0:n_],
                                      start=True, stop=True).then_inc(raw, 1)
                            j += 1

                @block.scalar
                def _(act):
                    j = 0
                    for t, at_, n_ in rows:
                        for h in range(8):
                            act.wait_ge(raw, j + 1)
                            if j >= 4:
                                act.wait_ge(summed, j - 3)
                            nc.scalar.activation(rel[:, j % 4, 0:n_], PS[:, j % 4, 0:n_], ACT.Relu).then_inc(relu, 1)
                            j += 1

                @block.vector
                def _(dve):
                    link = Chain(dve, chain)
                    j = 0
                    for t, at_, n_ in rows:
                        for h in range(8):
                            dve.wait_ge(relu, j + 1)
                            w = tokm[:, t, I_W + h:I_W + h + 1]
                            o = isc[:, at_:at_ + n_]
                            if h == 0:
                                ins = dve.tensor_scalar(o, rel[:, j % 4, 0:n_], w, None, ALU.mult)
                            else:
                                ins = dve.scalar_tensor_tensor(out=o, in0=rel[:, j % 4, 0:n_], scalar=w, in1=o, op0=ALU.mult, op1=ALU.add)
                            ins.then_inc(summed, 1)
                            j += 1
                            dve.wait_ge(summed, j)
                    for t, at_, n_ in rows:
                        dve.wait_ge(masked, t + 1)
                        cur = isc[:, at_:at_ + n_]
                        for r in range(TOPK // 8):
                            nxt = wk[:, r % 2, 0:n_]
                            link(dve.max(m8, cur))
                            link(dve.match_replace(nxt, m8, cur, SEL))
                            cur = nxt
                        link(dve.tensor_scalar(cur, cur, SEL, NEG, ALU.not_equal, ALU.mult))
                        dve.tensor_tensor(dsab[:, at_:at_ + n_], cur, const("cmask")[:, at_:at_ + n_], ALU.add).then_inc(selected, 1)
                        dve.wait_ge(selected, t + 1)
                    dve.nop()

                @block.gpsimd
                def _(pool):
                    for t, at_, n_ in rows:
                        pool.wait_ge(summed, 8 * (t + 1))
                        nc.gpsimd.affine_select(out=isc[:, at_:at_ + n_], in_=isc[:, at_:at_ + n_], compare_op=ALU.is_ge, fill=LOW,
                                                base=t * P, pattern=[[-1, n_]], channel_multiplier=1).then_inc(masked, 1)

            jobs = []

            def span(t):
                return slice(0, P) if t == 0 else slice(P, 3 * P)

            def keys(t):
                return slice(0, P * (t + 1))

            def vals(c0, t):
                return [tokm[:, s, c0:c0 + 64] for s in range(t + 1)]

            halves = [slice(0, 64), slice(64, P)]
            for m in range(2):
                for t in range(2):
                    jobs.append(dict(scores=[(q_dsa[b, m, t * P:(t + 1) * P], k_dsa[b, keys(t)]) for b in halves],
                                     groups=[(None, 0, 2, P * (t + 1), bc(dsab[:, span(t)], 2))], coef=None,
                                     outs=[(64 * z, [(z, vals(V_DSA, t))]) for z in range(2)],
                                     out=YT[:, m, t * P:(t + 1) * P]))
            for m in range(3):
                for t in range(2):
                    jobs.append(dict(scores=[(q_fox[b, m, t * P:(t + 1) * P], k_fox[b, m, keys(t)]) for b in halves],
                                     groups=[(None, 0, 2, P * (t + 1), foxb[:, 2 * m:2 * m + 2, span(t)])], coef=None,
                                     outs=[(64 * z, [(z, vals(V_FOX + 64 * (2 * m + z), t))]) for z in range(2)],
                                     out=YT[:, 2 + m, t * P:(t + 1) * P]))
            for h in range(6):
                g, j_ = h // 3, h % 3
                bq, bo = halves[g], 64 * (h % 2)
                for t in range(2):
                    q_, qr_ = (x[bq, j_, t * P:(t + 1) * P] for x in (q_nsa, qr_nsa))
                    jobs.append(dict(scores=[(q_, kcT[bq, 0:NC]), (qr_, k_slc[bq, keys(t)]), (qr_, k_win[bq, keys(t)])],
                                     groups=[(1, 0, 1, NC, const("cmpmask")[:, 16 * t:16 * t + NC]),
                                             (0, 1, 2, P * (t + 1), bc(const("cmask")[:, span(t)], 2))],
                                     coef=(0, tokm[:, t, N_G + h:N_G + 18:6]),
                                     outs=[(bo, [(1, vals(V_SLC + 64 * g, t)), (2, vals(V_WIN + 64 * g, t)),
                                                 (0, [vcn[0:NC, 64 * g:64 * g + 64]])])],
                                     out=YT[bo:bo + 64, 5 + h // 2, t * P:(t + 1) * P]))
            attention("attn2", jobs, 0.125, SCR2)
            pointwise("gate_mix", [("dve", lambda e: e.tensor_tensor(YT, YT, sgate, ALU.mult))])
            rs = area(4096, KT * T).rearrange("p (k t) -> p k t", k=KT)
            out_proj("out2", YT, rs)
            steps = []
            for k in range(KT):
                steps.append(("dve!" if k else "dve", lambda e, k=k: e.tensor_scalar(rs[:, k, :], rs[:, k, :], coef[:, 8 + k:9 + k], None, ALU.mult)))
            steps.append(("dve", lambda e: e.scalar_tensor_tensor(out=rs, in0=XT, scalar=ALPHA, in1=rs, op0=ALU.mult, op1=ALU.add)))
            pointwise("resid2", steps)
            norm("ln2", rs, lambda k: lsm("ln_g2", k, 1), plus_bias(XT, lsm("ln_b2")), center=True, eps=LN_EPS)
            ws.clear()

        with Stage(nc, "store", ["stored"]) as (block, (stored,)):
            @block.sync
            def _(sp):
                sp.dma_start(a["out"], XT).then_inc(stored, 16)
                sp.wait_ge(stored, 16)
                sp.nop()



def cols(v):
    v = np.asarray(v)
    return v.reshape(-1, P).T


def blocks(w):
    w = np.asarray(w)
    k, n = w.shape
    return w.reshape(k // P, P, n // P, P).transpose(2, 0, 1, 3)


def to_chunks(b):
    return b.reshape(-1, BLOCKS, P, P).transpose(0, 2, 1, 3).reshape(-1, P, CH)


def chunks(w):
    return to_chunks(blocks(w).reshape(-1, P, P))


def padded(w, n):
    out = np.zeros((w.shape[0], n), w.dtype)
    out[:, :w.shape[1]] = w
    return out


def ffn_chunks(w1, w3, w2):
    pair = np.stack([blocks(w1), blocks(w3)], 1)
    return [to_chunks(pair.reshape(-1, P, P)), chunks(w2)]


def expert_chunks(w1, w3, w2):
    pair = np.stack([blocks(w1), blocks(w3)], 1)
    return [to_chunks(pair.reshape(-1, P, P)), to_chunks(blocks(w2).transpose(1, 0, 2, 3).reshape(-1, P, P))]


def merged(main, side):
    at_main, at_side = interleave(len(main), len(side))
    out = np.empty((len(main) + len(side),) + main.shape[1:], main.dtype)
    out[at_main], out[at_side] = main, side
    return out


def two(w):
    out = np.zeros((P, P), w.dtype)
    out[0:64, 0:64] = w
    out[64:, 64:] = w
    return out


def layer_chunks(w_in, cmp_w1, cmp_w2, w_out):
    at, s = 0, {}
    for name, w in (("dsa_q", 256), ("dsa_k", 64), ("dsa_v", 64), ("idx_q", 256), ("idx_k", 32), ("idx_w", 8),
                    ("fox_q", 384), ("fox_k", 384), ("fox_v", 384), ("fox_f", 6), ("nsa_q", 384), ("kc", 128),
                    ("vc", 128), ("ks", 128), ("vs", 128), ("kw", 128), ("vw", 128), ("nsa_g", 18), ("gate", 1024)):
        s[name] = w_in[:, at:at + w]
        at += w
    q = s["nsa_q"].reshape(D, 2, 3, 64).transpose(0, 2, 1, 3).reshape(D, 384)
    feat = np.concatenate([s["dsa_q"], s["dsa_k"], s["dsa_k"], s["idx_q"]] + [s["idx_k"]] * 4 +
                          [s["fox_q"], s["fox_k"], q, s["kc"], s["vc"], s["ks"], s["kw"], s["gate"]], 1)
    tok = padded(np.concatenate([s["fox_v"], s["vs"], s["vw"], s["dsa_v"], s["idx_w"], s["nsa_g"], s["fox_f"]], 1), 768)
    small = np.zeros((8, P, P), w_in.dtype)
    small[0], small[1] = two(cmp_w2[0]), two(cmp_w2[1])
    inp = np.concatenate([blocks(feat).reshape(-1, P, P), small, blocks(tok).reshape(-1, P, P)], 0)
    w1 = np.stack([two(cmp_w1[z].reshape(32, 64, 64)[l]) for z in range(2) for l in range(32)], 0)
    return [to_chunks(inp), to_chunks(w1), chunks(w_out)]


def lay_out(i):
    i = {k: np.asarray(v) for k, v in i.items()}
    f = np.float32
    win = i["l0_w_in"]
    g0 = 4 * 512
    in0 = np.concatenate([win[:, :g0], padded(win[:, g0:g0 + 32], 256), win[:, g0 + 32:]], 1)
    m0 = chunks(i["l0_mod_w"])
    parts = [m0[:MOD_FIRST], merged(chunks(in0), m0[MOD_FIRST:]), chunks(i["l0_w_out"])]
    parts += [merged(np.concatenate(ffn_chunks(i["l0_ffn_w1"], i["l0_ffn_w3"], i["l0_ffn_w2"]), 0), chunks(i["l1_mod_w"]))]
    parts += [chunks(i["l1_conv_pw1_w"]), chunks(i["l1_conv_pw2_w"])]
    ada = np.concatenate([chunks(i["w_ada_2"][l]) for l in range(LAYERS)], 0)
    for e in range(NE):
        own = np.concatenate(expert_chunks(i["l1_moe_w1"][e], i["l1_moe_w3"][e], i["l1_moe_w2"][e]), 0)
        mixed = np.empty((EXPERT_CH,) + own.shape[1:], own.dtype)
        mixed[EXPERT_MAIN] = own
        mixed[EXPERT_SIDES] = ada[e * EXPERT_SIDE:(e + 1) * EXPERT_SIDE]
        parts.append(mixed)
    for l in range(LAYERS):
        parts += layer_chunks(i["w_in_2"][l], i["cmp_w1_2"][l], i["cmp_w2_2"][l], i["w_out_2"][l])
    stream = np.concatenate(parts, 0)

    def rows(m):
        out = np.zeros((P, m.shape[1]), m.dtype)
        out[:m.shape[0]] = m
        return out
    sm = {
        "c": cols(i["c"][0]), "c_ctx": cols(i["c_ctx"]), "mod_b0": cols(i["l0_mod_b"]), "pre0": cols(i["l0_mix_pre_g"]),
        "post0": cols(i["l0_mix_post_g"]), "gate_b": rows(i["l0_mlstm_gate_b"].reshape(4, 8).T),
        "conv_w": i["l0_mlstm_conv_w"].reshape(3, 8, P).transpose(2, 1, 0).reshape(P, 24),
        "mnorm": cols(i["l0_mlstm_norm_g"]),
        "lam": rows(np.stack([i["l0_lambda_q1"], i["l0_lambda_q2"], i["l0_lambda_k1"], i["l0_lambda_k2"]], 1)),
        "dnorm": cols(i["l0_diff_norm_g"]), "fpre0": cols(i["l0_ffn_pre_g"]), "fpost0": cols(i["l0_ffn_post_g"]),
        "mod_b1": cols(i["l1_mod_b"]), "pre1": cols(i["l1_mix_pre_g"]), "post1": cols(i["l1_mix_post_g"]),
        "pw1_b": cols(i["l1_conv_pw1_b"]), "dw_w": i["l1_conv_dw_w"].reshape(31, 8, P).transpose(2, 1, 0).reshape(P, 248),
        "dw_b": cols(i["l1_conv_dw_b"]), "ln_g": cols(i["l1_conv_ln_g"]), "ln_b": cols(i["l1_conv_ln_b"]),
        "pw2_b": cols(i["l1_conv_pw2_b"]), "fpre1": cols(i["l1_ffn_pre_g"]), "fpost1": cols(i["l1_ffn_post_g"]),
        "router": i["l1_router_w"].reshape(8, P, 8).transpose(1, 0, 2).reshape(P, 64), "c2": cols(i["c_2"][0]),
    }
    small = np.concatenate([sm[n] for n, _ in SMALL_W], 1).astype(f, copy=False)
    layer = []
    for l in range(LAYERS):
        pe = i["cmp_pe_2"][l]
        lm = {"b_ada": cols(i["b_ada_2"][l]), "pe_k": np.concatenate([pe[0].T] * 2, 0), "pe_v": np.concatenate([pe[1].T] * 2, 0),
              "ln_g2": cols(i["ln_g_2"][l]), "ln_b2": cols(i["ln_b_2"][l]), "b_f": np.stack([i["b_f_2"][l]] * P, 0)}
        layer.append(np.concatenate([lm[n] for n, _ in LAYER_W], 1))
    t = const_table()
    const = np.concatenate([t[n] for n, _ in CONST_W], 1).astype(f)

    def feature_major(x):
        return np.ascontiguousarray(x[0].T.reshape(KT, P, -1).transpose(1, 0, 2))
    return {"stream": stream, "small": np.ascontiguousarray(small), "layer_small": np.ascontiguousarray(np.stack(layer, 0)),
            "consts": const, "xT": feature_major(i["x"]), "ctxT": feature_major(i["ctx"])}


def kernel(**inputs):
    import concourse.bacc as _bacc
    from concourse.bass_utils import run_bass_kernel_spmd as _run

    arrays = lay_out(inputs)
    nc = _bacc.Bacc("TRN2", target_bir_lowering=False, num_devices=1)
    a = {n: nc.dram_tensor(n, v.shape, F32, kind="ExternalInput").ap() for n, v in arrays.items()}
    a["out"] = nc.dram_tensor("out", (P, KT, T), F32, kind="ExternalOutput").ap()
    build(nc, a)
    r = _run(nc, [arrays], core_ids=[0])
    y = r.results[0]["out"]
    return np.ascontiguousarray(y.transpose(1, 0, 2).reshape(D, T).T).reshape(1, T, D)
```

```python
from contextlib import ExitStack
import math

import numpy as np

import concourse.bass as bass
from concourse import mybir

F32 = mybir.dt.float32
ALU = mybir.AluOpType
ACT = mybir.ActivationFunctionType
AX = mybir.AxisListType.X

P = 128
D = 1024
KT = D // P
T = 256
C = 256
TT = T // P
FF = 2816
FT = FF // P
NE = 8
BLOCKS = 16
CH = BLOCKS * P
RING = 9
NEG = -1e30
FLOOR = -1e20
EPS = 1e-6
LN_EPS = 1e-5
ALPHA = (2.0 * 2) ** 0.25
LAM_INIT = 0.8 - 0.6 * math.exp(-0.3 * 0)
NC = 15
TOPK = 64
CAP = 112
LAYERS = 2

MOD_CH = 6 * D // P // 2
MOD_FIRST = 8
IN0_CH = 15
OUT_CH = KT * KT // BLOCKS
FFN_CH = 3 * KT * FT // BLOCKS
PW1_CH = 2 * OUT_CH
ADA_CH = 3 * D // P // 2
EXPERT_SIDE = LAYERS * ADA_CH // NE
EXPERT_CH = FFN_CH + EXPERT_SIDE
IN2_CH = 17
CMP_CH = 4
L2_CH = IN2_CH + CMP_CH + OUT_CH



def const_table():
    i = np.arange(P)
    r, c = i[:, None], i[None, :]
    t = {}
    t["ones"] = np.ones((P, P))
    t["ident"] = (r == c) * 1.0

    def rot(half, period):
        m = np.zeros((P, P))
        for o in range(P):
            k = o % period
            if k < half:
                m[o + half, o] = -1.0
            else:
                m[o - half, o] = 1.0
        return m

    t["rot_ax"] = rot(16, 32)
    t["rot64"] = rot(32, 64)
    t["rot32"] = rot(16, 32)
    tok = np.arange(T, dtype=np.float32)
    row, col = np.floor(tok / 64).astype(np.float32), (tok % 64).astype(np.float32)
    inv_ax = (np.float32(10000.0) ** (-np.arange(0, 32, 2, dtype=np.float32) / 32)).astype(np.float32)
    ang = np.zeros((P, T), np.float32)
    for o in range(P):
        ang[o] = (row if (o % 64) < 32 else col) * inv_ax[o % 16]
    t["cos_ax"], t["sin_ax"] = np.cos(ang), np.sin(ang)
    for name, half in (("64", 32), ("32", 16)):
        inv = (np.float32(10000.0) ** (-np.arange(half, dtype=np.float32) / half)).astype(np.float32)
        ang = inv[i % half][:, None] * tok[None, :]
        t["cos" + name], t["sin" + name] = np.cos(ang), np.sin(ang)
    s = np.arange(T)[None, :]
    t["ncum"] = np.concatenate([-1.0 * (r + P * k <= s) for k in range(TT)], 1)
    cd = np.where(c > r, NEG, 0.0)
    t["cmask"] = np.concatenate([cd, np.zeros((P, P)), cd], 1)
    t["fmask"] = np.concatenate([np.where(c < r, NEG, 0.0)] * 2, 1)
    t["bmask"] = np.concatenate([np.where(c > r, NEG, 0.0)] * 2, 1)
    cend = 16 * np.arange(16)[None, :] + 31
    t["cmpmask"] = np.concatenate([np.where((cend <= r + P * k) & (np.arange(16)[None, :] < NC), 0.0, NEG)
                                   for k in range(TT)], 1)
    t["iota"] = np.broadcast_to(np.arange(CAP)[None, :], (P, CAP))
    return t


def offsets(widths):
    at, out = 0, {}
    for n, w in widths:
        out[n] = (at, w)
        at += w
    return out, at


CONST_W = [("ones", P), ("ident", P), ("rot_ax", P), ("rot64", P), ("rot32", P), ("cos_ax", T), ("sin_ax", T),
           ("cos64", T), ("sin64", T), ("cos32", T), ("sin32", T), ("ncum", TT * T), ("cmask", 3 * P),
           ("fmask", T), ("bmask", T), ("cmpmask", TT * 16), ("iota", CAP)]
CONST_AT, CONST_N = offsets(CONST_W)

SMALL_W = [("c", 8), ("c_ctx", 8), ("mod_b0", 48), ("pre0", 8), ("post0", 8), ("gate_b", 4), ("conv_w", 24),
           ("mnorm", 4), ("lam", 4), ("dnorm", 4), ("fpre0", 8), ("fpost0", 8), ("mod_b1", 48), ("pre1", 8),
           ("post1", 8), ("pw1_b", 16), ("dw_w", 31 * 8), ("dw_b", 8), ("ln_g", 8), ("ln_b", 8), ("pw2_b", 8),
           ("fpre1", 8), ("fpost1", 8), ("router", 64), ("c2", 8)]
SMALL_AT, SMALL_N = offsets(SMALL_W)
LAYER_W = [("b_ada", 24), ("pe_k", 32), ("pe_v", 32), ("ln_g2", 8), ("ln_b2", 8), ("b_f", 6)]
LAYER_AT, LAYER_N = offsets(LAYER_W)



def interleave(n, m):
    main, side, at = [], [], 0
    for k in range(max(n, m)):
        if k < n:
            main.append(at)
            at += 1
        if k < m:
            side.append(at)
            at += 1
    return main, side


EXPERT_AFTER = [5, 11, 17]
EXPERT_MAIN = [k + sum(k > a for a in EXPERT_AFTER) for k in range(FFN_CH)]
EXPERT_SIDES = [a + 1 + z for z, a in enumerate(EXPERT_AFTER)]
assert sorted(EXPERT_MAIN + EXPERT_SIDES) == list(range(EXPERT_CH)) and EXPERT_CH % RING == 0


class Stream:

    def __init__(self, nc, ring, dram, sems):
        self.nc, self.ring, self.dram, self.landed = nc, ring, dram, sems
        self.used = self.issued = 0
        self.total = 0
        self.base = 0

    def begin(self, base, total):
        self.used = self.issued = 0
        self.total, self.base = total, base

    def chunk(self, g):
        return self.ring[:, (g % RING) * CH:(g % RING + 1) * CH]

    def wait(self, eng, g):
        eng.wait_ge(self.landed[g % RING], 16 * (g // RING + 1))

    def load(self, sp, first, n, freed):
        last = min(first + n + RING, self.total)
        for g in range(self.issued, last):
            old = g - RING
            if old >= first and old - first < n:
                sp.wait_ge(*freed[old - first])
            sp.dma_start(self.chunk(g), self.dram[self.base + g]).then_inc(self.landed[g % RING], 16)
        self.issued = max(self.issued, last)
        self.used = first + n

    def clear(self):
        for s in self.landed:
            self.nc.gpsimd.sem_clear(s)
        self.nc.all_engine_barrier()


class Stage:

    def __init__(self, nc, name, sems):
        self.nc, self.name, self.names = nc, name, sems

    def __enter__(self):
        self.stack = ExitStack()
        self.sems = {n: self.stack.enter_context(self.nc.semaphore(f"{self.name}_{n}")) for n in self.names}
        self.inner = ExitStack()
        self.block = self.inner.enter_context(self.nc.Block())
        return self.block, [self.sems[n] for n in self.names]

    def __exit__(self, *a):
        self.inner.close()
        for s in self.sems.values():
            self.nc.gpsimd.sem_clear(s)
        self.nc.all_engine_barrier()
        self.stack.close()


class Chain:

    def __init__(self, eng, sem):
        self.eng, self.sem, self.n = eng, sem, 0

    def __call__(self, ins):
        self.go(ins)
        self.sync()

    def go(self, ins):
        self.n += 1
        ins.then_inc(self.sem, 1)

    def sync(self):
        self.eng.wait_ge(self.sem, self.n)


def build(nc, a):
    ctx = ExitStack()
    with ctx:
        def sb(name, n):
            return ctx.enter_context(nc.sbuf_tensor("sb_" + name, [P, n], F32))

        ring = sb("ring", RING * CH)
        consts = sb("consts", CONST_N)
        small = sb("small", SMALL_N)
        all_small = sb("all_small", LAYERS * LAYER_N)
        layer_small = sb("layer_small", LAYER_N)
        XT = sb("XT", KT * T)[:, :].rearrange("p (k t) -> p k t", k=KT)
        U2 = sb("U2", KT * 2 * T)[:, :].rearrange("p (k t) -> p k t", k=KT)
        YT = sb("YT", KT * T)[:, :].rearrange("p (k t) -> p k t", k=KT)
        mod = sb("mod", 48)
        mod1 = sb("mod1", 48)
        modc = sb("modc", 16)
        adac = sb("adac", LAYERS * 24)
        coef = sb("coef", 16)
        cs = sb("cs", 24)
        rstd = sb("rstd", T)
        mean = sb("mean", T)
        lam = sb("lam", 8)
        arena = sb("arena", 18448)
        full_flag = ctx.enter_context(nc.sbuf_tensor("full_flag", [P, NE], mybir.dt.int32))
        PS = ctx.enter_context(nc.psum_tensor("PS", [P, 8, 512], F32))
        UX = U2[:, :, C:C + T]
        UC = U2[:, :, 0:C]

        def const(name):
            at, w = CONST_AT[name]
            return consts[:, at:at + w]

        def sm(name, i=0, n=None):
            at, w = SMALL_AT[name]
            return small[:, at + i:at + (w if n is None else i + n)]

        def lsm(name, i=0, n=None):
            at, w = LAYER_AT[name]
            return layer_small[:, at + i:at + (w if n is None else i + n)]

        ones, ident = const("ones"), const("ident")

        def area(at, n):
            return arena[:, at:at + n]

        landed = [ctx.enter_context(nc.semaphore(f"landed{i}")) for i in range(RING)]
        ws = Stream(nc, ring, a["stream"], landed)
        late = ctx.enter_context(nc.semaphore("late_inputs"))

        def bc(ap2, k):
            return ap2.unsqueeze(1).broadcast_to([ap2.shape[0], k, ap2.shape[1]])


        def first_modulation(name, n, vecs, bias, outs):
            acc = area(0, 2 * 512).rearrange("p (b v n) -> p b v n", b=2, v=2)
            first = ws.used
            sums, whole = (PS[:, b, 0:4 * n].rearrange("p (v j) -> p v j", v=2) for b in range(2))
            with Stage(nc, name, ["chain", "acc_ready", "acc_used", "whole_done", "done"]) as (
                    block, (chain, acc_ready, acc_used, whole_done, done)):
                @block.sync
                def _(sp):
                    ws.load(sp, first, n, [(whole_done if k % 2 else acc_ready, k // 2 + 1) for k in range(n)])
                    sp.wait_ge(late, 16 * 4)
                    sp.nop()

                @block.vector
                def _(dve):
                    link = Chain(dve, chain)
                    for k in range(0, n, 2):
                        ws.wait(dve, first + k)
                        if k >= 4:
                            dve.wait_ge(acc_used, k // 2 - 1)
                        w = ws.chunk(first + k).rearrange("p (n k c) -> p n k c", n=2, k=KT)
                        for kt in range(KT):
                            for v in range(2):
                                o = acc[:, k // 2 % 2, v, :].rearrange("p (n c) -> p n c", n=2)
                                if kt == 0:
                                    ins = dve.tensor_scalar(o, w[:, :, 0, :], vecs[:, v, 0:1], None, ALU.mult)
                                else:
                                    dve.wait_ge(chain, link.n - 1)
                                    ins = dve.scalar_tensor_tensor(out=o, in0=w[:, :, kt, :], scalar=vecs[:, v, kt:kt + 1], in1=o,
                                                                   op0=ALU.mult, op1=ALU.add)
                                if (kt, v) != (KT - 1, 1):
                                    link.go(ins)
                        link.sync()
                        ins.then_inc(acc_ready, 1)
                    dve.wait_ge(acc_used, n // 2)
                    dve.wait_ge(whole_done, n // 2)
                    for v in range(2):
                        for e, ps in enumerate((sums, whole)):
                            def odd(x):
                                return x.rearrange("p (q e h) -> p q e h", e=2, h=2)[:, :, e, :]
                            dve.tensor_tensor(odd(outs[v]), odd(ps[:, v, :]), odd(bias), ALU.add).then_inc(done, 1)

                @block.tensor
                def _(pe):
                    for k in range(n):
                        w = ws.chunk(first + k).rearrange("p (n k c) -> p n k c", n=2, k=KT)
                        if k % 2 == 0:
                            continue
                        ws.wait(pe, first + k)
                        for h in range(2):
                            for kt in range(KT):
                                ins = pe.matmul(whole[:, :, 2 * k + h], w[:, h, kt, :], vecs[:, :, kt], start=(kt == 0), stop=(kt == KT - 1))
                        ins.then_inc(whole_done, 1)
                        pe.wait_ge(acc_ready, k // 2 + 1)
                        for v in range(2):
                            for h in range(2):
                                ins = pe.matmul(sums[:, v, 2 * k - 2 + h:2 * k - 1 + h], acc[:, k // 2 % 2, v, h * P:(h + 1) * P],
                                                ones[:, 0:1], start=True, stop=True)
                        ins.then_inc(acc_used, 1)

        def norm(name, src, scale_of, finish, center=False, eps=EPS, prepare=None):
            sq = area(0, KT * T).rearrange("p (k t) -> p k t", k=KT)
            tmp = area(KT * T, KT * T).rearrange("p (k t) -> p k t", k=KT)
            with Stage(nc, name, ["chain", "sq_ready", "sum_ready", "centred", "var_ready", "std_ready", "scaled", "done"]) as (
                    block, (chain, sq_ready, sum_ready, centred, var_ready, std_ready, scaled, done)):
                def finishing(eng, who):
                    for k in range(KT):
                        if finish[0](k) == who:
                            eng.wait_ge(scaled, k + 1)
                            finish[1](eng, k, tmp[:, k, :]).then_inc(done, 1)

                @block.scalar
                def _(act):
                    for k in range(KT):
                        if center:
                            act.wait_ge(centred, k + 1)
                        nc.scalar.activation(sq[:, k, :], src[:, k, :], ACT.Square).then_inc(sq_ready, 1)
                    act.wait_ge(var_ready, 1)
                    nc.scalar.activation(rstd[:, :], rstd[:, :], ACT.Sqrt).then_inc(std_ready, 1)
                    finishing(act, "act")

                @block.tensor
                def _(pe):
                    if center:
                        for k in range(KT):
                            ins = pe.matmul(PS[:, 1, 0:T], ones, src[:, k, :], start=(k == 0), stop=(k == KT - 1))
                        ins.then_inc(sum_ready, 1)
                    for k in range(KT):
                        pe.wait_ge(sq_ready, k + 1)
                        ins = pe.matmul(PS[:, 0, 0:T], ones, sq[:, k, :], start=(k == 0), stop=(k == KT - 1))
                    ins.then_inc(sum_ready, 1)

                @block.gpsimd
                def _(pool):
                    finishing(pool, "pool")

                @block.vector
                def _(dve):
                    link = Chain(dve, chain)
                    if prepare:
                        prepare(dve, link)
                    if center:
                        dve.wait_ge(sum_ready, 1)
                        link(dve.tensor_scalar(mean[:, :], PS[:, 1, 0:T], 1.0 / D, None, ALU.mult))
                        for k in range(KT):
                            dve.tensor_tensor(src[:, k, :], src[:, k, :], mean[:, :], ALU.subtract).then_inc(centred, 1)
                    dve.wait_ge(sum_ready, 2 if center else 1)
                    dve.tensor_scalar(rstd[:, :], PS[:, 0, 0:T], 1.0 / D, eps, ALU.mult, ALU.add).then_inc(var_ready, 1)
                    dve.wait_ge(std_ready, 1)
                    link(dve.reciprocal(rstd[:, :], rstd[:, :]))
                    if center:
                        dve.wait_ge(centred, KT)
                    for k in range(KT):
                        dve.scalar_tensor_tensor(out=tmp[:, k, :], in0=src[:, k, :], scalar=scale_of(k), in1=rstd[:, :],
                                                 op0=ALU.mult, op1=ALU.mult).then_inc(scaled, 1)
                    finishing(dve, "dve")

        def plus_bias(dst, b, func=ACT.Identity):
            return (lambda k: "act",
                    lambda act, k, tmp: nc.scalar.activation(dst[:, k, :], tmp, func, bias=b[:, k:k + 1]))

        def modulated(name, src, dst, g, shift, scale):
            norm(name, src, lambda k: coef[:, k:k + 1], plus_bias(dst, shift),
                 prepare=lambda dve, link: link(dve.scalar_tensor_tensor(out=coef[:, 0:KT], in0=scale, scalar=1.0, in1=g,
                                                                         op0=ALU.add, op1=ALU.mult)))

        def residual(name, src, g, gate):
            norm(name, src, lambda k: coef[:, k:k + 1],
                 (lambda k: "pool" if k < 4 else "dve",
                  lambda eng, k, tmp: eng.tensor_tensor(XT[:, k, :], XT[:, k, :], tmp, ALU.add)),
                 prepare=lambda dve, link: link(dve.tensor_tensor(coef[:, 0:KT], gate, g, ALU.mult)))

        class Side:

            def __init__(self, places, vec, bias, out, col, acc_at):
                self.places, self.vec, self.bias, self.out, self.col = places, vec, bias, out, col
                self.acc = area(acc_at, 512).rearrange("p (b n) -> p b n", b=2)

            def sum_rows(self, dve, link, z, acc_ready, acc_used):
                ws.wait(dve, self.places[z])
                if z >= 2:
                    dve.wait_ge(acc_used, z - 1)
                w = ws.chunk(self.places[z]).rearrange("p (n k c) -> p n k c", n=2, k=KT)
                o = self.acc[:, z % 2, :].rearrange("p (n c) -> p n c", n=2)
                link(dve.tensor_scalar(o, w[:, :, 0, :], self.vec[:, 0:1], None, ALU.mult))
                for kt in range(1, KT):
                    ins = dve.scalar_tensor_tensor(out=o, in0=w[:, :, kt, :], scalar=self.vec[:, kt:kt + 1], in1=o,
                                                   op0=ALU.mult, op1=ALU.add)
                    if kt < KT - 1:
                        link(ins)
                ins.then_inc(acc_ready, 1)

            def sum_partitions(self, pe, z, acc_ready, acc_used):
                pe.wait_ge(acc_ready, z + 1)
                for h in range(2):
                    ins = pe.matmul(PS[:, 7, 2 * z + h:2 * z + h + 1], self.acc[:, z % 2, h * P:(h + 1) * P], ones[:, 0:1],
                                    start=True, stop=True)
                ins.then_inc(acc_used, 1)

            def finish(self, dve, acc_used):
                n = len(self.places)
                dve.wait_ge(acc_used, n)
                c = self.col
                return dve.tensor_tensor(self.out[:, c:c + 2 * n], PS[:, 7, 0:2 * n], self.bias[:, c:c + 2 * n], ALU.add)

        class Task:

            def __init__(self, chunk, matmuls, engine, evacuate, needs=(), serial=False):
                self.chunk, self.matmuls, self.engine, self.evacuate = chunk, matmuls, engine, evacuate
                self.needs, self.serial, self.count = needs, serial, None

        def project(name, n, tasks, side=None):
            first = ws.used
            nb = 7 if side else 8
            n_side = side[0] if side else 0
            main, places = interleave(n, n_side)
            sd = Side([first + p for p in places], *side[1:]) if side else None
            count = {"act": 0, "dve": 0}
            fills, last = [], {}
            for t in tasks:
                count[t.engine] += 1
                t.count = count[t.engine]
                if t.matmuls:
                    fills.append(t)
                    t.fill = len(fills)
                    if t.chunk is not None:
                        last[t.chunk] = len(fills)
            with Stage(nc, name, ["chain_d", "chain_a", "bank_full", "act_done", "dve_done", "acc_ready", "acc_used", "side_done"]) as (
                    block, (chain_d, chain_a, bank_full, act_done, dve_done, acc_ready, acc_used, side_done)):
                by = {"act": act_done, "dve": dve_done}

                def wait_done(eng, t):
                    eng.wait_ge(by[t.engine], t.count)

                @block.sync
                def _(sp):
                    freed = {main[k]: (bank_full, last[k]) for k in range(n)}
                    freed.update({p: (acc_ready, z + 1) for z, p in enumerate(places)})
                    ws.load(sp, first, n + n_side, [freed[p] for p in range(n + n_side)])

                @block.tensor
                def _(pe):
                    z = 0
                    for j, t in enumerate(fills):
                        if t.chunk is not None:
                            ws.wait(pe, first + main[t.chunk])
                        for need in t.needs:
                            wait_done(pe, need)
                        if j >= nb:
                            wait_done(pe, fills[j - nb])
                        chunk = None if t.chunk is None else ws.chunk(first + main[t.chunk])
                        for o, l, r, s, e in t.matmuls(PS[:, j % nb, :], chunk):
                            ins = pe.matmul(o, l, r, start=s, stop=e)
                        ins.then_inc(bank_full, 1)
                        k = t.chunk
                        if k is not None and last[k] == j + 1 and z < k and z < n_side:
                            sd.sum_partitions(pe, z, acc_ready, acc_used)
                            z += 1
                    for z in range(z, n_side):
                        sd.sum_partitions(pe, z, acc_ready, acc_used)

                def evacuate(eng, who, link):
                    z = 0
                    for t in tasks:
                        if t.engine == who:
                            if t.serial and t.count > 1:
                                eng.wait_ge(by[who], t.count - 1)
                            if t.matmuls:
                                eng.wait_ge(bank_full, t.fill)
                                t.evacuate(eng, PS[:, (t.fill - 1) % nb, :], link).then_inc(by[who], 1)
                            else:
                                for need in t.needs:
                                    wait_done(eng, need)
                                t.evacuate(eng, None, link).then_inc(by[who], 1)
                        if who == "dve" and t.matmuls and t.chunk is not None and last[t.chunk] == t.fill and z < n_side:
                            sd.sum_rows(eng, link, z, acc_ready, acc_used)
                            z += 1
                    if who == "dve" and n_side:
                        for z in range(z, n_side):
                            sd.sum_rows(eng, link, z, acc_ready, acc_used)
                        sd.finish(eng, acc_used).then_inc(side_done, 1)

                @block.scalar
                def _(act):
                    evacuate(act, "act", Chain(act, chain_a))

                @block.vector
                def _(dve):
                    evacuate(dve, "dve", Chain(dve, chain_d))

        def tile_task(k, h, rhs, engine, evacuate, ncols=P, c0=0):
            def matmuls(bank, chunk):
                w = chunk.rearrange("p (n k c) -> p n k c", n=2, k=KT)
                N = rhs.shape[2]
                return [(bank[0:ncols, 0:N], w[:, h, kt, c0:c0 + ncols], rhs[:, kt, :], kt == 0, kt == KT - 1)
                        for kt in range(KT)]
            return Task(k, matmuls, engine, evacuate)

        def token_task(k, lhs, t0, engine, evacuate):
            def matmuls(bank, chunk):
                w = chunk.rearrange("p (n k c) -> p n k c", n=2, k=KT)
                o = bank[:, 0:2 * P].rearrange("p (n c) -> p n c", n=2)
                return [(o, lhs[:, kt, t0:t0 + P], w[:, :, kt, :], kt == 0, kt == KT - 1) for kt in range(KT)]
            return Task(k, matmuls, engine, evacuate)

        def copy_to(dst, n=None, scale=1.0):
            def f(act, bank, link):
                o = dst
                src = bank[0:dst.shape[0], 0:dst.shape[1]] if len(dst.shape) == 2 else \
                    bank[:, 0:dst.shape[1] * dst.shape[2]].rearrange("p (a b) -> p a b", a=dst.shape[1])
                return nc.scalar.activation(o, src, ACT.Copy, scale=scale)
            return f

        def copy_bias(dst, b):
            def f(act, bank, link):
                return nc.scalar.activation(dst, bank[:, 0:dst.shape[1]], ACT.Identity, bias=b)
            return f

        def pointwise(name, steps, prefetch=False):
            with Stage(nc, name, ["step_done"]) as (block, (step_done,)):
                def run(eng, who):
                    for i, (w, f) in enumerate(steps):
                        if w.rstrip("!") == who:
                            assert w == who or steps[i - 1][0].rstrip("!") == who
                            if i and w == who:
                                eng.wait_ge(step_done, i)
                            f(eng).then_inc(step_done, 1)
                    eng.nop()

                if prefetch:
                    @block.sync
                    def _(sp):
                        ws.load(sp, ws.used, 0, [])

                @block.scalar
                def _(act):
                    run(act, "act")

                @block.vector
                def _(dve):
                    run(dve, "dve")

                @block.tensor
                def _(pe):
                    run(pe, "pe")

                @block.gpsimd
                def _(pool):
                    run(pool, "pool")

        def log_sigmoid_steps(z, t1, t2):
            return [("dve", lambda e: e.scalar_tensor_tensor(out=t1, in0=z, scalar=-1.0, in1=z, op0=ALU.mult, op1=ALU.max)),
                    ("act", lambda e: nc.scalar.activation(t1, t1, ACT.Exp, scale=-1.0)),
                    ("dve", lambda e: e.tensor_scalar(t1, t1, 1.0, None, ALU.add)),
                    ("act", lambda e: nc.scalar.activation(t2, t1, ACT.Ln)),
                    ("dve", lambda e: e.scalar_tensor_tensor(out=z, in0=z, scalar=0.0, in1=t2, op0=ALU.min, op1=ALU.subtract))]

        def rope_task(x, dst, tmp, rot, cos, sin, need):
            def f(dve, bank, link):
                link.go(dve.tensor_tensor(tmp[:, 0, :], bank[:, 0:T], const(sin), ALU.mult))
                link(dve.tensor_tensor(tmp[:, 1, :], x, const(cos), ALU.mult))
                return dve.tensor_tensor(dst, tmp[:, 0, :], tmp[:, 1, :], ALU.add)
            return Task(None, lambda bank, chunk: [(bank[:, 0:T], const(rot), x, True, True)], "dve", f, (need,), serial=True)

        def ffn(name, src, side):
            H = area(0, FT * T).rearrange("p (k t) -> p k t", k=FT)
            EX = area(FT * T, 2 * T).rearrange("p (b t) -> p b t", b=2)
            first = ws.used
            n2 = KT * FT // BLOCKS
            n_side = side[0]
            main, places = interleave(FFN_CH, n_side)
            sd = Side([first + p for p in places], *side[1:])
            with Stage(nc, name, ["chain", "pair_ready", "silu_ready", "hidden_done", "w2_chunk", "y_ready", "y_done",
                                  "acc_ready", "acc_used", "side_done"]) as (
                    block, (chain, pair_ready, silu_ready, hidden_done, w2_chunk, y_ready, y_done, acc_ready, acc_used, side_done)):
                @block.sync
                def _(sp):
                    own = [(pair_ready, m + 1) for m in range(FT)] + [(w2_chunk, q + 1) for q in range(n2 - 1)] + [(y_ready, KT)]
                    freed = dict(zip(main, own))
                    freed.update({p: (acc_ready, z + 1) for z, p in enumerate(places)})
                    ws.load(sp, first, FFN_CH + n_side, [freed[p] for p in range(FFN_CH + n_side)])

                @block.tensor
                def _(pe):
                    for m in range(FT):
                        ws.wait(pe, first + main[m])
                        if m >= 4:
                            pe.wait_ge(hidden_done, m - 3)
                        w = ws.chunk(first + main[m]).rearrange("p (n k c) -> p n k c", n=2, k=KT)
                        for h in range(2):
                            for kt in range(KT):
                                ins = pe.matmul(PS[:, m % 4, h * T:(h + 1) * T], w[:, h, kt, :], src[:, kt, :],
                                                start=(kt == 0), stop=(kt == KT - 1))
                        ins.then_inc(pair_ready, 1)
                        if m >= 1:
                            sd.sum_partitions(pe, m - 1, acc_ready, acc_used)
                    b = 0
                    for o in range(KT):
                        if o >= 3:
                            pe.wait_ge(y_done, o - 2)
                        for m in range(FT):
                            if b % BLOCKS == 0:
                                ws.wait(pe, first + main[FT + b // BLOCKS])
                            if o == 0:
                                pe.wait_ge(hidden_done, m + 1)
                            w = ws.chunk(first + main[FT + b // BLOCKS])
                            ins = pe.matmul(PS[:, 4 + o % 3, 0:T], w[:, (b % BLOCKS) * P:(b % BLOCKS + 1) * P], H[:, m, :],
                                            start=(m == 0), stop=(m == FT - 1))
                            if m == FT - 1:
                                ins.then_inc(y_ready, 1)
                            elif b % BLOCKS == BLOCKS - 1:
                                ins.then_inc(w2_chunk, 1)
                            b += 1
                        if o == 0:
                            for z in range(FT - 1, n_side):
                                sd.sum_partitions(pe, z, acc_ready, acc_used)

                @block.scalar
                def _(act):
                    for m in range(FT):
                        act.wait_ge(pair_ready, m + 1)
                        if m >= 2:
                            act.wait_ge(hidden_done, m - 1)
                        nc.scalar.activation(EX[:, m % 2, :], PS[:, m % 4, 0:T], ACT.Silu).then_inc(silu_ready, 1)
                    for o in range(KT):
                        act.wait_ge(y_ready, o + 1)
                        nc.scalar.activation(YT[:, o, :], PS[:, 4 + o % 3, 0:T], ACT.Copy).then_inc(y_done, 1)

                @block.vector
                def _(dve):
                    link = Chain(dve, chain)
                    for m in range(FT):
                        e = EX[:, m % 2, :]
                        dve.wait_ge(silu_ready, m + 1)
                        dve.tensor_tensor(H[:, m, :], PS[:, m % 4, T:2 * T], e, ALU.mult).then_inc(hidden_done, 1)
                        sd.sum_rows(dve, link, m, acc_ready, acc_used)
                    for z in range(FT, n_side):
                        sd.sum_rows(dve, link, z, acc_ready, acc_used)
                    sd.finish(dve, acc_used).then_inc(side_done, 1)

        def attention(name, jobs, scale, at):
            SB = area(at, 2 * 1024).rearrange("p (j b n) -> p j b n", j=2, b=2)
            PB = area(at + 2048, 3 * 1024).rearrange("p (j b n) -> p j b n", j=3, b=2)
            PT = area(at + 5120, 2 * 640).rearrange("p (j n) -> p j n", j=2)
            ST = mean[:, 0:48].rearrange("p (j n) -> p j n", j=3)
            n = len(jobs)
            cum = [sum(len(j["scores"]) for j in jobs[:i + 1]) for i in range(n)]

            def branch(buf, job, bi):
                for bank, b0, c, w, _ in job["groups"]:
                    if b0 <= bi < b0 + c:
                        return buf[:, bi, 0:w] if bank is None else buf[:, bank, 256 * (bi - b0):256 * (bi - b0) + w]

            def group(buf, g):
                bank, b0, c, w, _ = g
                if bank is None:
                    return buf[:, :, 0:w]
                return buf[:, bank, 0:w] if c == 1 else buf[:, bank, :].rearrange("p (c n) -> p c n", c=c)[:, :, 0:w]

            def scores_ps(i):
                return PS[:, 2 * (i % 2):2 * (i % 2) + 2, :]

            def pieces(job):
                out = []
                for base, brs in job["outs"]:
                    for bi, vs in brs:
                        for z, v in enumerate(vs):
                            out.append((base, bi, z * P, v.shape[0], v, len(out) * P))
                return out

            def turned_ps(q, at_):
                return PS[:, 4 + q % 2, at_:at_ + P] if at_ < 512 else PS[:, 6 + q % 2, 256:256 + P]

            def out_ps(q):
                o, base = jobs[q]["out"], jobs[q]["outs"][0][0]
                return PS[base:base + o.shape[0], 6 + q % 2, 0:o.shape[1]]

            with Stage(nc, name, ["chain", "scores", "negmax", "exps", "probs", "turned", "turned_copied", "out_ready", "out_done"]) as (
                    block, (chain, scores, negmax, exps, probs, turned, copied, out_ready, out_done)):
                @block.tensor
                def _(pe):
                    for i in range(n + 3):
                        if i < n:
                            job = jobs[i]
                            if i >= 2 and jobs[i - 2]["groups"][0][4] is None:
                                pe.wait_ge(exps, cum[i - 2])
                            elif i >= 2:
                                pe.wait_ge(negmax, i - 1)
                            for bi, (q_, k_) in enumerate(job["scores"]):
                                ins = pe.matmul(branch(scores_ps(i), job, bi), q_, k_, start=True, stop=True)
                            ins.then_inc(scores, 1)
                        q = i - 2
                        if 0 <= q < n:
                            pe.wait_ge(probs, q + 1)
                            if q >= 2:
                                pe.wait_ge(copied, q - 1)
                                if len(pieces(jobs[q])) > 4:
                                    pe.wait_ge(out_done, q - 1)
                            for _b, bi, k0, rows, _v, at_ in pieces(jobs[q]):
                                src = branch(PB[:, q % 3], jobs[q], bi)[:, k0:k0 + rows]
                                ins = pe.transpose(turned_ps(q, at_)[0:rows, :], src, ident)
                            ins.then_inc(turned, 1)
                        q = i - 3
                        if 0 <= q < n:
                            pe.wait_ge(copied, q + 1)
                            if q >= 2:
                                pe.wait_ge(out_done, q - 1)
                            ps = pieces(jobs[q])
                            for z, (base, bi, k0, rows, v, at_) in enumerate(ps):
                                p_ = PT[0:rows, q % 2, at_:at_ + P]
                                if jobs[q].get("token_major"):
                                    o, l, r = PS[:, 6 + q % 2, 0:v.shape[1]], p_, v
                                else:
                                    o, l, r = PS[base:base + v.shape[1], 6 + q % 2, 0:P], v, p_
                                ins = pe.matmul(o, l, r, start=(z == 0 or ps[z - 1][0] != base),
                                                stop=(z == len(ps) - 1 or ps[z + 1][0] != base))
                            ins.then_inc(out_ready, 1)

                @block.vector
                def _(dve):
                    link = Chain(dve, chain)
                    for i in range(n + 3):
                        job, q = (jobs[i] if i < n else None), i - 1 if i <= n else -1
                        S_, R_ = ST[:, i % 3, :], ST[:, q % 3, :]
                        if job:
                            dve.wait_ge(scores, i + 1)
                            for g in job["groups"]:
                                if g[4] is not None:
                                    if i >= 2:
                                        dve.wait_ge(exps, cum[i - 2])
                                    link.go(dve.scalar_tensor_tensor(out=group(SB[:, i % 2], g), in0=group(scores_ps(i), g), scalar=scale,
                                                                     in1=g[4], op0=ALU.mult, op1=ALU.add))
                        if q >= 0:
                            dve.wait_ge(exps, cum[q])
                            nb = len(jobs[q]["scores"])
                            link.go(dve.tensor_scalar(R_[:, 8:8 + nb], R_[:, 8:8 + nb], 1e-30, None, ALU.max))
                        link.sync()
                        if job:
                            for g in job["groups"]:
                                src = scores_ps(i) if g[4] is None else SB[:, i % 2]
                                link.go(dve.reduce_max(S_[:, g[1]:g[1] + g[2]], group(src, g), AX))
                        if q >= 0:
                            link.go(dve.reciprocal(R_[:, 12:12 + nb], R_[:, 8:8 + nb]))
                        link.sync()
                        if job:
                            c = len(job["scores"])
                            f = -scale if job["groups"][0][4] is None else -1.0
                            dve.tensor_scalar(S_[:, 4:4 + c], S_[:, 0:c], FLOOR, f, ALU.max, ALU.mult).then_inc(negmax, 1)
                        if q >= 0:
                            if jobs[q]["coef"] is not None:
                                b0, cf = jobs[q]["coef"]
                                link(dve.tensor_tensor(R_[:, 12 + b0:12 + nb], R_[:, 12 + b0:12 + nb], cf, ALU.mult))
                            for bi in range(nb):
                                r_, p_ = R_[:, 12 + bi:13 + bi], branch(PB[:, q % 3], jobs[q], bi)
                                if bi and jobs[q].get("minus"):
                                    link.sync()
                                    o_ = branch(PB[:, q % 3], jobs[q], 0)
                                    ins = dve.scalar_tensor_tensor(out=o_, in0=p_, scalar=r_, in1=o_, op0=ALU.mult, op1=ALU.add)
                                else:
                                    ins = dve.tensor_scalar(p_, p_, r_, None, ALU.mult)
                                if bi < nb - 1:
                                    link.go(ins)
                            link.sync()
                            ins.then_inc(probs, 1)
                        q = i - 3
                        if q >= 0 and jobs[q].get("gate") is not None:
                            dve.wait_ge(out_ready, q + 1)
                            dve.tensor_tensor(jobs[q]["out"], out_ps(q), jobs[q]["gate"], ALU.mult).then_inc(out_done, 1)

                @block.scalar
                def _(act):
                    for i in range(n + 3):
                        if i < n:
                            job = jobs[i]
                            act.wait_ge(negmax, i + 1)
                            if i >= 3:
                                act.wait_ge(turned, i - 2)
                            for bi in range(len(job["scores"])):
                                biased = job["groups"][0][4] is not None
                                s = branch(SB[:, i % 2] if biased else scores_ps(i), job, bi)
                                nc.scalar.activation(branch(PB[:, i % 3], job, bi), s, ACT.Exp, bias=ST[:, i % 3, 4 + bi:5 + bi],
                                                     scale=1.0 if biased else scale,
                                                     accum_out=ST[:, i % 3, 8 + bi:9 + bi]).then_inc(exps, 1)
                        q = i - 2
                        if 0 <= q < n:
                            act.wait_ge(turned, q + 1)
                            if q >= 2:
                                act.wait_ge(out_ready, q - 1)
                            ps = pieces(jobs[q])
                            z = 0
                            while z < len(ps):
                                e = z + 1
                                while e < min(len(ps), 4) and ps[e][3] == ps[z][3] and z < 4:
                                    e += 1
                                w_ = P * (e - z)
                                rows, at_ = ps[z][3], ps[z][5]
                                src = PS[0:rows, 4 + q % 2, at_:at_ + w_] if at_ < 512 else turned_ps(q, at_)[0:rows, :]
                                ins = nc.scalar.activation(PT[0:rows, q % 2, at_:at_ + w_], src, ACT.Copy)
                                z = e
                            ins.then_inc(copied, 1)
                        q = i - 3
                        if 0 <= q < n and jobs[q].get("gate") is None:
                            act.wait_ge(out_ready, q + 1)
                            nc.scalar.activation(jobs[q]["out"], out_ps(q), ACT.Copy).then_inc(out_done, 1)


        ws.begin(0, MOD_CH + IN0_CH + OUT_CH + FFN_CH + MOD_CH + PW1_CH + OUT_CH)
        with Stage(nc, "load", ["loaded"]) as (block, (loaded,)):
            @block.sync
            def _(sp):
                sp.dma_start(small[:, :], a["small"]).then_inc(loaded, 16)
                sp.dma_start(consts[:, 0:2 * P], a["consts"][:, 0:2 * P]).then_inc(loaded, 16)
                ws.load(sp, 0, 0, [])
                for dst, src in ((XT, a["xT"]), (UC, a["ctxT"]), (consts[:, 2 * P:], a["consts"][:, 2 * P:]),
                                 (all_small[:, :], a["layer_small"])):
                    sp.dma_start(dst, src).then_inc(late, 16)
                sp.wait_ge(loaded, 32)
                sp.nop()

        silu_in = small[:, SMALL_AT["c"][0]:SMALL_AT["c"][0] + 16]
        lq = sm("lam")
        pointwise("silu_c", [
            ("act", lambda e: nc.scalar.activation(cs[:, 0:16], silu_in, ACT.Silu)),
            ("dve", lambda e: e.tensor_tensor(lam[:, 0:2], lq[:, 0:2], lq[:, 2:4], ALU.mult)),
            ("pe", lambda e: e.matmul(PS[:, 0, 0:2], ones[0:64, :], lam[0:64, 0:2], start=True, stop=True)),
            ("act", lambda e: nc.scalar.activation(lam[:, 2:4], PS[:, 0, 0:2], ACT.Exp)),
            ("dve", lambda e: e.tensor_tensor(lam[:, 4:5], lam[:, 3:4], lam[:, 2:3], ALU.subtract)),
            ("dve", lambda e: e.tensor_scalar(lam[:, 5:6], lam[:, 4:5], -LAM_INIT, None, ALU.add))])

        first_modulation("mod0", MOD_FIRST, cs[:, 0:16].rearrange("p (v k) -> p v k", v=2), sm("mod_b0", 0, 2 * MOD_FIRST),
                         [mod[:, 0:2 * MOD_FIRST], modc[:, 0:2 * MOD_FIRST]])

        def mpart(i, m=None):
            return (mod if m is None else m)[:, KT * i:KT * (i + 1)]

        modulated("norm_ctx", UC, UC, sm("pre0"), modc[:, 0:8], modc[:, 8:16])
        modulated("norm_x", XT, UX, sm("pre0"), mpart(0), mpart(1))

        qm = area(0, 1024).rearrange("p (k t) -> p k t", k=4)
        km = area(1024, 2048).rearrange("p (k t) -> p k t", k=4)
        vm = area(3072, 2080).rearrange("p (s h d) -> p s h d", s=4, h=8)
        om = area(5152, 1024).rearrange("p (k t) -> p k t", k=4)
        gt = area(6176, 2048).rearrange("p (g t) -> p g t", g=4)
        dq = area(8224, 1024).rearrange("p (k t) -> p k t", k=4)
        dk = area(9248, 2048).rearrange("p (k t) -> p k t", k=4)
        dv = area(11296, 2048).rearrange("p (s n) -> p s n", s=4)
        SCR = 13344
        mixT = YT
        cw = sm("conv_w")

        def conv3(dst, col, segs):
            def f(dve, bank, link):
                for z, (s0, d0) in enumerate(segs):
                    x, y = bank[:, s0:s0 + T], dst[:, d0:d0 + T]
                    link(dve.tensor_scalar(y, x, cw[:, 3 * col + 1:3 * col + 2], None, ALU.mult))
                    link(dve.scalar_tensor_tensor(out=y[:, 1:T], in0=x[:, 0:T - 1], scalar=cw[:, 3 * col:3 * col + 1],
                                                  in1=y[:, 1:T], op0=ALU.mult, op1=ALU.add))
                    ins = dve.scalar_tensor_tensor(out=y[:, 0:T - 1], in0=x[:, 1:T], scalar=cw[:, 3 * col + 2:3 * col + 3],
                                                   in1=y[:, 0:T - 1], op0=ALU.mult, op1=ALU.add)
                    if z < len(segs) - 1:
                        link(ins)
                return ins
            return f

        gB = area(SCR + 512, 1024).rearrange("p (d t) -> p d t", d=2)
        gM = area(SCR + 1536, 1024).rearrange("p (d t) -> p d t", d=2)
        gN = area(SCR + 2560, 1024).rearrange("p (d e t) -> p d e t", d=2, e=2)
        tA = area(SCR + 3584, 64).rearrange("p (d s h) -> p d s h", d=2, s=4)
        tM = area(SCR + 3584 + 64, 32).rearrange("p (d s h) -> p d s h", d=2, s=2)
        rtmp0 = area(SCR + 3696, 2 * T).rearrange("p (b t) -> p b t", b=2)
        lf, ig = gt[0:8, 1:4:2, :], gt[0:8, 0:4:2, :]
        o512 = ones[0:8, 0:1].broadcast_to([8, 512])
        B8, M8, A8 = gB[0:8], gM[0:8], gt[0:8, 0:4:2, :]

        def gate_copy(g):
            return lambda act, bank, link: nc.scalar.activation(gt[0:8, g, :], bank[0:8, 0:512], ACT.Identity, bias=sm("gate_b", g, 1)[0:8, :])
        tasks = [tile_task(0, 0, U2, "act", gate_copy(g), ncols=8, c0=8 * g) for g in range(4)]
        tasks.append(Task(None, None, "dve", lambda e, b, link: e.memset(gN, 0.0)))
        gate_steps = []

        def gate_step(engine, f):
            need = gate_steps[-1] if gate_steps else tasks[3]
            gate_steps.append(Task(None, None, engine, lambda e, b, link: f(e), (need,)))
        for engine, f in log_sigmoid_steps(lf, B8, M8):
            gate_step(engine, f)
        gate_step("dve", lambda e: e.tensor_tensor_scan(B8[:, 0, :], o512, gt[0:8, 1, :], 0.0, ALU.mult, ALU.add))
        gate_step("dve", lambda e: e.tensor_tensor_scan(B8[:, 1, C - 1::-1], o512[:, 0:C], gt[0:8, 3, C - 1::-1], 0.0, ALU.mult, ALU.add))
        gate_step("dve", lambda e: e.tensor_tensor_scan(B8[:, 1, 511:C - 1:-1], o512[:, 0:T], gt[0:8, 3, 511:C - 1:-1], B8[:, 1, 0:1], ALU.mult, ALU.add))
        gate_step("dve", lambda e: e.tensor_tensor(A8, ig, B8, ALU.subtract))
        gate_step("dve", lambda e: e.tensor_tensor_scan(M8[:, 0, :], gt[0:8, 0, :], gt[0:8, 0, :], NEG, ALU.max, ALU.max))
        gate_step("dve", lambda e: e.tensor_tensor_scan(M8[:, 1, C - 1::-1], gt[0:8, 2, C - 1::-1], gt[0:8, 2, C - 1::-1], NEG, ALU.max, ALU.max))
        gate_step("dve", lambda e: e.tensor_tensor_scan(M8[:, 1, 511:C - 1:-1], gt[0:8, 2, 511:C - 1:-1], gt[0:8, 2, 511:C - 1:-1], M8[:, 1, 0:1], ALU.max, ALU.max))
        gate_step("dve", lambda e: e.tensor_scalar(gN[0:8, :, 0, :], M8[:, :, C:], -1.0, None, ALU.mult))
        gate_step("dve", lambda e: e.tensor_tensor(B8[:, :, C:], B8[:, :, C:], M8[:, :, C:], ALU.add))
        gate_step("act", lambda e: nc.scalar.activation(gN[0:8, :, 1, :], B8[:, :, C:], ACT.Exp, scale=-1.0))

        def turn_gates(bank, chunk):
            eye = ident[0:8, 0:8]
            return [(bank[:, (d * 4 + s) * 8:(d * 4 + s + 1) * 8], gt[0:8, 2 * d, s * P:(s + 1) * P], eye, True, True)
                    for d in range(2) for s in range(4)] + \
                   [(bank[:, 64 + (d * 2 + s) * 8:64 + (d * 2 + s + 1) * 8], gN[0:8, d, 1, s * P:(s + 1) * P], eye, True, True)
                    for d in range(2) for s in range(2)]
        gate_turn = Task(None, turn_gates, "act", lambda act, bank, link: nc.scalar.activation(area(SCR + 3584, 96), bank[:, 0:96], ACT.Copy),
                         (gate_steps[-1],))

        ax = ("rot_ax", "cos_ax", "sin_ax")
        waiting = []

        def spread(n):
            for _ in range(n):
                if gate_steps:
                    tasks.append(gate_steps.pop(0))
        for m in range(8):
            dst = dq[:, m, :] if m < 4 else dk[:, m - 4, :]
            tasks.append(tile_task(1 + m // 2, m % 2, UX if m < 4 else U2, "act", copy_to(dst)))
            x = dst if m < 4 else dk[:, m - 4, C:C + T]
            waiting.append(rope_task(x, x, rtmp0, *ax, tasks[-1]))
            if len(waiting) > 1:
                tasks.append(waiting.pop(0))
            spread(1)
        tasks += waiting

        def silu_of(x, need):
            return Task(None, None, "act", lambda act, b, link: nc.scalar.activation(x, x, ACT.Silu), (need,))
        for m in range(8):
            if m < 4:
                tasks.append(tile_task(5 + m // 2, m % 2, UX, "dve", conv3(qm[:, m, :], m, [(0, 0)])))
            else:
                tasks.append(tile_task(5 + m // 2, m % 2, U2, "dve", conv3(km[:, m - 4, :], m, [(0, 0), (C, C)])))
            waiting = waiting[8:] + [silu_of(qm[:, m, :] if m < 4 else km[:, m - 4, :], tasks[-1])]
            spread(1)
            tasks += waiting
            waiting = []

        def copy_v(s, h0):
            return lambda act, bank, link: nc.scalar.activation(vm[:, s, h0:h0 + 4, 0:64],
                                                                bank[:, 0:256].rearrange("p (h d) -> p h d", h=4), ACT.Copy)
        tasks.append(Task(None, None, "dve", lambda e, b, link: e.memset(vm[:, :, :, 64:65], 1.0)))
        for c_ in range(2):
            for s in range(4):
                tasks.append(token_task(9 + c_, U2, s * P, "act", copy_v(s, 4 * c_)))
                spread(1)
        for m in range(4):
            tasks.append(tile_task(11 + m // 2, m % 2, UX, "act",
                                   lambda act, bank, link, m=m: nc.scalar.activation(om[:, m, :], bank[:, 0:T], ACT.Sigmoid)))
        assert not gate_steps
        tasks.append(gate_turn)
        for c_ in range(2):
            for s in range(4):
                tasks.append(token_task(13 + c_, U2, s * P, "act", copy_to(dv[:, s, 256 * c_:256 * (c_ + 1)])))
        side_bias = sm("mod_b0")
        project("in0", IN0_CH, tasks, (MOD_CH - MOD_FIRST, cs[:, 0:8], side_bias, mod, 2 * MOD_FIRST, SCR))

        Hm = area(SCR, 1024).rearrange("p (t h d) -> p t h d", t=2, h=8)
        EE = U2.rearrange("p k t -> p (k t)").rearrange("p (j d s t) -> p j d s t", j=2, d=2, s=4)
        dn = mean[:, 0:16].rearrange("p (j n) -> p j n", j=2)
        NH = 8
        with Stage(nc, "mlstm", ["chain", "kq", "mrow", "e_done", "s_done", "num", "h_done"]) as (
                block, (chain, kq, mrow, e_done, s_done, num, h_done)):
            def base(h):
                return 64 * (h % 2)

            def scores_of(h):
                return PS[:, 2 * (h % 2):2 * (h % 2) + 2, :].rearrange("p b (s t) -> p (b s) t", s=2)

            @block.tensor
            def _(pe):
                for i in range(NH + 1):
                    if i < NH:
                        h = i
                        b0 = base(h)
                        if h >= 2:
                            pe.wait_ge(s_done, 6 * (h - 1))
                        for s in range(4):
                            ins = pe.matmul(scores_of(h)[:, s, :], km[b0:b0 + 64, h // 2, s * P:(s + 1) * P],
                                            qm[b0:b0 + 64, h // 2, :], start=True, stop=True)
                        ins.then_inc(kq, 1)
                        if h >= 1:
                            pe.wait_ge(e_done, 10 * h)
                        for d in range(2):
                            lhs = ident[:, h:h + 1].broadcast_to([P, P])
                            pe.matmul(PS[:, 4 + d, 0:T], lhs, gN[:, d, 0, :], start=True, stop=True)
                            pe.matmul(PS[:, 4 + d, T:2 * T], lhs, gN[:, d, 0, :], start=True, stop=False)
                            ins = pe.matmul(PS[:, 4 + d, T:2 * T], ident, const("bmask" if d else "fmask"), start=False, stop=True)
                            ins.then_inc(mrow, 1)
                    if i >= 1:
                        h = i - 1
                        pe.wait_ge(s_done, 6 * (h + 1))
                        if h >= 1:
                            pe.wait_ge(h_done, h)
                        for d in range(2):
                            for t in range(2):
                                keys = [0, 1] + ([2] if (d, t) == (0, 0) else [3] if (d, t) == (1, 1) else [2, 3])
                                o = PS[:, 6 + d, t * 65:(t + 1) * 65]
                                for z, s in enumerate(keys):
                                    ins = pe.matmul(o, EE[:, h % 2, d, s, t * P:(t + 1) * P], vm[:, s, h, :],
                                                    start=(z == 0), stop=(z == len(keys) - 1))
                        ins.then_inc(num, 1)

            def regions(d):
                return [(2, 0, P, 1), (2, P, P, 0), (3, P, P, 1)] if d == 0 else [(3, 0, P, 0), (3, P, P, 1), (2, 0, P, 1)]

            @block.scalar
            def _(act):
                for h in range(NH):
                    if h >= 2:
                        act.wait_ge(num, h - 1)
                    for d in range(2):
                        act.wait_ge(mrow, 2 * h + d + 1)
                        for s in range(2):
                            nc.scalar.activation(EE[:, h % 2, d, s, :], PS[:, 4 + d, 0:T], ACT.Exp,
                                                 bias=tA[:, d, s, h:h + 1]).then_inc(e_done, 1)
                        for s, q0, nq, masked in regions(d):
                            nc.scalar.activation(EE[:, h % 2, d, s, q0:q0 + nq], PS[:, 4 + d, masked * T + q0:masked * T + q0 + nq],
                                                 ACT.Exp, bias=tA[:, d, s, h:h + 1]).then_inc(e_done, 1)

            @block.vector
            def _(dve):
                link = Chain(dve, chain)
                for i in range(NH + 1):
                    if i < NH:
                        h = i
                        dve.wait_ge(kq, h + 1)
                        for d in range(2):
                            dve.wait_ge(e_done, 10 * h + 5 * d + 5)
                            sc = scores_of(h)
                            full, half, q0 = (2, 3, P) if d == 0 else (3, 2, 0)
                            e_ = EE[:, h % 2, d]
                            for x, y in ((e_[:, 0:2, :], sc[:, 0:2, :]), (e_[:, full, :], sc[:, full, :]),
                                         (e_[:, half, q0:q0 + P], sc[:, half, q0:q0 + P])):
                                dve.scalar_tensor_tensor(out=x, in0=y, scalar=0.125, in1=x, op0=ALU.mult,
                                                         op1=ALU.mult).then_inc(s_done, 1)
                    if i >= 1:
                        h = i - 1
                        dve.wait_ge(num, h + 1)
                        nm = PS[:, 6:8, 0:130].rearrange("p d (t n) -> p d t n", t=2)
                        den = nm[:, :, :, 64]
                        r = dn[:, h % 2, 0:4].rearrange("p (d t) -> p d t", d=2)
                        r2 = dn[:, h % 2, 4:8].rearrange("p (d t) -> p d t", d=2)
                        link(dve.tensor_scalar(r2, den, -1.0, None, ALU.mult))
                        link(dve.tensor_tensor(r, den, r2, ALU.max))
                        link(dve.tensor_tensor(r, r, tM[:, :, :, h], ALU.max))
                        link(dve.reciprocal(r2, r))
                        for t in range(2):
                            link(dve.tensor_scalar(Hm[:, t, h, :], nm[:, 0, t, 0:64], r2[:, 0, t:t + 1], None, ALU.mult))
                        for t in range(2):
                            ins = dve.scalar_tensor_tensor(out=Hm[:, t, h, :], in0=nm[:, 1, t, 0:64], scalar=r2[:, 1, t:t + 1],
                                                           in1=Hm[:, t, h, :], op0=ALU.mult, op1=ALU.add)
                            if t == 0:
                                link(ins)
                        ins.then_inc(h_done, 1)

        def turn_heads(name, src_of, dst_of, n_tiles):
            with Stage(nc, name, ["turned", "copied"]) as (block, (turned, copied)):
                @block.tensor
                def _(pe):
                    for m in range(n_tiles):
                        if m >= 4:
                            pe.wait_ge(copied, m - 3)
                        for t in range(2):
                            ins = pe.transpose(PS[:, m % 4, t * P:(t + 1) * P], src_of(m, t), ident)
                        ins.then_inc(turned, 1)

                @block.vector
                def _(dve):
                    for m in range(n_tiles):
                        dve.wait_ge(turned, m + 1)
                        dst_of(dve, m, PS[:, m % 4, 0:T]).then_inc(copied, 1)
                    dve.wait_ge(copied, n_tiles)
                    dve.nop()

        def head_norm_steps(H, n_heads, dim, sq, st, factor=1.0):
            G = 2 * n_heads
            Hf = H.rearrange("p t h d -> p (t h) d")
            sqf = sq.rearrange("p (g d) -> p g d", g=G)
            return [("act", lambda e: nc.scalar.activation(sqf, Hf, ACT.Square)),
                    ("dve", lambda e: e.reduce_sum(st[:, 0:G], sqf, AX)),
                    ("dve", lambda e: e.tensor_scalar(st[:, 0:G], st[:, 0:G], 1.0 / dim, EPS, ALU.mult, ALU.add)),
                    ("act", lambda e: nc.scalar.activation(st[:, G:2 * G], st[:, 0:G], ACT.Sqrt)),
                    ("dve", lambda e: e.reciprocal(st[:, 0:G], st[:, G:2 * G])),
                    ("dve", lambda e: e.tensor_scalar(st[:, 0:G], st[:, 0:G], factor, None, ALU.mult)),
                    ("dve", lambda e: e.tensor_tensor(Hf, Hf, st[:, 0:G].unsqueeze(2).broadcast_to([P, G, dim]), ALU.mult))]

        st0 = rstd[:, 0:32]
        pointwise("mnorm", head_norm_steps(Hm, 8, 64, area(0, 1024), st0))
        turn_heads("mturn", lambda m, t: Hm[:, t, 2 * m:2 * m + 2, :].rearrange("p h d -> p (h d)"),
                   lambda dve, m, ps: dve.scalar_tensor_tensor(out=mixT[:, m, :], in0=ps, scalar=sm("mnorm", m, 1),
                                                               in1=om[:, m, :], op0=ALU.mult, op1=ALU.mult), 4)

        Hd = area(SCR, 1024).rearrange("p (t h d) -> p t h d", t=2, h=4)
        jobs = []
        for h in range(4):
            for t in range(2):
                sides = [slice(0, 64), slice(64, P)]
                jobs.append(dict(scores=[(dq[b, h, t * P:(t + 1) * P], dk[b, h, :]) for b in sides], groups=[(None, 0, 2, 512, None)],
                                 coef=(1, lam[:, 5:6]), minus=True, outs=[(0, [(0, [dv[:, s, h * P:(h + 1) * P] for s in range(4)])])],
                                 token_major=True, out=Hd[:, t, h, :]))
        attention("diff", jobs, 0.125, 0)
        pointwise("dnorm", head_norm_steps(Hd, 4, 128, area(0, 1024), st0, 1.0 - LAM_INIT))
        turn_heads("dturn", lambda m, t: Hd[:, t, m, :],
                   lambda dve, m, ps: dve.tensor_scalar(mixT[:, 4 + m, :], ps, sm("dnorm", m, 1), None, ALU.mult), 4)

        def out_proj(name, src, dst, bias=None):
            project(name, OUT_CH, [tile_task(m // 2, m % 2, src, "act",
                                             copy_to(dst[:, m, :]) if bias is None else copy_bias(dst[:, m, :], bias[:, m:m + 1]))
                                   for m in range(KT)])

        big = area(4096, KT * T).rearrange("p (k t) -> p k t", k=KT)
        out_proj("out0", mixT, big)
        residual("res0", big, sm("post0"), mpart(2))
        modulated("norm_f0", XT, UX, sm("fpre0"), mpart(3), mpart(4))
        ffn("ffn0", UX, (MOD_CH, cs[:, 0:8], sm("mod_b1"), mod1, 0, 8192))
        residual("res_f0", YT, sm("fpost0"), mpart(5))

        modulated("norm_c1", XT, UX, sm("pre1"), mpart(0, mod1), mpart(1, mod1))
        W = 31
        PADL = (W - 1) // 2
        TW = T + W - 1
        glu_a = area(0, 2048).rearrange("p (k t) -> p k t", k=KT)
        glu_g = area(2048, 2048).rearrange("p (k t) -> p k t", k=KT)
        hp = area(4096, KT * TW).rearrange("p (k t) -> p k t", k=KT)
        dw = sm("dw_w").rearrange("p (k w) -> p k w", k=KT)
        ND = 6
        DG = area(6400, (KT - ND) * W * P).rearrange("p (k w n) -> p k w n", k=KT - ND, w=W)

        def diagonals(k, w0, w1):
            def f(act, b, link):
                for w in range(w0, w1):
                    ins = nc.scalar.activation(DG[:, k - ND, w, :], ident, ACT.Copy, scale=dw[:, k, w:w + 1])
                    if w < w1 - 1:
                        link.go(ins)
                link.sync()
                return ins
            return Task(None, None, "act", f, ())

        def convolve_pair(k0):
            def f(dve, b, link):
                for w in range(W):
                    for k in (k0, k0 + 1):
                        x, y = hp[:, k, w:w + T], YT[:, k, :]
                        if w == 0:
                            ins = dve.tensor_scalar(y, x, dw[:, k, 0:1], sm("dw_b", k, 1), ALU.mult, ALU.add)
                        else:
                            dve.wait_ge(link.sem, link.n - 1)
                            ins = dve.scalar_tensor_tensor(out=y, in0=x, scalar=dw[:, k, w:w + 1], in1=y, op0=ALU.mult, op1=ALU.add)
                        if (w, k) != (W - 1, k0 + 1):
                            link.go(ins)
                link.sync()
                return ins
            return Task(None, None, "dve", f, gated[k0:k0 + 2])

        def gate_tile(m, need):
            return Task(None, None, "dve", lambda dve, b, link: dve.tensor_tensor(hp[:, m, PADL:PADL + T], glu_a[:, m, :], glu_g[:, m, :],
                                                                                  ALU.mult), (need,), serial=True)
        tasks = [Task(None, None, "dve", lambda dve, b, link: dve.memset(hp, 0.0))]
        gated = []
        for m in range(KT):
            tasks.append(tile_task(m, 0, UX, "act", copy_bias(glu_a[:, m, :], sm("pw1_b", m, 1))))
            tasks.append(tile_task(m, 1, UX, "act", lambda act, bank, link, m=m: nc.scalar.activation(
                glu_g[:, m, :], bank[:, 0:T], ACT.Sigmoid, bias=sm("pw1_b", KT + m, 1))))
            gated.append(gate_tile(m, tasks[-1]))
            tasks.append(gated[-1])
            if m % 2 and m < 4:
                tasks.append(convolve_pair(m - 1))
            tasks.append(diagonals(ND + m // 4, 8 * (m % 4), min(8 * (m % 4) + 8, W)))
        tasks.append(convolve_pair(4))

        def conv_task(k):
            def matmuls(bank, chunk):
                return [(bank[:, 0:T], DG[:, k - ND, w, :], hp[:, k, w:w + T], w == 0, w == W - 1) for w in range(W)]
            return Task(None, matmuls, "act", copy_bias(YT[:, k, :], sm("dw_b", k, 1)), (gated[k], tasks[-2]))
        tasks += [conv_task(k) for k in range(ND, KT)]
        project("pw1", PW1_CH, tasks)

        norm("ln1", YT, lambda k: sm("ln_g", k, 1), plus_bias(YT, sm("ln_b"), ACT.Silu), center=True)
        out_proj("pw2", YT, big, sm("pw2_b"))
        residual("res1", big, sm("post1"), mpart(2, mod1))
        modulated("norm_m1", XT, UX, sm("fpre1"), mpart(3, mod1), mpart(4, mod1))

        H = area(0, FT * T).rearrange("p (k t) -> p k t", k=FT)
        EX = area(FT * T, 2 * T).rearrange("p (b t) -> p b t", b=2)
        UTM = area(6144, 2048).rearrange("p (t n) -> p t n", t=2)
        YTM = area(8192, 2048).rearrange("p (t n) -> p t n", t=2)
        UCT = area(10240, KT * CAP).rearrange("p (k c) -> p k c", k=KT)
        S1 = area(11136, 2 * CAP).rearrange("p (t c) -> p t c", t=2)
        SG = area(11360, 2 * CAP).rearrange("p (t c) -> p t c", t=2)
        PL = area(11584, T)
        YC = area(11840, D)
        rt = area(12864, 208)
        ACC = area(13072, 3 * 256).rearrange("p (z n) -> p z n", z=3)
        ro = sm("router").rearrange("p (k e) -> p k e", k=KT)

        def rv(i, n=16):
            return rt[:, i:i + n]
        steps = []
        for t in range(2):
            for kt in range(KT):
                steps.append(("pe!" if t + kt else "pe", lambda e, t=t, kt=kt: e.matmul(PS[:, 0, 8 * t:8 * t + 8], UX[:, kt, t * P:(t + 1) * P], ro[:, kt, :],
                                                                   start=(kt == 0), stop=(kt == KT - 1))))
        L = rv(0).rearrange("p (t e) -> p t e", t=2)
        EQ = rv(16).rearrange("p (t e) -> p t e", t=2)
        CU = rv(32).rearrange("p (t e) -> p t e", t=2)
        F1 = rv(48).rearrange("p (t e) -> p t e", t=2)
        F2 = rv(64).rearrange("p (t e) -> p t e", t=2)
        V1, V2, G1, G2 = rv(80, 2), rv(82, 2), rv(84, 2), rv(86, 2)

        def b8(v):
            return v.unsqueeze(2).broadcast_to([P, 2, 8])
        steps.append(("dve", lambda e: e.tensor_copy(rv(0), PS[:, 0, 0:16])))
        for Fx, Vx in ((F1, V1), (F2, V2)):
            steps += [("dve", lambda e, Vx=Vx: e.reduce_max(Vx, L, AX)),
                      ("dve", lambda e, Vx=Vx: e.tensor_tensor(EQ, L, b8(Vx), ALU.is_equal))]
            for t in range(2):
                steps.append(("dve", lambda e, t=t: e.tensor_tensor_scan(CU[:, t, :], ones[:, 0:8], EQ[:, t, :], 0.0, ALU.mult, ALU.add)))
            steps += [("dve", lambda e, Fx=Fx: e.scalar_tensor_tensor(out=Fx, in0=CU, scalar=1.0, in1=EQ, op0=ALU.is_equal, op1=ALU.mult)),
                      ("dve", lambda e, Fx=Fx: e.scalar_tensor_tensor(out=L, in0=Fx, scalar=NEG, in1=L, op0=ALU.mult, op1=ALU.add))]
        steps += [("dve", lambda e: e.tensor_tensor(G2, V2, V1, ALU.subtract)),
                  ("act", lambda e: nc.scalar.activation(G2, G2, ACT.Exp)),
                  ("dve", lambda e: e.tensor_scalar(G1, G2, 1.0, None, ALU.add)),
                  ("dve", lambda e: e.reciprocal(G1, G1)),
                  ("dve", lambda e: e.tensor_tensor(G2, G2, G1, ALU.mult)),
                  ("dve", lambda e: e.tensor_tensor(F1, F1, b8(G1), ALU.mult)),
                  ("dve", lambda e: e.tensor_tensor(F2, F2, b8(G2), ALU.mult)),
                  ("dve", lambda e: e.tensor_tensor(F1, F1, F2, ALU.add)),
                  ("dve", lambda e: e.memset(YT, 0.0))][:-1]
        MK = rt[:, 128:146].rearrange("p (t e) -> p t e", t=2)
        POS = rt[:, 146:164].rearrange("p (t e) -> p t e", t=2)
        GA = rt[:, 164:182].rearrange("p (t e) -> p t e", t=2)
        GC = rt[:, 182:200].rearrange("p (t e) -> p t e", t=2)
        FIT = rt[:, 200:208]
        steps.insert(-6, ("dve", lambda e: e.memset(rt[:, 128:200], 0.0)))
        steps.insert(-6, ("dve", lambda e: e.tensor_tensor(MK[:, :, 0:8], F1, F2, ALU.add)))
        steps.append(("dve", lambda e: e.tensor_copy(GA[:, :, 0:8], F1)))
        ncum_ = const("ncum").rearrange("p (k s) -> p k s", k=2)
        for t in range(2):
            for k in range(2):
                steps.append(("pe", lambda e, t=t, k=k: e.matmul(PS[:, 1, 8 * t:8 * t + 8], ncum_[:, k, t * P:(t + 1) * P],
                                                                 MK[:, k, 0:8], start=(k == 0), stop=(k == 1))))
        for k in range(2):
            steps.append(("pe", lambda e, k=k: e.matmul(PS[:, 2, 0:8], ones, MK[:, k, 0:8], start=(k == 0), stop=(k == 1))))
        steps += [("dve", lambda e: e.tensor_scalar(POS[:, :, 0:8], PS[:, 1, 0:16].rearrange("p (t e) -> p t e", t=2), -1.0, -1.0,
                                                    ALU.mult, ALU.add)),
                  ("dve", lambda e: e.tensor_scalar(full_flag[:, :], PS[:, 2, 0:8], float(CAP), None, ALU.is_gt)),
                  ("dve", lambda e: e.tensor_scalar(FIT, PS[:, 2, 0:8], float(CAP), None, ALU.is_le)),
                  ("dve", lambda e: e.tensor_tensor(GC[:, :, 0:8], GA[:, :, 0:8], FIT.unsqueeze(1).broadcast_to([P, 2, 8]), ALU.mult))]
        pointwise("router", steps)
        with Stage(nc, "uturn", ["turned", "copied"]) as (block, (turned, copied)):
            @block.tensor
            def _(pe):
                for j in range(4):
                    t, half = j // 2, j % 2
                    for k in range(4):
                        ins = pe.transpose(PS[:, j, k * P:(k + 1) * P], UX[:, 4 * half + k, t * P:(t + 1) * P], ident)
                    ins.then_inc(turned, 1)

            @block.scalar
            def _(act):
                for j in range(4):
                    act.wait_ge(turned, j + 1)
                    nc.scalar.activation(UTM[:, j // 2, (j % 2) * 512:(j % 2 + 1) * 512], PS[:, j, :], ACT.Copy)

            @block.vector
            def _(dve):
                dve.memset(YTM, 0.0)
        ws.clear()
        moe_base = ws.total
        W13 = FT
        USES = EXPERT_CH // RING

        with Stage(nc, "experts", ["built", "chunk_done", "silu_ready", "hidden", "place_turned", "gathered", "act_copied",
                                   "y_copied", "y_ready", "y_added", "acc_ready", "acc_chain"]) as (
                block, (built, chunk_done, silu_ready, hidden, place_turned, gathered, act_copied, y_copied, y_ready, y_added,
                        acc_ready, acc_chain)):
            @block.sync
            def _(sp):
                for k in range(RING):
                    sp.dma_start(ws.chunk(k), a["stream"][moe_base + k]).then_inc(landed[k], 16)

                def refill(e, k, source):
                    if k in EXPERT_SIDES:
                        sp.wait_ge(acc_ready, e * EXPERT_SIDE + EXPERT_SIDES.index(k) + 1)
                    else:
                        sp.wait_ge(chunk_done, e * FFN_CH + EXPERT_MAIN.index(k) + 1)
                    sp.dma_start(ws.chunk(k), source).then_inc(landed[k % RING], 16)

                with sp.Fori(0, NE - 1) as e:
                    for k in range(EXPERT_CH):
                        refill(e, k, a["stream"][e * EXPERT_CH + (moe_base + k + RING)])
                for k in range(EXPERT_CH - RING):
                    refill(NE - 1, k, a["stream"][moe_base + (NE - 1) * EXPERT_CH + k + RING])

            def here(eng, e, k):
                eng.wait_ge(landed[k % RING], e * (16 * USES) + 16 * (k // RING + 1))

            def main(k):
                return ws.chunk(EXPERT_MAIN[k])

            @block.tensor
            def _(pe):
                def gather(e):
                    for k in range(KT):
                        for t in range(2):
                            ins = pe.matmul(PS[:, 6 + k // 4, (k % 4) * CAP:(k % 4 + 1) * CAP], UTM[:, t, k * P:(k + 1) * P], S1[:, t, :],
                                            start=(t == 0), stop=(t == 1))
                    ins.then_inc(gathered, 1)

                def hidden_products(e, src, n):
                    for m in range(W13):
                        here(pe, e, EXPERT_MAIN[m])
                        if m >= 4:
                            pe.wait_ge(hidden, e * FT + m - 3)
                        else:
                            pe.wait_ge(y_added, e * 4)
                        w = main(m).rearrange("p (n k c) -> p n k c", n=2, k=KT)
                        for h in range(2):
                            for kt in range(KT):
                                ins = pe.matmul(PS[:, m % 4, h * T:h * T + n], w[:, h, kt, :], src[:, kt, 0:n],
                                                start=(kt == 0), stop=(kt == KT - 1))
                        ins.then_inc(chunk_done, 1)

                pe.wait_ge(built, 2)
                gather(0)
                with pe.Fori(0, NE) as e:
                    full = pe.value_load(full_flag[0:1, bass.ds(e, 1)], min_val=0, max_val=1)
                    pe.wait_ge(act_copied, e * 4 + 2)
                    with pe.If(full < 1):
                        hidden_products(e, UCT, CAP)
                    with pe.Else():
                        hidden_products(e, UX, T)
                    pe.wait_ge(built, e * 4 + 6)
                    gather(e)
                    pe.wait_ge(hidden, e * FT + FT - 3)
                    for t in range(2):
                        pe.transpose(PS[0:CAP, 2, t * P:(t + 1) * P], SG[:, t, :], ident)
                    pe.wait_ge(acc_ready, e * EXPERT_SIDE + EXPERT_SIDE)
                    for z in range(2 * EXPERT_SIDE):
                        ins = pe.matmul(PS[:, 2, T + z:T + z + 1], ACC[:, z // 2, (z % 2) * P:(z % 2 + 1) * P], ones[:, 0:1],
                                        start=True, stop=True)
                    ins.then_inc(place_turned, 1)
                    pe.wait_ge(hidden, e * FT + FT)
                    with pe.If(full < 1):
                        for q in range(FFN_CH - W13):
                            here(pe, e, EXPERT_MAIN[W13 + q])
                            for m in range(2):
                                for half in range(2):
                                    ins = pe.matmul(PS[0:CAP, 4 + half, :], H[:, 2 * q + m, 0:CAP],
                                                    main(W13 + q)[:, m * D + half * 512:m * D + (half + 1) * 512],
                                                    start=(q + m == 0), stop=(2 * q + m == FT - 1))
                            ins.then_inc(chunk_done, 1)
                        for j in (0, 2, 1, 3):
                            pe.wait_ge(y_copied, e * 2 + j % 2 + 1)
                            pe.matmul(PS[:, j, :], PL[0:CAP, (j // 2) * P:(j // 2 + 1) * P], YC[0:CAP, (j % 2) * 512:(j % 2 + 1) * 512],
                                      start=True, stop=True).then_inc(y_ready, 1)
                    with pe.Else():
                        pe.wait_ge(act_copied, e * 4 + 6)
                        for q in range(FFN_CH - W13):
                            here(pe, e, EXPERT_MAIN[W13 + q])
                            for m in range(2):
                                for j in range(4):
                                    ins = pe.matmul(PS[:, 4 + j, :], H[:, 2 * q + m, (j // 2) * P:(j // 2 + 1) * P],
                                                    main(W13 + q)[:, m * D + (j % 2) * 512:m * D + (j % 2 + 1) * 512],
                                                    start=(q + m == 0), stop=(2 * q + m == FT - 1))
                            ins.then_inc(chunk_done, 1)
                        for j in range(4):
                            ins = pe.matmul(PS[:, 0, 0:1], ident, ident[:, 0:1], start=True, stop=True)
                            ins.then_inc(y_ready, 1)
                    pe.nop()

            @block.scalar
            def _(act):
                def silus(e, n):
                    act.wait_ge(hidden, e * FT)
                    for m in range(FT):
                        act.wait_ge(chunk_done, e * FFN_CH + m + 1)
                        if m >= 2:
                            act.wait_ge(hidden, e * FT + m - 1)
                        nc.scalar.activation(EX[:, m % 2, 0:n], PS[:, m % 4, 0:n], ACT.Silu).then_inc(silu_ready, 1)

                def copy_gathered():
                    for b in range(2):
                        nc.scalar.activation(UCT[:, 4 * b:4 * b + 4, :], PS[:, 6 + b, 0:4 * CAP].rearrange("p (k c) -> p k c", k=4),
                                             ACT.Copy).then_inc(act_copied, 1)
                act.wait_ge(gathered, 1)
                copy_gathered()
                with act.Fori(0, NE) as e:
                    full = act.value_load(full_flag[0:1, bass.ds(e, 1)], min_val=0, max_val=1)
                    with act.If(full < 1):
                        silus(e, CAP)
                    with act.Else():
                        silus(e, T)
                    act.wait_ge(gathered, e + 2)
                    copy_gathered()
                    act.wait_ge(place_turned, e + 1)
                    nc.scalar.activation(PL[0:CAP, :], PS[0:CAP, 2, 0:T], ACT.Copy).then_inc(act_copied, 1)
                    nc.scalar.activation(adac[:, bass.ds(e * (2 * EXPERT_SIDE), 2 * EXPERT_SIDE)], PS[:, 2, T:T + 2 * EXPERT_SIDE],
                                         ACT.Copy).then_inc(act_copied, 1)
                    with act.If(full < 1):
                        act.wait_ge(chunk_done, e * FFN_CH + FFN_CH)
                        for b in range(2):
                            nc.scalar.activation(YC[0:CAP, b * 512:(b + 1) * 512], PS[0:CAP, 4 + b, :], ACT.Copy).then_inc(y_copied, 1)
                    with act.Else():
                        for b in range(2):
                            act.nop().then_inc(y_copied, 1)
                    act.nop()

            @block.vector
            def _(dve):
                def build(e, which):
                    dst, val = (S1, MK) if which == 0 else (SG, GC)
                    for t in range(2):
                        dve.tensor_scalar(dst[:, t, :], const("iota"), POS[:, t, bass.ds(e, 1)], val[:, t, bass.ds(e, 1)],
                                          ALU.is_equal, ALU.mult).then_inc(built, 1)

                def side(e, z):
                    here(dve, e, EXPERT_SIDES[z])
                    if z == 0:
                        dve.wait_ge(place_turned, e)
                    w = ws.chunk(EXPERT_SIDES[z]).rearrange("p (n k c) -> p n k c", n=2, k=KT)
                    o = ACC[:, z, :].rearrange("p (n c) -> p n c", n=2)
                    for kt in range(KT):
                        if kt == 0:
                            ins = dve.tensor_scalar(o, w[:, :, 0, :], sm("c2", 0, 1), None, ALU.mult)
                        else:
                            dve.wait_ge(acc_chain, (e * EXPERT_SIDE + z) * (KT - 1) + kt)
                            ins = dve.scalar_tensor_tensor(out=o, in0=w[:, :, kt, :], scalar=sm("c2", kt, 1), in1=o,
                                                           op0=ALU.mult, op1=ALU.add)
                        ins.then_inc(acc_chain if kt < KT - 1 else acc_ready, 1)

                def hiddens(e, n):
                    for m in range(FT):
                        x = EX[:, m % 2, 0:n]
                        dve.wait_ge(silu_ready, e * FT + m + 1)
                        dve.tensor_tensor(H[:, m, 0:n], PS[:, m % 4, T:T + n], x, ALU.mult).then_inc(hidden, 1)
                        if m in EXPERT_AFTER:
                            side(e, EXPERT_AFTER.index(m))

                build(0, 0)
                with dve.Fori(0, NE) as e:
                    full = dve.value_load(full_flag[0:1, bass.ds(e, 1)], min_val=0, max_val=1)
                    dve.wait_ge(gathered, e + 1)
                    build(e + 1, 0)
                    dve.wait_ge(place_turned, e)
                    build(e, 1)
                    with dve.If(full < 1):
                        hiddens(e, CAP)
                    with dve.Else():
                        hiddens(e, T)
                    with dve.If(full < 1):
                        for nth, j in enumerate((0, 2, 1, 3)):
                            dve.wait_ge(y_ready, e * 4 + nth + 1)
                            y = YTM[:, j // 2, (j % 2) * 512:(j % 2 + 1) * 512]
                            dve.tensor_tensor(y, y, PS[:, j, :], ALU.add).then_inc(y_added, 1)
                    with dve.Else():
                        for j in range(4):
                            dve.wait_ge(y_ready, e * 4 + 4)
                            y = YTM[:, j // 2, (j % 2) * 512:(j % 2 + 1) * 512]
                            dve.scalar_tensor_tensor(out=y, in0=PS[:, 4 + j, :], scalar=GA[:, j // 2, bass.ds(e, 1)], in1=y,
                                                     op0=ALU.mult, op1=ALU.add).then_inc(y_added, 1)
                    dve.nop()
        ws.clear()
        turn_heads("yturn", lambda m, t: YTM[:, t, m * P:(m + 1) * P], lambda dve, m, ps: dve.tensor_copy(YT[:, m, :], ps), KT)
        residual("res_m1", YT, sm("fpost1"), mpart(5, mod1))

        q_dsa = area(0, 512).rearrange("p (k t) -> p k t", k=2)
        k_dsa = area(512, 256)
        q_idx = area(768, 512).rearrange("p (k t) -> p k t", k=2)
        k_idx = area(1280, 256)
        q_fox = area(1536, 768).rearrange("p (k t) -> p k t", k=3)
        k_fox = area(2304, 768).rearrange("p (k t) -> p k t", k=3)
        q_nsa = area(3072, 768).rearrange("p (k t) -> p k t", k=3)
        qr_nsa = area(3840, 768).rearrange("p (k t) -> p k t", k=3)
        kc_in = area(4608, 256)
        vc_in = area(4864, 256)
        k_slc = area(5120, 256)
        k_win = area(5376, 256)
        sgate = area(5632, 2048).rearrange("p (k t) -> p k t", k=KT)
        tokm = area(7680, 2 * 768).rearrange("p (t n) -> p t n", t=2)
        V_FOX, V_SLC, V_WIN, V_DSA, I_W, N_G, F_F = 0, 384, 512, 640, 704, 712, 730
        kcT = area(9216, 16)
        vcn = area(9232, 128)
        foxb = area(9360, 6 * 384).rearrange("p (h n) -> p h n", h=6)
        dsab = area(11664, 384)
        SCR2 = 12048
        with nc.Fori(0, LAYERS) as ly:
            ws.begin(moe_base + NE * EXPERT_CH + ly * L2_CH, L2_CH)

            def u_apply():
                st = [("dve", lambda e: e.tensor_copy(layer_small[:, :], all_small[:, bass.ds(ly * LAYER_N, LAYER_N)])),
                      ("dve", lambda e: e.tensor_tensor(mod[:, 0:24], adac[:, bass.ds(ly * 24, 24)], lsm("b_ada"), ALU.add)),
                      ("dve", lambda e: e.tensor_scalar(coef[:, 0:8], mod[:, 8:16], 1.0, None, ALU.add)),
                      ("dve", lambda e: e.tensor_scalar(coef[:, 8:16], mod[:, 16:24], 1.0, None, ALU.add))]
                for k in range(KT):
                    st.append(("dve!" if k else "dve", lambda e, k=k: e.tensor_scalar(UX[:, k, :], XT[:, k, :], coef[:, k:k + 1], mod[:, k:k + 1],
                                                                     ALU.mult, ALU.add)))
                return st
            pointwise("u2", u_apply(), prefetch=True)

            hc1 = area(SCR2, 32)
            hc = area(SCR2 + 32, 32)
            kb = area(SCR2 + 256, 2 * 480).rearrange("p (z l c) -> p z l c", z=2, l=32)
            isc = area(SCR2 + 1248, 384)
            wk = area(SCR2 + 1632, 2 * 256).rearrange("p (j n) -> p j n", j=2)
            m8 = area(SCR2 + 2144, 8)
            rtmp = area(SCR2 + 2176, 2 * T).rearrange("p (b t) -> p b t", b=2)
            ptmp = area(SCR2 + 2688, T)
            lt1, lt2 = (area(SCR2 + at_, 12).rearrange("p (t n) -> p t n", t=2) for at_ in (2944, 2960))
            tasks = []

            def add(*args, **kw):
                tasks.append(Task(*args, **kw))
                return tasks[-1]

            def feature_tile(m, dst, func=ACT.Copy):
                k = chunk_of_tile(m)
                tasks.append(tile_task(k, m % 2, UX, "act", lambda act, bank, link: nc.scalar.activation(dst, bank[:, 0:T], func)))
                return tasks[-1]

            def chunk_of_tile(m):
                k = m // 2 + (3 if m >= 4 else 0)
                return k if m < 6 else k + min(k - 5, CMP_CH)

            r32, r64 = ("rot32", "cos32", "sin32"), ("rot64", "cos64", "sin64")
            qi = [feature_tile(m, q_idx[:, m, :]) for m in range(2)]
            ki = feature_tile(2, k_idx)
            kd = feature_tile(3, k_dsa)
            roped = []
            for x, need, r in ((q_idx[:, 0, :], qi[0], r32), (q_idx[:, 1, :], qi[1], r32), (k_idx, ki, r32), (k_dsa, kd, r64)):
                tasks.append(rope_task(x, x, rtmp, *r, need))
                roped.append(tasks[-1])
            for c_ in (2, 0, 1):
                for t in range(2):
                    tasks.append(token_task(2 + (2, 0, 1).index(c_), UX, t * P, "act", copy_to(tokm[:, t, 256 * c_:256 * (c_ + 1)])))
                if c_ == 2:
                    small_cols = tasks[-1]
            kc_t, vc_t = feature_tile(4, kc_in), feature_tile(5, vc_in)

            iw = tokm[:, :, I_W:I_W + 8]
            iw_t = add(None, None, "dve", lambda e, b, link: e.tensor_scalar(iw, iw, 8.0 ** -0.5, None, ALU.mult), (small_cols,))
            ng = tokm[:, :, N_G:N_G + 18]
            add(None, None, "act", lambda e, b, link: nc.scalar.activation(ng, ng, ACT.Sigmoid), (small_cols,))
            fz = tokm[:, :, F_F:F_F + 6]
            fb = lsm("b_f").unsqueeze(1).broadcast_to([P, 2, 6])

            def forget_in(e, b, link):
                link(e.tensor_tensor(fz, fz, fb, ALU.add))
                return e.scalar_tensor_tensor(out=lt1, in0=fz, scalar=-1.0, in1=fz, op0=ALU.mult, op1=ALU.max)
            forget = Task(None, None, "dve", forget_in, (small_cols,))
            forget_steps = [forget]
            for engine, f in (("act", lambda e, b, link: nc.scalar.activation(lt1, lt1, ACT.Exp, scale=-1.0)),
                              ("dve", lambda e, b, link: e.tensor_scalar(lt1, lt1, 1.0, None, ALU.add)),
                              ("act", lambda e, b, link: nc.scalar.activation(lt2, lt1, ACT.Ln)),
                              ("dve", lambda e, b, link: e.scalar_tensor_tensor(out=fz, in0=fz, scalar=0.0, in1=lt2, op0=ALU.min,
                                                                                op1=ALU.subtract))):
                forget = Task(None, None, engine, f, (forget,))
                forget_steps.append(forget)

            def build_blocks(z, half):
                def f(dve, b, link):
                    src, pe_ = ((kc_in, "pe_k"), (vc_in, "pe_v"))[z]
                    tok = src[:, 16 * half:16 * half + 16 * NC].rearrange("p (c l) -> p l c", l=16)
                    pos = lsm(pe_, 16 * half, 16).unsqueeze(2).broadcast_to([P, 16, NC])
                    return dve.tensor_tensor(kb[:, z, 16 * half:16 * half + 16, :], tok, pos, ALU.add)
                return f
            built = [[add(None, None, "dve", build_blocks(z, half), ((kc_t, vc_t)[z],)) for half in range(2)] for z in range(2)]

            rows = [(0, 0, P), (1, P, 2 * P)]

            def index_head(t, at_, n_, h):
                b0 = 32 * (h % 4)

                def f(dve, bank, link):
                    o, w = isc[:, at_:at_ + n_], tokm[:, t, I_W + h:I_W + h + 1]
                    if h == 0:
                        return dve.tensor_scalar(o, bank[:, 0:n_], 0.0, w, ALU.max, ALU.mult)
                    link(dve.tensor_scalar(ptmp[:, 0:n_], bank[:, 0:n_], 0.0, w, ALU.max, ALU.mult))
                    return dve.tensor_tensor(o, o, ptmp[:, 0:n_], ALU.add)
                return Task(None, lambda bank, chunk: [(bank[:, 0:n_], q_idx[b0:b0 + 32, h // 4, t * P:(t + 1) * P], k_idx[b0:b0 + 32, 0:n_],
                                                        True, True)], "dve", f, (iw_t, *roped[0:3]), serial=True)
            heads = [index_head(t, at_, n_, h) for t, at_, n_ in rows for h in range(8)]

            def half_sum(z, half):
                def matmuls(bank, chunk):
                    return [(bank[:, 0:NC], chunk[:, l * P:(l + 1) * P], kb[:, z, 16 * half + l, :], l == 0, l == 15) for l in range(16)]

                def f(dve, bank, link):
                    s_ = slice(NC * z, NC * (z + 1))
                    if half == 0:
                        return dve.tensor_copy(hc1[:, s_], bank[:, 0:NC])
                    return dve.tensor_tensor(hc[:, s_], hc1[:, s_], bank[:, 0:NC], ALU.add)
                return Task(6 + 2 * (2 * z + half), matmuls, "dve", f, (built[z][half],), serial=True)
            waiting, fed = [], [0]

            def rest_tile():
                m = fed[0]
                fed[0] += 1
                x, dst = rest[m]
                done = feature_tile(6 + m if m < 8 else 7 + m, x, ACT.Silu if m >= len(rest) - KT else ACT.Copy)
                if dst is not None:
                    waiting.append(rope_task(x, dst, rtmp, *r64, done))
                if len(waiting) > 1 or (waiting and dst is None):
                    tasks.append(waiting.pop(0))
            rest = [(q_dsa[:, 0, :], q_dsa[:, 0, :]), (q_dsa[:, 1, :], q_dsa[:, 1, :]), (k_slc, k_slc), (k_win, k_win)] + \
                   [(q_nsa[:, m, :], qr_nsa[:, m, :]) for m in range(3)] + \
                   [(q_fox[:, m, :], None) for m in range(3)] + [(k_fox[:, m, :], None) for m in range(3)] + \
                   [(sgate[:, m, :], None) for m in range(KT)]
            for z in range(2):
                for half in range(2):
                    tasks.append(half_sum(z, half))
                    first_layer = tasks[-1]
                    for _ in range(2):
                        tasks += heads[0:2]
                        heads = heads[2:]
                        rest_tile()
                    tasks.append(forget_steps.pop(0))
            tasks += forget_steps
            need = add(None, None, "act", lambda e, b, link: nc.scalar.activation(hc[:, 0:2 * NC], hc[:, 0:2 * NC], ACT.Silu), (first_layer,))

            SEL = -3.0e38

            def search(t, at_, n_, step):
                def f(dve, b, link):
                    row = isc[:, at_:at_ + n_]
                    if step == 0:
                        link(dve.tensor_tensor(row, row, const("cmask")[:, at_:at_ + n_], ALU.add))
                    for r in range(2 * step, 2 * step + 2):
                        cur, nxt = (wk[:, (r - 1) % 2, 0:n_] if r else row), wk[:, r % 2, 0:n_]
                        link(dve.max(m8, cur))
                        ins = dve.match_replace(nxt, m8, cur, SEL)
                        if r % 2 == 0 or r == TOPK // 8 - 1:
                            link(ins)
                    if step == TOPK // 16 - 1:
                        link(dve.tensor_scalar(nxt, nxt, SEL, NEG, ALU.not_equal, ALU.mult))
                        ins = dve.tensor_tensor(dsab[:, at_:at_ + n_], nxt, const("cmask")[:, at_:at_ + n_], ALU.add)
                    return ins
                return Task(None, None, "dve", f, (), serial=True)
            work = [search(*r, step) for r in rows for step in range(TOPK // 16)]

            ncum = const("ncum").rearrange("p (k s) -> p k s", k=2)

            def fox_bias(h):
                def f(dve, bank, link):
                    link.go(dve.tensor_tensor(foxb[:, h, 0:P], bank[:, 0:P], const("cmask")[:, 0:P], ALU.add))
                    return dve.tensor_tensor(foxb[:, h, P:3 * P], bank[:, 0:T], const("cmask")[:, P:3 * P], ALU.add)
                return Task(None, lambda bank, chunk: [(bank[:, 0:T], fz[:, t, h:h + 1].broadcast_to([P, P]), ncum[:, t, :], t == 0, t == 1)
                                                       for t in range(2)], "dve", f, (forget,))
            work = [w_ for pair in zip(work, [fox_bias(h) for h in range(6)]) for w_ in pair] + work[6:]

            def second_k(bank, chunk):
                return [(bank[:, 0:NC], chunk[:, 0:P], hc[:, 0:NC], True, True)]

            def second_v(bank, chunk):
                return [(bank[0:NC, 0:P], hc[:, NC:2 * NC], chunk[:, P:2 * P], True, True)]
            tasks += heads
            small_chunk = 6 + 2 * CMP_CH
            add(small_chunk, second_k, "act", lambda e, b, link: nc.scalar.activation(kcT[:, 0:NC], b[:, 0:NC], ACT.Copy), (need,))
            add(small_chunk, second_v, "act", lambda e, b, link: nc.scalar.activation(vcn[0:NC, :], b[0:NC, 0:P], ACT.Copy), (need,))
            while fed[0] < len(rest):
                rest_tile()
                tasks += work[0:1]
                work = work[1:]
            tasks += waiting + work
            project("in2", IN2_CH + CMP_CH, tasks)

            jobs = []

            def span(t):
                return slice(0, P) if t == 0 else slice(P, 3 * P)

            def keys(t):
                return slice(0, P * (t + 1))

            def vals(c0, t):
                return [tokm[:, s, c0:c0 + 64] for s in range(t + 1)]

            halves = [slice(0, 64), slice(64, P)]
            for m in range(2):
                for t in range(2):
                    jobs.append(dict(scores=[(q_dsa[b, m, t * P:(t + 1) * P], k_dsa[b, keys(t)]) for b in halves],
                                     groups=[(None, 0, 2, P * (t + 1), bc(dsab[:, span(t)], 2))], coef=None,
                                     outs=[(64 * z, [(z, vals(V_DSA, t))]) for z in range(2)],
                                     out=YT[:, m, t * P:(t + 1) * P], gate=sgate[:, m, t * P:(t + 1) * P]))
            for m in range(3):
                for t in range(2):
                    jobs.append(dict(scores=[(q_fox[b, m, t * P:(t + 1) * P], k_fox[b, m, keys(t)]) for b in halves],
                                     groups=[(None, 0, 2, P * (t + 1), foxb[:, 2 * m:2 * m + 2, span(t)])], coef=None,
                                     outs=[(64 * z, [(z, vals(V_FOX + 64 * (2 * m + z), t))]) for z in range(2)],
                                     out=YT[:, 2 + m, t * P:(t + 1) * P], gate=sgate[:, 2 + m, t * P:(t + 1) * P]))
            for h in range(6):
                g, j_ = h // 3, h % 3
                bq, bo = halves[g], 64 * (h % 2)
                for t in range(2):
                    q_, qr_ = (x[bq, j_, t * P:(t + 1) * P] for x in (q_nsa, qr_nsa))
                    jobs.append(dict(scores=[(q_, kcT[bq, 0:NC]), (qr_, k_slc[bq, keys(t)]), (qr_, k_win[bq, keys(t)])],
                                     groups=[(1, 0, 1, NC, const("cmpmask")[:, 16 * t:16 * t + NC]),
                                             (0, 1, 2, P * (t + 1), bc(const("cmask")[:, span(t)], 2))],
                                     coef=(0, tokm[:, t, N_G + h:N_G + 18:6]),
                                     outs=[(bo, [(1, vals(V_SLC + 64 * g, t)), (2, vals(V_WIN + 64 * g, t)),
                                                 (0, [vcn[0:NC, 64 * g:64 * g + 64]])])],
                                     out=YT[bo:bo + 64, 5 + h // 2, t * P:(t + 1) * P],
                                     gate=sgate[bo:bo + 64, 5 + h // 2, t * P:(t + 1) * P]))
            attention("attn2", jobs, 0.125, SCR2)
            rs = area(4096, KT * T).rearrange("p (k t) -> p k t", k=KT)
            tasks = [Task(None, None, "dve", lambda dve, b, link: dve.tensor_scalar(XT, XT, ALPHA, None, ALU.mult))]

            def gated_residual(k):
                return lambda dve, bank, link: dve.scalar_tensor_tensor(out=rs[:, k, :], in0=bank[:, 0:T], scalar=coef[:, 8 + k:9 + k],
                                                                        in1=XT[:, k, :], op0=ALU.mult, op1=ALU.add)
            for k in range(KT):
                tasks.append(tile_task(k // 2, k % 2, YT, "dve", gated_residual(k)))
                tasks[-1].serial = k == 0
            project("out2", OUT_CH, tasks)
            norm("ln2", rs, lambda k: lsm("ln_g2", k, 1), plus_bias(XT, lsm("ln_b2")), center=True, eps=LN_EPS)
            ws.clear()

        with Stage(nc, "store", ["stored"]) as (block, (stored,)):
            @block.sync
            def _(sp):
                sp.dma_start(a["out"], XT).then_inc(stored, 16)
                sp.wait_ge(stored, 16)
                sp.nop()



def cols(v):
    v = np.asarray(v)
    return v.reshape(-1, P).T


def blocks(w):
    w = np.asarray(w)
    k, n = w.shape
    return w.reshape(k // P, P, n // P, P).transpose(2, 0, 1, 3)


def to_chunks(b):
    return b.reshape(-1, BLOCKS, P, P).transpose(0, 2, 1, 3).reshape(-1, P, CH)


def chunks(w):
    return to_chunks(blocks(w).reshape(-1, P, P))


def padded(w, n):
    out = np.zeros((w.shape[0], n), w.dtype)
    out[:, :w.shape[1]] = w
    return out


def ffn_chunks(w1, w3, w2):
    pair = np.stack([blocks(w1), blocks(w3)], 1)
    return [to_chunks(pair.reshape(-1, P, P)), chunks(w2)]


def glu_chunks(w):
    return to_chunks(blocks(w).reshape(2, KT, KT, P, P).transpose(1, 0, 2, 3, 4).reshape(-1, P, P))


def expert_chunks(w1, w3, w2):
    pair = np.stack([blocks(w1), blocks(w3)], 1)
    return [to_chunks(pair.reshape(-1, P, P)), to_chunks(blocks(w2).transpose(1, 0, 2, 3).reshape(-1, P, P))]


def merged(main, side):
    at_main, at_side = interleave(len(main), len(side))
    out = np.empty((len(main) + len(side),) + main.shape[1:], main.dtype)
    out[at_main], out[at_side] = main, side
    return out


def two(w):
    out = np.zeros((P, P), w.dtype)
    out[0:64, 0:64] = w
    out[64:, 64:] = w
    return out


def layer_chunks(w_in, cmp_w1, cmp_w2, w_out):
    at, s = 0, {}
    for name, w in (("dsa_q", 256), ("dsa_k", 64), ("dsa_v", 64), ("idx_q", 256), ("idx_k", 32), ("idx_w", 8),
                    ("fox_q", 384), ("fox_k", 384), ("fox_v", 384), ("fox_f", 6), ("nsa_q", 384), ("kc", 128),
                    ("vc", 128), ("ks", 128), ("vs", 128), ("kw", 128), ("vw", 128), ("nsa_g", 18), ("gate", 1024)):
        s[name] = w_in[:, at:at + w]
        at += w
    q = s["nsa_q"].reshape(D, 2, 3, 64).transpose(0, 2, 1, 3).reshape(D, 384)
    one = np.concatenate([s["idx_q"]] + [s["idx_k"]] * 4 + [s["dsa_k"], s["dsa_k"]], 1)
    tok = padded(np.concatenate([s["fox_v"], s["vs"], s["vw"], s["dsa_v"], s["idx_w"], s["nsa_g"], s["fox_f"]], 1), 768)
    tok = np.concatenate([tok[:, 512:], tok[:, :512]], 1)
    two_ = np.concatenate([s["kc"], s["vc"]], 1)
    rest = np.concatenate([s["dsa_q"], s["ks"], s["kw"], q, s["fox_q"], s["fox_k"], s["gate"]], 1)
    small = np.zeros((8, P, P), w_in.dtype)
    small[0], small[1] = two(cmp_w2[0]), two(cmp_w2[1])
    w1 = np.stack([two(cmp_w1[z].reshape(32, 64, 64)[l]) for z in range(2) for l in range(32)], 0)
    tiles = blocks(rest).reshape(-1, P, P)
    parts = [blocks(one), blocks(tok), blocks(two_)]
    for k in range(CMP_CH):
        parts += [w1[BLOCKS * k:BLOCKS * (k + 1)], tiles[BLOCKS * k:BLOCKS * (k + 1)]]
    parts += [small, tiles[BLOCKS * CMP_CH:]]
    inp = np.concatenate([b.reshape(-1, P, P) for b in parts], 0)
    return [to_chunks(inp), chunks(w_out)]


def lay_out(i):
    i = {k: np.asarray(v) for k, v in i.items()}
    f = np.float32
    win = i["l0_w_in"]
    g0 = 4 * 512
    gates, diff = win[:, g0:g0 + 32], win[:, g0 + 32:]
    in0 = np.concatenate([padded(gates, 256), diff[:, :2 * 512], win[:, :g0], diff[:, 2 * 512:]], 1)
    m0 = chunks(i["l0_mod_w"])
    parts = [m0[:MOD_FIRST], merged(chunks(in0), m0[MOD_FIRST:]), chunks(i["l0_w_out"])]
    parts += [merged(np.concatenate(ffn_chunks(i["l0_ffn_w1"], i["l0_ffn_w3"], i["l0_ffn_w2"]), 0), chunks(i["l1_mod_w"]))]
    parts += [glu_chunks(i["l1_conv_pw1_w"]), chunks(i["l1_conv_pw2_w"])]
    ada = np.concatenate([chunks(i["w_ada_2"][l]) for l in range(LAYERS)], 0)
    for e in range(NE):
        own = np.concatenate(expert_chunks(i["l1_moe_w1"][e], i["l1_moe_w3"][e], i["l1_moe_w2"][e]), 0)
        mixed = np.empty((EXPERT_CH,) + own.shape[1:], own.dtype)
        mixed[EXPERT_MAIN] = own
        mixed[EXPERT_SIDES] = ada[e * EXPERT_SIDE:(e + 1) * EXPERT_SIDE]
        parts.append(mixed)
    for l in range(LAYERS):
        parts += layer_chunks(i["w_in_2"][l], i["cmp_w1_2"][l], i["cmp_w2_2"][l], i["w_out_2"][l])
    stream = np.concatenate(parts, 0)

    def rows(m):
        out = np.zeros((P, m.shape[1]), m.dtype)
        out[:m.shape[0]] = m
        return out
    sm = {
        "c": cols(i["c"][0]), "c_ctx": cols(i["c_ctx"]), "mod_b0": cols(i["l0_mod_b"]), "pre0": cols(i["l0_mix_pre_g"]),
        "post0": cols(i["l0_mix_post_g"]), "gate_b": rows(i["l0_mlstm_gate_b"].reshape(4, 8).T),
        "conv_w": i["l0_mlstm_conv_w"].reshape(3, 8, P).transpose(2, 1, 0).reshape(P, 24),
        "mnorm": cols(i["l0_mlstm_norm_g"]),
        "lam": rows(np.stack([i["l0_lambda_q1"], i["l0_lambda_q2"], i["l0_lambda_k1"], i["l0_lambda_k2"]], 1)),
        "dnorm": cols(i["l0_diff_norm_g"]), "fpre0": cols(i["l0_ffn_pre_g"]), "fpost0": cols(i["l0_ffn_post_g"]),
        "mod_b1": cols(i["l1_mod_b"]), "pre1": cols(i["l1_mix_pre_g"]), "post1": cols(i["l1_mix_post_g"]),
        "pw1_b": cols(i["l1_conv_pw1_b"]), "dw_w": i["l1_conv_dw_w"].reshape(31, 8, P).transpose(2, 1, 0).reshape(P, 248),
        "dw_b": cols(i["l1_conv_dw_b"]), "ln_g": cols(i["l1_conv_ln_g"]), "ln_b": cols(i["l1_conv_ln_b"]),
        "pw2_b": cols(i["l1_conv_pw2_b"]), "fpre1": cols(i["l1_ffn_pre_g"]), "fpost1": cols(i["l1_ffn_post_g"]),
        "router": i["l1_router_w"].reshape(8, P, 8).transpose(1, 0, 2).reshape(P, 64), "c2": cols(i["c_2"][0]),
    }
    small = np.concatenate([sm[n] for n, _ in SMALL_W], 1).astype(f, copy=False)
    layer = []
    for l in range(LAYERS):
        pe = i["cmp_pe_2"][l]
        lm = {"b_ada": cols(i["b_ada_2"][l]), "pe_k": np.concatenate([pe[0].T] * 2, 0), "pe_v": np.concatenate([pe[1].T] * 2, 0),
              "ln_g2": cols(i["ln_g_2"][l]), "ln_b2": cols(i["ln_b_2"][l]), "b_f": np.stack([i["b_f_2"][l]] * P, 0)}
        layer.append(np.concatenate([lm[n] for n, _ in LAYER_W], 1))
    t = const_table()
    const = np.concatenate([t[n] for n, _ in CONST_W], 1).astype(f)

    def feature_major(x):
        return np.ascontiguousarray(x[0].T.reshape(KT, P, -1).transpose(1, 0, 2))
    return {"stream": stream, "small": np.ascontiguousarray(small), "layer_small": np.ascontiguousarray(np.concatenate(layer, 1)),
            "consts": const, "xT": feature_major(i["x"]), "ctxT": feature_major(i["ctx"])}


def kernel(**inputs):
    import concourse.bacc as _bacc
    from concourse.bass_utils import run_bass_kernel_spmd as _run

    arrays = lay_out(inputs)
    nc = _bacc.Bacc("TRN2", target_bir_lowering=False, num_devices=1)
    a = {n: nc.dram_tensor(n, v.shape, F32, kind="ExternalInput").ap() for n, v in arrays.items()}
    a["out"] = nc.dram_tensor("out", (P, KT, T), F32, kind="ExternalOutput").ap()
    build(nc, a)
    r = _run(nc, [arrays], core_ids=[0])
    y = r.results[0]["out"]
    return np.ascontiguousarray(y.transpose(1, 0, 2).reshape(D, T).T).reshape(1, T, D)
```
